# Optimizing a Trainium2 kernel written in Bass

```python
import math
import jax
import jax.numpy as jnp
from jax import lax
import numpy as np
import jax, jax.numpy as jnp

D_MODEL = 1024
BATCH = 1
SEQ = 256
DEPTH = 1

HEAD_DIM = 64
CONV_CH = 256
CONV_WIDTH = 31
N_Q_HEADS = 12
N_KV_HEADS = 4
Q_PER_KV = N_Q_HEADS // N_KV_HEADS
NSA_WIDTH = N_Q_HEADS * HEAD_DIM
MIX_WIDTH = CONV_CH + NSA_WIDTH
KV_WIDTH = N_KV_HEADS * HEAD_DIM
CMP_LEN = 32
CMP_STRIDE = 16
CMP_HIDDEN = 256
SEL_BLOCK = 64
SEL_TOPK = 8
WINDOW = 512
Q_BLOCK = 64
N_BRANCH = 3
FORCED_BONUS = 1000.0
D_FF = -(-8 * D_MODEL // (3 * 256)) * 256
IN_COLS = 2 * CONV_CH + NSA_WIDTH + 6 * KV_WIDTH + N_BRANCH * N_Q_HEADS
EPS = 1e-6


def rms_norm(x, g):
    xf = x.astype(jnp.float32)
    y = xf * lax.rsqrt(jnp.mean(xf * xf, axis=-1, keepdims=True) + EPS)
    return (y * g.astype(jnp.float32)).astype(x.dtype)

def layer_norm(x, g, b):
    xf = x.astype(jnp.float32)
    mu = jnp.mean(xf, axis=-1, keepdims=True)
    var = jnp.mean(jnp.square(xf - mu), axis=-1, keepdims=True)
    y = (xf - mu) * lax.rsqrt(var + EPS)
    return (y * g.astype(jnp.float32) + b.astype(jnp.float32)).astype(x.dtype)

def alibi_slopes(n):
    def pow2_slopes(m):
        start = 2.0 ** (-8.0 / m)
        return [start ** (i + 1) for i in range(m)]
    if math.log2(n).is_integer():
        s = pow2_slopes(n)
    else:
        c = 2 ** math.floor(math.log2(n))
        s = pow2_slopes(c) + pow2_slopes(2 * c)[0::2][: n - c]
    return np.asarray(s, dtype=np.float32)

def masked_softmax(s, mask):
    s = jnp.where(mask, s.astype(jnp.float32), -jnp.inf)
    m = jnp.max(s, axis=-1, keepdims=True)
    m = jnp.where(jnp.isfinite(m), m, 0.0)
    p = jnp.exp(s - m)
    return p / jnp.maximum(jnp.sum(p, axis=-1, keepdims=True), 1e-30)

def conv_mixer(a, w_dw, b_dw, ln_g, ln_b):
    u, v = jnp.split(a, 2, axis=-1)
    y = u * jax.nn.sigmoid(v)
    y = lax.conv_general_dilated(
        y, w_dw[:, None, :], window_strides=(1,),
        padding=[(CONV_WIDTH - 1, 0)],
        dimension_numbers=("NWC", "WIO", "NWC"),
        feature_group_count=CONV_CH) + b_dw
    y = layer_norm(y, ln_g, ln_b)
    return jax.nn.silu(y)

def compress(kr, pe, w1, w2):
    b, t = kr.shape[:2]
    chunks = kr.reshape(b, t // CMP_STRIDE, CMP_STRIDE, N_KV_HEADS, HEAD_DIM)
    lo = jnp.einsum("bclgd,ldh->bcgh", chunks, w1[:CMP_STRIDE])
    hi = jnp.einsum("bclgd,ldh->bcgh", chunks, w1[CMP_STRIDE:])
    h = lo[:, :-1] + hi[:, 1:] + jnp.einsum("ld,ldh->h", pe, w1)
    return jnp.einsum("bngh,hd->bngd", jax.nn.silu(h), w2)

def nsa_attention(q, kc, vc, ks, vs, kw, vw, gates):
    b, t = q.shape[:2]
    n_cmp = kc.shape[1]
    n_sel = t // SEL_BLOCK
    k_top = min(SEL_TOPK, n_sel)
    scale = HEAD_DIM ** -0.5
    slopes = jnp.asarray(alibi_slopes(N_Q_HEADS)).reshape(N_KV_HEADS, Q_PER_KV)[None, :, :, None, None]
    cmp_idx = jnp.arange(n_cmp)
    cmp_start = cmp_idx * CMP_STRIDE
    cmp_center = cmp_start.astype(jnp.float32) + 0.5 * (CMP_LEN - 1)
    cmp_end = cmp_start + CMP_LEN - 1
    sel_start = jnp.arange(n_sel) * SEL_BLOCK
    overlap = ((cmp_start[:, None] < sel_start[None, :] + SEL_BLOCK)
               & (cmp_start[:, None] + CMP_LEN > sel_start[None, :])).astype(jnp.float32)
    ks_blk = ks.reshape(b, n_sel, SEL_BLOCK, N_KV_HEADS, HEAD_DIM).transpose(0, 3, 1, 2, 4)
    vs_blk = vs.reshape(b, n_sel, SEL_BLOCK, N_KV_HEADS, HEAD_DIM).transpose(0, 3, 1, 2, 4)
    pad = ((0, 0), (WINDOW, 0), (0, 0), (0, 0))
    kw_pad = jnp.pad(kw, pad)
    vw_pad = jnp.pad(vw, pad)
    b_idx = jnp.arange(b)[:, None, None, None]
    g_idx = jnp.arange(N_KV_HEADS)[None, :, None, None]
    offs = jnp.arange(SEL_BLOCK)
    win_offs = jnp.arange(WINDOW + Q_BLOCK) - WINDOW
    sel_j = jnp.arange(n_sel)

    def block(i):
        t0 = i * Q_BLOCK
        tq = t0 + jnp.arange(Q_BLOCK)
        tqf = tq.astype(jnp.float32)
        qb = lax.dynamic_slice_in_dim(q, t0, Q_BLOCK, axis=1) * scale
        gb = lax.dynamic_slice_in_dim(gates, t0, Q_BLOCK, axis=1)

        s_c = jnp.einsum("bqgrd,bngd->bgrqn", qb, kc) - slopes * (tqf[:, None] - cmp_center[None, :])
        p_c = masked_softmax(s_c, cmp_end[None, :] <= tq[:, None])
        o_c = jnp.einsum("bgrqn,bngd->bqgrd", p_c, vc)

        imp = jnp.einsum("bgrqn,nj->bgqj", p_c, overlap)
        cur = tq // SEL_BLOCK
        forced = ((sel_j[None, :] == 0) | (sel_j[None, :] == cur[:, None])
                  | (sel_j[None, :] == cur[:, None] - 1))
        imp = jnp.where(sel_j[None, :] <= cur[:, None],
                        imp + FORCED_BONUS * forced.astype(jnp.float32), -jnp.inf)
        top_s, top_i = lax.top_k(imp, k_top)

        kg = ks_blk[b_idx, g_idx, top_i]
        vg = vs_blk[b_idx, g_idx, top_i]
        pos = top_i[..., None] * SEL_BLOCK + offs
        mask_s = jnp.isfinite(top_s)[..., None] & (pos <= tq[None, None, :, None, None])
        dist_s = (tqf[None, None, :, None, None] - pos.astype(jnp.float32))[:, :, None]
        s_s = jnp.einsum("bqgrd,bgqksd->bgrqks", qb, kg) - slopes[..., None] * dist_s
        s_s = s_s.reshape(b, N_KV_HEADS, Q_PER_KV, Q_BLOCK, k_top * SEL_BLOCK)
        p_s = masked_softmax(s_s, mask_s.reshape(b, N_KV_HEADS, 1, Q_BLOCK, k_top * SEL_BLOCK))
        o_s = jnp.einsum("bgrqs,bgqsd->bqgrd", p_s,
                         vg.reshape(b, N_KV_HEADS, Q_BLOCK, k_top * SEL_BLOCK, HEAD_DIM))

        kwb = lax.dynamic_slice_in_dim(kw_pad, t0, WINDOW + Q_BLOCK, axis=1)
        vwb = lax.dynamic_slice_in_dim(vw_pad, t0, WINDOW + Q_BLOCK, axis=1)
        pos_w = t0 + win_offs
        dist_w = tq[:, None] - pos_w[None, :]
        mask_w = (dist_w >= 0) & (dist_w < WINDOW) & (pos_w[None, :] >= 0)
        s_w = jnp.einsum("bqgrd,bkgd->bgrqk", qb, kwb) - slopes * dist_w.astype(jnp.float32)
        p_w = masked_softmax(s_w, mask_w)
        o_w = jnp.einsum("bgrqk,bkgd->bqgrd", p_w, vwb)

        out = gb[..., 0:1] * o_c + gb[..., 1:2] * o_s + gb[..., 2:3] * o_w
        return out.astype(q.dtype)

    outs = lax.map(block, jnp.arange(t // Q_BLOCK))
    return jnp.moveaxis(outs, 0, 1).reshape(b, t, NSA_WIDTH)

def hybrid_layer(x, attn_norm, w_in, conv_w, conv_b, conv_ln_g, conv_ln_b,
                 cmp_k_pe, cmp_k_w1, cmp_k_w2, cmp_v_pe, cmp_v_w1, cmp_v_w2,
                 w_out, ffn_norm, w_gate_up, w_down):
    b, t, _ = x.shape
    h = rms_norm(x, attn_norm)
    z = h @ w_in
    splits = np.cumsum([2 * CONV_CH, NSA_WIDTH] + [KV_WIDTH] * 6).tolist()
    a_conv, q, kc_r, vc_r, ks, vs, kw, vw, g = jnp.split(z, splits, axis=-1)
    kv_shape = (b, t, N_KV_HEADS, HEAD_DIM)
    conv_out = conv_mixer(a_conv, conv_w, conv_b, conv_ln_g, conv_ln_b)
    kc = compress(kc_r.reshape(kv_shape), cmp_k_pe, cmp_k_w1, cmp_k_w2)
    vc = compress(vc_r.reshape(kv_shape), cmp_v_pe, cmp_v_w1, cmp_v_w2)
    gates = jax.nn.sigmoid(g).reshape(b, t, N_KV_HEADS, Q_PER_KV, N_BRANCH)
    nsa_out = nsa_attention(q.reshape(b, t, N_KV_HEADS, Q_PER_KV, HEAD_DIM), kc, vc,
                            ks.reshape(kv_shape), vs.reshape(kv_shape),
                            kw.reshape(kv_shape), vw.reshape(kv_shape), gates)
    mix = jnp.concatenate([conv_out, nsa_out.astype(conv_out.dtype)], axis=-1)
    x = x + mix @ w_out
    h = rms_norm(x, ffn_norm)
    gu = h @ w_gate_up
    gate, up = jnp.split(gu, 2, axis=-1)
    return x + (jax.nn.silu(gate) * up) @ w_down

def first_inputs(seed: int = 0) -> dict:
    key = jax.random.key(seed)
    ks = jax.random.split(key, 20)
    f32 = jnp.float32

    def nrm(k, shape, scale):
        return jax.random.normal(k, shape, f32) * scale

    return {
        "x": nrm(ks[0], (BATCH, SEQ, D_MODEL), 1.0),
        "attn_norm": 1.0 + nrm(ks[1], (DEPTH, D_MODEL), 0.05),
        "w_in": nrm(ks[2], (DEPTH, D_MODEL, IN_COLS), D_MODEL ** -0.5),
        "conv_w": nrm(ks[3], (DEPTH, CONV_WIDTH, CONV_CH), CONV_WIDTH ** -0.5),
        "conv_b": nrm(ks[4], (DEPTH, CONV_CH), 0.01),
        "conv_ln_g": 1.0 + nrm(ks[5], (DEPTH, CONV_CH), 0.05),
        "conv_ln_b": nrm(ks[6], (DEPTH, CONV_CH), 0.01),
        "cmp_k_pe": nrm(ks[7], (DEPTH, CMP_LEN, HEAD_DIM), 0.1),
        "cmp_k_w1": nrm(ks[8], (DEPTH, CMP_LEN, HEAD_DIM, CMP_HIDDEN), (CMP_LEN * HEAD_DIM) ** -0.5),
        "cmp_k_w2": nrm(ks[9], (DEPTH, CMP_HIDDEN, HEAD_DIM), CMP_HIDDEN ** -0.5),
        "cmp_v_pe": nrm(ks[10], (DEPTH, CMP_LEN, HEAD_DIM), 0.1),
        "cmp_v_w1": nrm(ks[11], (DEPTH, CMP_LEN, HEAD_DIM, CMP_HIDDEN), (CMP_LEN * HEAD_DIM) ** -0.5),
        "cmp_v_w2": nrm(ks[12], (DEPTH, CMP_HIDDEN, HEAD_DIM), CMP_HIDDEN ** -0.5),
        "w_out": nrm(ks[13], (DEPTH, MIX_WIDTH, D_MODEL), MIX_WIDTH ** -0.5),
        "ffn_norm": 1.0 + nrm(ks[14], (DEPTH, D_MODEL), 0.05),
        "w_gate_up": nrm(ks[15], (DEPTH, D_MODEL, 2 * D_FF), D_MODEL ** -0.5),
        "w_down": nrm(ks[16], (DEPTH, D_FF, D_MODEL), D_FF ** -0.5),
        "final_norm": 1.0 + nrm(ks[17], (D_MODEL,), 0.05),
    }

def first_block(x, attn_norm, w_in, conv_w, conv_b, conv_ln_g, conv_ln_b,
              cmp_k_pe, cmp_k_w1, cmp_k_w2, cmp_v_pe, cmp_v_w1, cmp_v_w2,
              w_out, ffn_norm, w_gate_up, w_down, final_norm):
    for l in range(DEPTH):
        x = hybrid_layer(x, attn_norm[l], w_in[l], conv_w[l], conv_b[l], conv_ln_g[l], conv_ln_b[l],
                         cmp_k_pe[l], cmp_k_w1[l], cmp_k_w2[l], cmp_v_pe[l], cmp_v_w1[l], cmp_v_w2[l],
                         w_out[l], ffn_norm[l], w_gate_up[l], w_down[l])
    return rms_norm(x, final_norm)


DEPTH_2 = 2

N_MIXERS = 2
N_RWKV_LAYERS = (DEPTH_2 + 1) // 2
N_DSA_LAYERS = DEPTH_2 // 2
N_META = 16
D_FF_2 = 2816
NORM_EPS = 1e-6
ROPE_DIM = HEAD_DIM // 4
ROPE_THETA = 500000.0
RWKV_HEADS = D_MODEL // HEAD_DIM
D_DECAY_LORA = 64
D_AAA_LORA = 64
D_GATE_LORA = 160
RWKV_LN_EPS = 64e-5
ATT_HEADS = D_MODEL // HEAD_DIM
ATT_KV_HEADS = 4
ATT_GROUP = ATT_HEADS // ATT_KV_HEADS
IDX_HEADS = 8
IDX_DIM = 64
TOPK_MAX = 256
Q_BLOCK_2 = 128
ATT_Q_W = ATT_HEADS * HEAD_DIM
ATT_KV_W = ATT_KV_HEADS * HEAD_DIM
IDX_Q_W = IDX_HEADS * IDX_DIM
ATT_SPLITS = (ATT_Q_W, ATT_Q_W + ATT_KV_W, ATT_Q_W + 2 * ATT_KV_W,
              ATT_Q_W + 2 * ATT_KV_W + IDX_Q_W, ATT_Q_W + 2 * ATT_KV_W + IDX_Q_W + IDX_DIM)
ATT_IN_W = ATT_Q_W + 2 * ATT_KV_W + IDX_Q_W + IDX_DIM + IDX_HEADS


def rms_norm_2(x, g, eps=NORM_EPS):
    xf = x.astype(jnp.float32)
    y = xf * lax.rsqrt(jnp.mean(xf * xf, axis=-1, keepdims=True) + eps)
    return y.astype(x.dtype) * g

def swiglu(h, w_in, w_out):
    gate, up = jnp.split(h @ w_in, 2, axis=-1)
    return (jax.nn.silu(gate) * up) @ w_out

def rope_tables(n_pos, dtype):
    inv = ROPE_THETA ** (-jnp.arange(0, ROPE_DIM, 2, dtype=jnp.float32) / ROPE_DIM)
    ang = jnp.arange(n_pos, dtype=jnp.float32)[:, None] * inv[None, :]
    return jnp.cos(ang).astype(dtype), jnp.sin(ang).astype(dtype)

def partial_rope(x, cos, sin):
    half = ROPE_DIM // 2
    x1 = x[..., :half]
    x2 = x[..., half:ROPE_DIM]
    c = cos[None, :, None, :]
    s = sin[None, :, None, :]
    return jnp.concatenate([x1 * c - x2 * s, x2 * c + x1 * s, x[..., ROPE_DIM:]], axis=-1)

def wkv7_scan(r, w, k, v, a, b):
    B, T, H, N = r.shape
    xs = tuple(jnp.moveaxis(t.astype(jnp.float32), 1, 0) for t in (r, w, k, v, a, b))

    def step(S, inp):
        r_t, w_t, k_t, v_t, a_t, b_t = inp
        sa = jnp.einsum("bhij,bhj->bhi", S, a_t)
        S = S * w_t[:, :, None, :] + sa[..., None] * b_t[:, :, None, :] + v_t[..., None] * k_t[:, :, None, :]
        y = jnp.einsum("bhij,bhj->bhi", S, r_t)
        return S, y

    S0 = jnp.zeros((B, H, N, N), jnp.float32)
    _, ys = lax.scan(step, S0, xs)
    return jnp.moveaxis(ys, 0, 1).astype(r.dtype)

def rwkv7_time_mix(h, mix, w_r, w_k, w_v, w_o, w0, w1, w2, a0, a1, a2, g1, g2,
                   k_k, k_a, r_k, lnx_g, lnx_b):
    B, T, D = h.shape
    H, N = RWKV_HEADS, HEAD_DIM
    xx = jnp.pad(h, ((0, 0), (1, 0), (0, 0)))[:, :-1] - h
    xm = h[None] + xx[None] * mix[:, None, None, :]
    xr, xw, xk, xv, xa, xg = xm[0], xm[1], xm[2], xm[3], xm[4], xm[5]
    r = xr @ w_r
    k = xk @ w_k
    v = xv @ w_v
    w_log = -jax.nn.softplus(-(w0 + jnp.tanh(xw @ w1) @ w2)) - 0.5
    a = jax.nn.sigmoid(a0 + (xa @ a1) @ a2)
    g = jax.nn.sigmoid(xg @ g1) @ g2
    kk = (k * k_k).reshape(B, T, H, N).astype(jnp.float32)
    kk = (kk / jnp.maximum(jnp.sqrt(jnp.sum(kk * kk, axis=-1, keepdims=True)), 1e-12)).astype(h.dtype)
    k = k * (1.0 + (a - 1.0) * k_a)
    decay = jnp.exp(-jnp.exp(w_log.astype(jnp.float32)))
    rh = r.reshape(B, T, H, N)
    kh = k.reshape(B, T, H, N)
    vh = v.reshape(B, T, H, N)
    ah = a.reshape(B, T, H, N)
    y = wkv7_scan(rh, decay.reshape(B, T, H, N), kh, vh, -kk, kk * ah)
    yf = y.astype(jnp.float32)
    mu = jnp.mean(yf, axis=-1, keepdims=True)
    var = jnp.mean((yf - mu) ** 2, axis=-1, keepdims=True)
    yn = ((yf - mu) * lax.rsqrt(var + RWKV_LN_EPS)).astype(h.dtype).reshape(B, T, D) * lnx_g + lnx_b
    bonus = (jnp.sum(rh * kh * r_k, axis=-1, keepdims=True) * vh).reshape(B, T, D)
    return ((yn + bonus) * g) @ w_o

def dsa_attention(h, w_in, q_g, k_g, w_o, cos, sin, topk):
    B, T, D = h.shape
    q, k, v, qi, ki, wi = jnp.split(h @ w_in, ATT_SPLITS, axis=-1)
    q = partial_rope(rms_norm_2(q.reshape(B, T, ATT_HEADS, HEAD_DIM), q_g), cos, sin)
    k = partial_rope(rms_norm_2(k.reshape(B, T, ATT_KV_HEADS, HEAD_DIM), k_g), cos, sin)
    v = v.reshape(B, T, ATT_KV_HEADS, HEAD_DIM)
    qi = partial_rope(qi.reshape(B, T, IDX_HEADS, IDX_DIM), cos, sin)
    ki = partial_rope(ki[:, :, None, :], cos, sin)[:, :, 0, :]
    wi = wi * (IDX_HEADS ** -0.5 * IDX_DIM ** -0.5)

    n_blk = -(-T // Q_BLOCK_2)
    pad = n_blk * Q_BLOCK_2 - T

    def to_blocks(t):
        t = jnp.pad(t, [(0, 0), (0, pad)] + [(0, 0)] * (t.ndim - 2))
        return jnp.moveaxis(t.reshape((B, n_blk, Q_BLOCK_2) + t.shape[2:]), 1, 0)

    starts = jnp.arange(n_blk, dtype=jnp.int32) * Q_BLOCK_2
    kpos = jnp.arange(T, dtype=jnp.int32)
    scale = HEAD_DIM ** -0.5

    def block(args):
        qb, qib, wib, start = args
        qpos = start + jnp.arange(Q_BLOCK_2, dtype=jnp.int32)
        rel = jax.nn.relu(jnp.einsum("bqhd,bkd->bqhk", qib, ki))
        score = jnp.einsum("bqh,bqhk->bqk", wib, rel).astype(jnp.float32)
        causal = kpos[None, :] <= qpos[:, None]
        score = jnp.where(causal[None], score, -jnp.inf)
        _, idx = lax.top_k(score, topk)
        valid = idx <= qpos[None, :, None]
        kg = jax.vmap(lambda kb, ib: kb[ib])(k, idx)
        vg = jax.vmap(lambda vb, ib: vb[ib])(v, idx)
        qg = qb.reshape(B, Q_BLOCK_2, ATT_KV_HEADS, ATT_GROUP, HEAD_DIM)
        logits = jnp.einsum("bqgrd,bqkgd->bqgrk", qg, kg).astype(jnp.float32) * scale
        logits = jnp.where(valid[:, :, None, None, :], logits, -jnp.inf)
        p = jax.nn.softmax(logits, axis=-1).astype(v.dtype)
        o = jnp.einsum("bqgrk,bqkgd->bqgrd", p, vg)
        return o.reshape(B, Q_BLOCK_2, ATT_Q_W)

    out = lax.map(block, (to_blocks(q), to_blocks(qi), to_blocks(wi), starts))
    out = jnp.moveaxis(out, 0, 1).reshape(B, n_blk * Q_BLOCK_2, ATT_Q_W)[:, :T]
    return out @ w_o

def second_inputs(seed: int = 0) -> dict:
    key = jax.random.key(seed)
    ks = jax.random.split(key, 32)
    f32 = jnp.float32

    def nrm(k, shape, scale):
        return jax.random.normal(k, shape, f32) * scale

    D = D_MODEL
    A = N_RWKV_LAYERS
    S = N_DSA_LAYERS
    return {
        "x": nrm(ks[0], (BATCH, SEQ, D), 1.0),
        "meta": nrm(ks[1], (N_META, D), 1.0),
        "norm_g": 1.0 + nrm(ks[2], (DEPTH_2, 3, D), 0.02),
        "ffn_w_in": nrm(ks[3], (DEPTH_2, 2, D, 2 * D_FF_2), D ** -0.5),
        "ffn_w_out": nrm(ks[4], (DEPTH_2, 2, D_FF_2, D), D_FF_2 ** -0.5),
        "rk_mix": jax.random.uniform(ks[5], (A, 6, D), f32),
        "rk_w_r": nrm(ks[6], (A, D, D), D ** -0.5),
        "rk_w_k": nrm(ks[7], (A, D, D), D ** -0.5),
        "rk_w_v": nrm(ks[8], (A, D, D), D ** -0.5),
        "rk_w_o": nrm(ks[9], (A, D, D), D ** -0.5),
        "rk_w0": -0.6 + nrm(ks[10], (A, D), 0.3),
        "rk_w1": nrm(ks[11], (A, D, D_DECAY_LORA), D ** -0.5),
        "rk_w2": nrm(ks[12], (A, D_DECAY_LORA, D), 0.1 * D_DECAY_LORA ** -0.5),
        "rk_a0": nrm(ks[13], (A, D), 0.1),
        "rk_a1": nrm(ks[14], (A, D, D_AAA_LORA), D ** -0.5),
        "rk_a2": nrm(ks[15], (A, D_AAA_LORA, D), 0.1 * D_AAA_LORA ** -0.5),
        "rk_g1": nrm(ks[16], (A, D, D_GATE_LORA), D ** -0.5),
        "rk_g2": nrm(ks[17], (A, D_GATE_LORA, D), D_GATE_LORA ** -0.5),
        "rk_k_k": 0.85 + nrm(ks[18], (A, D), 0.05),
        "rk_k_a": 1.0 + nrm(ks[19], (A, D), 0.05),
        "rk_r_k": nrm(ks[20], (A, RWKV_HEADS, HEAD_DIM), 0.1),
        "rk_lnx_g": 1.0 + nrm(ks[21], (A, D), 0.02),
        "rk_lnx_b": nrm(ks[22], (A, D), 0.02),
        "at_w_in": nrm(ks[23], (S, D, ATT_IN_W), D ** -0.5),
        "at_q_g": 1.0 + nrm(ks[24], (S, HEAD_DIM), 0.02),
        "at_k_g": 1.0 + nrm(ks[25], (S, HEAD_DIM), 0.02),
        "at_w_o": nrm(ks[26], (S, ATT_Q_W, D), ATT_Q_W ** -0.5),
    }

def second_block(x, meta, norm_g, ffn_w_in, ffn_w_out, rk_mix, rk_w_r, rk_w_k, rk_w_v, rk_w_o,
              rk_w0, rk_w1, rk_w2, rk_a0, rk_a1, rk_a2, rk_g1, rk_g2, rk_k_k, rk_k_a, rk_r_k,
              rk_lnx_g, rk_lnx_b, at_w_in, at_q_g, at_k_g, at_w_o):
    B, L, D = x.shape
    topk = min(TOPK_MAX, L // 4)
    h = jnp.concatenate([jnp.broadcast_to(meta.astype(x.dtype)[None], (B, N_META, D)), x], axis=1)
    T = h.shape[1]
    cos, sin = rope_tables(T, x.dtype)
    for i in range(DEPTH_2):
        g = norm_g[i]
        h = h + 0.5 * swiglu(rms_norm_2(h, g[0]), ffn_w_in[i, 0], ffn_w_out[i, 0])
        hn = rms_norm_2(h, g[1])
        j = i // N_MIXERS
        if i % N_MIXERS == 0:
            h = h + rwkv7_time_mix(hn, rk_mix[j], rk_w_r[j], rk_w_k[j], rk_w_v[j], rk_w_o[j],
                                   rk_w0[j], rk_w1[j], rk_w2[j], rk_a0[j], rk_a1[j], rk_a2[j],
                                   rk_g1[j], rk_g2[j], rk_k_k[j], rk_k_a[j], rk_r_k[j],
                                   rk_lnx_g[j], rk_lnx_b[j])
        else:
            h = h + dsa_attention(hn, at_w_in[j], at_q_g[j], at_k_g[j], at_w_o[j], cos, sin, topk)
        h = h + 0.5 * swiglu(rms_norm_2(h, g[2]), ffn_w_in[i, 1], ffn_w_out[i, 1])
    return h[:, N_META:]


def setup_inputs(seed=0):
    out = dict(first_inputs(seed))
    for name, value in second_inputs(seed + 1).items():
        if name != "x":
            out[name + "_2"] = value
    return out


def reference(
    x, attn_norm, w_in, conv_w, conv_b, conv_ln_g, conv_ln_b, cmp_k_pe, cmp_k_w1, cmp_k_w2,
    cmp_v_pe, cmp_v_w1, cmp_v_w2, w_out, ffn_norm, w_gate_up, w_down, final_norm, meta_2,
    norm_g_2, ffn_w_in_2, ffn_w_out_2, rk_mix_2, rk_w_r_2, rk_w_k_2, rk_w_v_2, rk_w_o_2,
    rk_w0_2, rk_w1_2, rk_w2_2, rk_a0_2, rk_a1_2, rk_a2_2, rk_g1_2, rk_g2_2, rk_k_k_2, rk_k_a_2,
    rk_r_k_2, rk_lnx_g_2, rk_lnx_b_2, at_w_in_2, at_q_g_2, at_k_g_2, at_w_o_2,
):
    x = first_block(
        x, attn_norm, w_in, conv_w, conv_b, conv_ln_g, conv_ln_b, cmp_k_pe, cmp_k_w1, cmp_k_w2,
        cmp_v_pe, cmp_v_w1, cmp_v_w2, w_out, ffn_norm, w_gate_up, w_down, final_norm,
    )
    return second_block(
        x, meta_2, norm_g_2, ffn_w_in_2, ffn_w_out_2, rk_mix_2, rk_w_r_2, rk_w_k_2, rk_w_v_2,
        rk_w_o_2, rk_w0_2, rk_w1_2, rk_w2_2, rk_a0_2, rk_a1_2, rk_a2_2, rk_g1_2, rk_g2_2,
        rk_k_k_2, rk_k_a_2, rk_r_k_2, rk_lnx_g_2, rk_lnx_b_2, at_w_in_2, at_q_g_2, at_k_g_2,
        at_w_o_2,
    )


_drawn_inputs = setup_inputs


def setup_inputs(seed=0):
    import zlib

    import numpy as np

    out = dict(_drawn_inputs(seed))
    spreads = {}
    factors = {'conv_b': 3.152,
     'conv_ln_b': 4.774,
     'cmp_k_pe': 4.954,
     'rk_w1_2': 3.674,
     'rk_w2_2': 3.62,
     'rk_k_k_2': 3.376,
     'rk_lnx_g_2': 3.051,
     'rk_lnx_b_2': 2.901,
     'at_q_g_2': 8.0,
     'at_k_g_2': 8.0}
    for name, (base, spread) in spreads.items():
        noise = np.random.default_rng([zlib.crc32(name.encode()), seed]).standard_normal(out[name].shape)
        drawn = base * np.exp(spread * noise) if base else spread * noise
        out[name] = jnp.asarray(drawn.astype(out[name].dtype))
    for name, factor in factors.items():
        out[name] = (out[name] * factor).astype(out[name].dtype)
    return out
```

```python
from contextlib import ExitStack

import numpy as np
import concourse.bass as bass
from concourse import mybir

F32 = mybir.dt.float32
ALU = mybir.AluOpType
ACT = mybir.ActivationFunctionType
AX = mybir.AxisListType
P = 128

T1 = 256
T2 = 272
NM = 16
KT = 8
DFF = 2816
MT = DFF // P
C = 68
NC = 4
CH = 2048
RING = 3
SLOT = 2208
BIG = 3.0e38
KAPPA = float(np.exp(-0.5))

HO1 = [0, 3, 1, 4, 2, 5, 6, 9, 7, 10, 8, 11]
HO2 = [0, 4, 1, 5, 2, 6, 3, 7, 8, 12, 9, 13, 10, 14, 11, 15]


def slopes12():
    s8 = [2.0 ** (-(i + 1)) for i in range(8)]
    s16 = [2.0 ** (-0.5 * (i + 1)) for i in range(16)]
    return np.asarray(s8 + s16[0::2][:4], dtype=np.float32)


class Ins:

    def __init__(self, q, fn, amount=1, sem=None):
        self.q, self.fn, self.wanted, self.value = q, fn, sem is not None, None
        self.amount, self.sem = amount, sem


class Queue:

    def __init__(self, sem):
        self.sem, self.items = sem, []

    def wait(self, *producers):
        for p in producers:
            if p is not None:
                p.wanted = True
                self.items.append(p)

    def op(self, fn, *producers):
        self.wait(*producers)
        i = Ins(self, fn)
        self.items.append((i,))
        return i

    def dma(self, fn, sem, *producers):
        self.wait(*producers)
        i = Ins(self, fn, 16, sem)
        self.items.append((i,))
        return i

    def last(self):
        for it in reversed(self.items):
            if isinstance(it, tuple):
                return it[0]
        return None

    def number(self, counts):
        for it in self.items:
            if isinstance(it, tuple) and it[0].wanted:
                i = it[0]
                s = i.sem if i.sem is not None else self.sem
                i.sem = s
                counts[s] = counts.get(s, 0) + i.amount
                i.value = counts[s]

    def emit(self, eng):
        seen = {}
        for it in self.items:
            if isinstance(it, tuple):
                i = it[0]
                r = i.fn(eng)
                if i.wanted:
                    r.then_inc(i.sem, i.amount)
            elif seen.get(it.sem, 0) < it.value:
                eng.wait_ge(it.sem, it.value)
                seen[it.sem] = it.value


class Bank:
    def __init__(self, ap):
        self.ap, self.free = ap, []


def consts():
    parts, at = [], {}
    n = 0

    def put(name, a):
        nonlocal n
        a = np.asarray(a, np.float32)
        full = np.zeros((P, a.shape[1]), np.float32)
        full[:a.shape[0]] = a
        parts.append(full)
        at[name] = n
        n += a.shape[1]

    p = np.arange(P)
    put("ident", np.eye(P))
    put("ones", np.ones((P, P)))
    E = np.zeros((P, KT, 16))
    for k in range(KT):
        E[p, k, 2 * k + p // 64] = 1.0
    put("E", E.reshape(P, -1))
    put("ET", E.transpose(2, 1, 0).reshape(16, -1))
    R = np.zeros((P, P))
    for b in (0, 64):
        for d in range(8):
            R[b + d, b + d + 8] = -1.0
            R[b + d + 8, b + d] = 1.0
    put("RT", R.T)
    inv = (np.float32(500000.0) ** (-np.arange(0, 16, 2, dtype=np.float32) / np.float32(16))).astype(np.float32)
    ang = np.arange(T2, dtype=np.float32)[:, None] * inv[None, :]
    cf, sf = np.ones((P, T2)), np.zeros((P, T2))
    for b in (0, 64):
        for d in range(16):
            cf[b + d] = np.cos(ang[:, d % 8])
            sf[b + d] = np.sin(ang[:, d % 8])
    put("cos", cf)
    put("sin", sf)
    s, t = np.arange(C)[:, None], np.arange(C)[None, :]
    put("mst", np.concatenate([(s < t), (s <= t)], axis=1))
    put("m1", ((s % 2 == 1) & (t == s - 1)))
    for lv in (1, 2, 4, 8, 16, 32, 64):
        put(f"l{lv}", (s // (2 * lv) == t // (2 * lv)) & (s // lv % 2 == 0) & (t // lv % 2 == 1))
    tq = np.arange(T1).reshape(2, P).T[:, :, None]
    pos = np.arange(T1)[None, None, :]
    put("D", np.where(pos <= tq, tq - pos, BIG).reshape(P, -1))
    sl = slopes12()
    n15 = np.arange(15)[None, None, None, :]
    t4 = tq[:, :, :, None]
    bc = -sl[HO1][None, None, :, None] * (t4 - (16.0 * n15 + 15.5))
    put("Bc", np.where(16 * n15 + 31 <= t4, bc, -BIG).reshape(P, -1))
    put("cm", np.where(t <= s, 0.0, -BIG))
    return np.concatenate(parts, axis=1), at


def params():
    want = [
        ("attn_norm", (0,), "col"), ("ffn_norm", (0,), "col"), ("final_norm", (), "col"),
        ("conv_w", (0,), "rows"), ("conv_b", (0,), "col"), ("conv_ln_g", (0,), "col"), ("conv_ln_b", (0,), "col"),
        ("cmp_k_pe", (0,), "pe"), ("cmp_v_pe", (0,), "pe"),
    ]
    for i in range(2):
        for j in range(3):
            want.append(("norm_g_2", (i, j), "col"))
    for j in range(6):
        want.append(("rk_mix_2", (0, j), "col"))
    for nm in ("rk_w0_2", "rk_a0_2", "rk_k_k_2", "rk_k_a_2", "rk_lnx_g_2", "rk_lnx_b_2"):
        want.append((nm, (0,), "col"))
    want.append(("rk_r_k_2", (0,), "col"))
    want.append(("at_q_g_2", (0,), "dup"))
    want.append(("at_k_g_2", (0,), "dup"))
    return want


PW = {"conv_w": 62, "conv_b": 2, "conv_ln_g": 2, "conv_ln_b": 2, "cmp_k_pe": 16, "cmp_v_pe": 16,
      "at_q_g_2": 1, "at_k_g_2": 1}


def param_offsets():
    at, n = {}, 0
    for name, idx, kind in params():
        at[(name,) + idx] = n
        n += PW.get(name, 8)
    return at, n


def pack_params(inp):
    out = []
    for name, idx, kind in params():
        a = np.asarray(inp[name])[idx]
        if kind == "col":
            a = a.reshape(-1, P).T
        elif kind == "rows":
            a = a.reshape(31, 2, P).transpose(2, 1, 0).reshape(P, 62)
        elif kind == "pe":
            a = a.reshape(16, P).T
        else:
            a = np.concatenate([a, a]).reshape(P, 1)
        out.append(a)
    return np.ascontiguousarray(np.concatenate(out, axis=1))


class Stream:

    def __init__(self, ring, sync, pe, sems):
        self.ring, self.sync, self.pe, self.sems = ring, sync, pe, sems
        self.plan, self.n, self.pos = [], 0, CH
        self.load = None
        self.last_use = []
        self.dram = None

    def tile(self, key, k0, kp, cols, w):
        if self.pos + w > CH:
            if self.n:
                self.last_use.append(self.pe.last())
            c = self.n
            self.n += 1
            self.pos = 0
            s = c % RING
            before = [self.last_use[c - RING]] if c >= RING else []
            self.load = self.sync.dma(
                lambda e, c=c, s=s: e.dma_start(self.ring[:, s * CH:(s + 1) * CH], self.dram[c]),
                self.sems[s], *before)
        off = self.pos
        self.pos += w
        c = self.n - 1
        self.plan.append((c, off, key, k0, kp, cols, w))
        s = c % RING
        return self.ring[0:kp, s * CH + off:s * CH + off + w], self.load


def build(nc, out, wdecl, cdram, pdram, xdram, mdram, NCOL, CAT, PAT, NPAR):
    with ExitStack() as ctx:
        def sb(name, n):
            return ctx.enter_context(nc.sbuf_tensor(name, [P, n], F32))

        def sem(name):
            return ctx.enter_context(nc.semaphore(name))

        h_ = sb("h", KT * T2)
        hn_ = sb("hn", KT * (T2 + 1))
        cs = sb("cs", NCOL)
        pr = sb("pr", NPAR)
        ring = sb("ring", RING * CH)
        AR = sb("arena", 15 * SLOT)
        ms = sb("misc", 2700)
        psum = [ctx.enter_context(nc.psum_tensor(f"ps{i}", [P, 512], F32)) for i in range(8)]

        pe, dve, act, pool, sp = (Queue(sem(n)) for n in ("s_pe", "s_dve", "s_act", "s_pool", "s_sp"))
        st = Stream(ring, sp, pe, [sem(f"s_ring{i}") for i in range(RING)])
        s_in = [sem(f"s_in{i}") for i in range(4)]
        s_x = [sem(f"s_cx{i}") for i in range(8)]
        s_out = sem("s_out")

        h = h_[:, :].rearrange("p (k t) -> p k t", k=KT)
        hn = hn_[:, :].rearrange("p (k t) -> p k t", k=KT)
        hx = h[:, :, NM:T2]

        def slot(i, off=0, n=SLOT, rows=P):
            return AR[0:rows, i * SLOT + off:i * SLOT + off + n]

        def v3(ap, a):
            return ap.rearrange("p (a b) -> p a b", a=a)

        def v4(ap, a, b):
            return ap.rearrange("p (a b c) -> p a b c", a=a, b=b)

        def con(name, n, rows=P):
            return cs[0:rows, CAT[name]:CAT[name] + n]

        def par(*key, i=0, rows=P):
            o = PAT[key] + i
            return pr[0:rows, o:o + 1]

        ident = con("ident", P)
        ones = con("ones", P)
        EH = v3(con("E", 128), KT)
        ETH = v3(con("ET", 1024, 16), KT)
        free = [Bank(p) for p in psum]

        def take():
            return free.pop(0)

        def give(b, *readers):
            b.free = list(readers)
            free.append(b)

        def mm(o, lhsT, rhs, start, stop, *w):
            return pe.op(lambda e: e.matmul(o, lhsT, rhs, start=start, stop=stop), *w)

        def tr(o, a, n, *w):
            return pe.op(lambda e: e.transpose(o, a, ident[0:n, 0:n]), *w)

        def tt(q, o, a, b, op, *w):
            return q.op(lambda e: e.tensor_tensor(o, a, b, op), *w)

        def stt(o, a, s, b, op0, op1, *w):
            return dve.op(lambda e: e.scalar_tensor_tensor(out=o, in0=a, scalar=s, in1=b, op0=op0, op1=op1), *w)

        def ts(q, o, a, s1, s2, op0, op1, *w):
            if op1 is None:
                return q.op(lambda e: e.tensor_scalar(o, a, s1, None, op0), *w)
            return q.op(lambda e: e.tensor_scalar(o, a, s1, s2, op0, op1), *w)

        def cp(q, o, a, *w):
            if q is act:
                return q.op(lambda e: e.activation(o, a, ACT.Copy), *w)
            return q.op(lambda e: e.tensor_copy(o, a), *w)

        def af(o, a, f, *w, bias=0.0, scale=1.0, acc=None):
            if acc is None:
                return act.op(lambda e: e.activation(o, a, f, bias=bias, scale=scale), *w)
            return act.op(lambda e: e.activation(o, a, f, bias=bias, scale=scale, accum_out=acc), *w)

        def rec(o, a, *w):
            return dve.op(lambda e: e.reciprocal(o, a), *w)

        def rsqrt(dst, psap, scale, eps, mmi, floor=None):
            a = ts(dve, dst, psap, scale, eps, ALU.mult, ALU.add, mmi)
            b = af(dst, dst, ACT.Sqrt, a)
            return rec(dst, dst, b), a

        d_c = act.dma(lambda e: e.dma_start(cs[:, :], cdram), s_in[0])
        d_p = act.dma(lambda e: e.dma_start(pr[:, :], pdram), s_in[1])
        d_x = sp.dma(lambda e: e.dma_start(hx, xdram), s_in[2])
        d_m = sp.dma(lambda e: e.dma_start(h[:, :, 0:NM], mdram), s_in[3])
        z0 = pool.op(lambda e: e.memset(hn[:, :, 0:1], 0.0))
        eps = ms[:, 2690:2691]

        def norm(src, T, key, ready, dst, w_dst=()):
            sq = slot(4)[:, 0:KT * T].rearrange("p (k t) -> p k t", k=KT)
            b = take()
            last = None
            for k in range(KT):
                i = af(sq[:, k, :], src[:, k, :], ACT.Square, ready[k], *(w_dst if k == 0 else ()))
                last = mm(b.ap[:, 0:T], ones, sq[:, k, :], k == 0, k == KT - 1, i, d_c, *(b.free if k == 0 else ()))
            rs = slot(3, 816, T)
            r, rd = rsqrt(rs, b.ap[:, 0:T], 1.0 / 1024, 1e-6, last)
            give(b, rd)
            res = []
            for k in range(KT):
                res.append(stt(dst[:, k, :], src[:, k, :], par(*key, i=k), rs, ALU.mult, ALU.mult, r, d_p))
            return res

        def dense(x, T, kt, key, n0, nw, ready, kp=P, b=None):
            b = take()
            last = None
            for k in range(kt):
                w, ld = st.tile(key, k * P, kp, (n0, nw), nw)
                last = mm(b.ap[0:nw, 0:T], w, x[:, k, :] if kt > 1 or kp == P else x, k == 0, k == kt - 1, ld,
                          ready[k], *(b.free if k == 0 else ()))
            return b, last

        def ffn(hv, T, nkey, w1, w2, scale, ready):
            xn = hn[:, :, 1:1 + T]
            rn = norm(hv, T, nkey, ready, xn)
            prod = AR[:, 0:MT * T].rearrange("p (m t) -> p m t", m=MT)
            done, tmp_use = [], [None] * 3
            for m in range(MT):
                bg, g = dense(xn, T, KT, w1, m * P, P, rn)
                bu, u = dense(xn, T, KT, w1, DFF + m * P, P, rn)
                tmp = slot(3, (m % 3) * T2, T)
                s = af(tmp, bg.ap[:, 0:T], ACT.Silu, g, tmp_use[m % 3])
                give(bg, s)
                i = tt(dve, prod[:, m, :], tmp, bu.ap[:, 0:T], ALU.mult, s, u)
                tmp_use[m % 3] = i
                give(bu, i)
                done.append(i)
            res = []
            for n in range(KT):
                b, i = dense(prod, T, MT, w2, n * P, P, done)
                r = stt(hv[:, n, :], b.ap[:, 0:T], scale, hv[:, n, :], ALU.mult, ALU.add, i)
                give(b, r)
                res.append(r)
            return res

        T = T1
        xn = hn[:, :, 1:1 + T]
        rn = norm(hx, T, ("attn_norm", 0), [d_x] * KT, xn)
        mix = v3(slot(0, 0, KT * T), KT)
        qT = v3(slot(1, 0, 6 * T), 6)
        ksT, kwT, kcT, vcT = (v3(slot(2, 512 * i, 512), 2) for i in range(4))
        V = v4(slot(3, 0, 1024), 2, 2)
        G = v3(slot(3, 1100, 72), 2)
        yp = v3(slot(3, 1200, 572), 2)
        Xc = [v3(slot(4, 1024 * i, 1024), 4) for i in range(2)]
        XW = [v3(slot(5, 976 * i, 976), 16) for i in range(2)]
        acc = v3(slot(6, 0, 512), 2)
        sqc = v3(slot(6, 512, 512), 2)
        mu = slot(6, 1024, 256)
        rsc = slot(6, 1280, 256)
        sg = v3(slot(6, 1536, 512), 2)
        zy = pool.op(lambda e: e.memset(yp[:, :, 0:30], 0.0))

        def proj(dst, n0, nt, eng, scale=None):
            res = []
            for i in range(nt):
                b, m = dense(xn, T, KT, ("w_in", 0), n0 + i * P, P, rn)
                if scale is None:
                    r = cp(eng, dst[:, i, :], b.ap[:, 0:T], m, z0)
                else:
                    r = af(dst[:, i, :], b.ap[:, 0:T], ACT.Copy, m, scale=scale)
                give(b, r)
                res.append(r)
            return res

        r_c = [proj(kcT, 1280, 2, dve), proj(vcT, 1536, 2, dve)]
        r_x = []
        for j, src in enumerate((kcT, vcT)):
            ds = []
            for gp in range(2):
                for par_ in range(2):
                    n = T - par_
                    ds.append(act.dma(
                        lambda e, j=j, gp=gp, par_=par_, n=n, src=src: e.dma_start(
                            Xc[j].rearrange("p (a b) t -> p a b t", b=2)[64 * par_:64 * par_ + 64, :, gp, 0:n],
                            src[64 * gp:64 * gp + 64, :, par_:par_ + n]),
                        s_x[4 * j + 2 * gp + par_], *r_c[j]))
            r_x.append(ds)
        for i in range(2):
            bu, u = dense(xn, T, KT, ("w_in", 0), i * P, P, rn)
            bv, v = dense(xn, T, KT, ("w_in", 0), 256 + i * P, P, rn)
            s = af(sg[:, i, :], bv.ap[:, 0:T], ACT.Sigmoid, v)
            give(bv, s)
            yi = tt(dve, yp[:, i, 30:286], bu.ap[:, 0:T], sg[:, i, :], ALU.mult, s, u)
            give(bu, yi)
            if i == 0:
                yi0 = yi
        r_q = proj(qT, 512, 6, act, scale=0.125)
        r_ks = proj(ksT, 1792, 2, act)
        r_kw = proj(kwT, 2304, 2, act)
        bs = [[take(), take()] for _ in range(2)]
        for k in range(KT):
            w, ld = st.tile("w_vg", k * P, P, (0, 548), 548)
            for t in range(2):
                x_ = xn[:, k, t * P:t * P + P]
                mm(bs[t][0].ap[:, 0:292], x_, w[:, 0:292], k == 0, k == KT - 1, ld, rn[k],
                   *((bs[t][0].free + bs[t][1].free) if k == 0 else ()))
                vl = mm(bs[t][1].ap[:, 0:256], x_, w[:, 292:548], k == 0, k == KT - 1)
        r_v, r_g = [], []
        for t in range(2):
            a = cp(act, V[:, t, 0, :], bs[t][0].ap[:, 0:256], vl)
            g_ = af(G[:, t, :], bs[t][0].ap[:, 256:292], ACT.Sigmoid, vl)
            c_ = cp(act, V[:, t, 1, :], bs[t][1].ap[:, 0:256], vl)
            give(bs[t][0], g_)
            give(bs[t][1], c_)
            r_v.append(c_)
            r_g.append(g_)
        hc = [v3(slot(12, 128 * j, 120), 2) for j in range(2)]
        kcc = slot(12, 300, 60)
        vcc = v3(slot(12, 400, 256, 15), 4)
        for j in range(2):
            a = pool.op(lambda e, j=j: e.tensor_copy(XW[j][:, :, 60], pr[:, PAT[(("cmp_k_pe", "cmp_v_pe")[j], 0)]:][:, 0:16]), d_p)
            for g in range(4):
                src = Xc[j][:, g, :]
                for l2 in range(16):
                    pass
                r = pool.op(lambda e, j=j, g=g: e.tensor_copy(
                    XW[j][:, 0:8, g * 15:g * 15 + 15],
                    Xc[j][:, g, 0:240].rearrange("p (n l) -> p l n", l=16)[:, 0:16:2, :]), *r_x[j])
                r2 = pool.op(lambda e, j=j, g=g: e.tensor_copy(
                    XW[j][:, 8:16, g * 15:g * 15 + 15],
                    Xc[j][:, g, 16:256].rearrange("p (n l) -> p l n", l=16)[:, 0:16:2, :]))
            rw = r2
            nm = ("cmp_k", "cmp_v")[j]
            r_h = []
            for ht in range(2):
                b = take()
                for l2 in range(16):
                    w, ld = st.tile(nm + "_w1", l2 * P, P, (ht * P, P), P)
                    m = mm(b.ap[:, 0:61], w, XW[j][:, l2, :], l2 == 0, l2 == 15, ld, rw,
                           *(b.free if l2 == 0 else ()))
                pc = slot(12, 700 + 2 * j + ht, 1)
                i1 = cp(dve, pc, b.ap[:, 60:61], m)
                i2 = af(hc[j][:, ht, :], b.ap[:, 0:60], ACT.Silu, i1, bias=pc)
                give(b, i2)
                r_h.append(i2)
            b = take()
            if j == 0:
                for ht in range(2):
                    w, ld = st.tile(nm + "_w2d", ht * P, P, (0, P), P)
                    m = mm(b.ap[:, 0:60], w, hc[j][:, ht, :], ht == 0, ht == 1, ld, r_h[ht], *b.free)
                r_kc = cp(dve, kcc, b.ap[:, 0:60], m)
                give(b, r_kc)
            else:
                wt = []
                for ht in range(2):
                    wt.append(st.tile(nm + "_w2", ht * P, P, (0, 64), 64))
                for g in range(4):
                    for ht in range(2):
                        m = mm(b.ap[0:15, g * 64:g * 64 + 64], hc[j][:, ht, g * 15:g * 15 + 15], wt[ht][0],
                               ht == 0, ht == 1, wt[ht][1], r_h[ht], *b.free)
                r_vc = cp(dve, vcc, v3(b.ap[0:15, 0:256], 4), m)
                give(b, r_vc)
        PcT = AR[0:15, 8 * SLOT:8 * SLOT + 3072].rearrange("p (t h q) -> p t h q", t=2, h=12)
        r_pc = []
        for t in range(2):
            bb = [take(), take()]
            for p in range(12):
                hf, g = p % 2, HO1[p] // 3
                m = mm(bb[hf].ap[:, p // 2 * 15:p // 2 * 15 + 15], qT[64 * hf:64 * hf + 64, p // 2, t * P:t * P + P],
                       kcc[64 * hf:64 * hf + 64, g * 15:g * 15 + 15], True, True, r_q[p // 2], r_kc,
                       *bb[hf].free)
            s4 = slot(7, t * 300, 180).rearrange("p (a f n) -> p a f n", a=6, f=2)
            B4 = con("Bc", 360)[:, t * 180:t * 180 + 180].rearrange("p (a f n) -> p a f n", a=6, f=2)
            r = []
            for hf in range(2):
                r.append(tt(dve, s4[:, :, hf, :], v3(bb[hf].ap[:, 0:90], 6), B4[:, :, hf, :], ALU.add, m))
                give(bb[hf], r[-1])
            s3 = v3(slot(7, t * 300, 180), 12)
            mx, cf = slot(7, t * 300 + 200, 12), slot(7, t * 300 + 220, 12)
            i = dve.op(lambda e, mx=mx, s3=s3: e.tensor_reduce(mx, s3, AX.X, ALU.max), *r)
            i = ts(dve, mx, mx, -1e35, None, ALU.max, None, i)
            i = tt(dve, s3, s3, mx.unsqueeze(2).to_broadcast([P, 12, 15]), ALU.subtract, i)
            i = af(s3, s3, ACT.Exp, i)
            i = dve.op(lambda e, cf=cf, s3=s3: e.tensor_reduce(cf, s3, AX.X, ALU.add), i)
            i = ts(dve, cf, cf, 1e-30, None, ALU.max, None, i)
            i = rec(cf, cf, i)
            i = tt(dve, cf, cf, G[:, t, 0:12], ALU.mult, i, r_g[t])
            i = tt(dve, s3, s3, cf.unsqueeze(2).to_broadcast([P, 12, 15]), ALU.mult, i)
            for q3 in range(3):
                b = take()
                for p in range(4):
                    m = tr(b.ap[0:15, p * P:p * P + P], s3[:, q3 * 4 + p, :], P, i, *b.free)
                c_ = cp(act, PcT[:, t, q3 * 4:q3 * 4 + 4, :], v3(b.ap[0:15, :], 4), m)
                give(b, c_)
            r_pc.append(c_)
        cv = [None, None]
        for j in range(31):
            for i in range(2):
                w = pr[:, PAT[("conv_w", 0)] + i * 31 + j:][:, 0:1]
                if j == 0:
                    cv[i] = ts(dve, acc[:, i, :], yp[:, i, 0:256], w, par("conv_b", 0, i=i), ALU.mult, ALU.add, zy, yi, yi0)
                else:
                    cv[i] = stt(acc[:, i, :], yp[:, i, j:j + 256], w, acc[:, i, :], ALU.mult, ALU.add, cv[i])
        sl = slopes12()
        units = [(t, p) for t in range(2) for p in range(12)]
        obank = {}
        s_use, pt_use = [None] * 3, [None] * 3
        stt_ = {}
        r_mix = {}

        def att_s(n):
            t, p = units[n]
            hf, g, kw = p % 2, HO1[p] // 3, P * (t + 1)
            b = take()
            q_ = qT[64 * hf:64 * hf + 64, p // 2, t * P:t * P + P]
            for br, kk_ in enumerate((ksT, kwT)):
                m = mm(b.ap[:, br * kw:br * kw + kw], q_, kk_[64 * hf:64 * hf + 64, g // 2, 0:kw], True, True,
                       r_q[p // 2], r_ks[g // 2], r_kw[g // 2], *b.free)
            s = v3(slot(10, (n % 3) * 512, 2 * kw), 2)
            D_ = con("D", 512)[:, t * 256:t * 256 + kw].unsqueeze(1).to_broadcast([P, 2, kw])
            a = stt(s, D_, -float(sl[HO1[p]]), v3(b.ap[:, 0:2 * kw], 2), ALU.mult, ALU.add, m, s_use[n % 3])
            give(b, a)
            o = 1600 + (n % 3) * 8
            mx, sm = slot(10, o, 2), slot(10, o + 2, 2)
            i = dve.op(lambda e: e.tensor_reduce(mx, s, AX.X, ALU.max, negate=True), a)
            for br in range(2):
                e_ = af(s[:, br, :], s[:, br, :], ACT.Exp, i, bias=mx[:, br:br + 1], acc=sm[:, br:br + 1])
            stt_[n] = (s, sm, e_)

        def att_p(n):
            t, p = units[n]
            s, sm, e_ = stt_[n]
            kw = P * (t + 1)
            i = ts(dve, sm, sm, 1e-30, None, ALU.max, None, e_)
            i = rec(sm, sm, i)
            i = tt(dve, sm, sm, G[:, t, 12 + p:36:12], ALU.mult, i, r_g[t])
            i = tt(dve, s, s, sm.unsqueeze(2).to_broadcast([P, 2, kw]), ALU.mult, i)
            stt_[n] = (s, i)

        def att_t(n):
            t, p = units[n]
            s, i = stt_[n]
            b = take()
            for br in range(2):
                for kc in range(t + 1):
                    m = tr(b.ap[:, (br * (t + 1) + kc) * P:][:, 0:P], s[:, br, kc * P:kc * P + P], P, i, *b.free)
            s_use[n % 3] = m
            n_ = 2 * (t + 1) * P
            pt = slot(11, (n % 3) * 512, n_)
            c_ = cp(act, pt, b.ap[:, 0:n_], m, pt_use[n % 3])
            give(b, c_)
            stt_[n] = (pt, c_)

        def att_v(n):
            t, p = units[n]
            hf, g = p % 2, HO1[p] // 3
            pt, c_ = stt_[n]
            if hf == 0:
                obank[n // 2] = take()
            b = obank[n // 2]
            o = b.ap[64 * hf:64 * hf + 64, 0:P]
            mm(o, vcc[:, g, :], PcT[:, t, p, :], True, False, r_vc, r_pc[t], c_, r_v[0], r_v[1], *b.free)
            for br in range(2):
                for kc in range(t + 1):
                    m = mm(o, V[:, kc, br, g * 64:g * 64 + 64], pt[:, (br * (t + 1) + kc) * P:][:, 0:P], False,
                           br == 1 and kc == t)
            pt_use[n % 3] = m
            if hf == 1:
                r = cp(act, mix[:, 2 + p // 2, t * P:t * P + P], b.ap[:, 0:P], m)
                give(b, r)
                r_mix[(p // 2, t)] = r

        for n in range(len(units) + 3):
            if n < len(units):
                att_s(n)
            if 0 <= n - 1 < len(units):
                att_p(n - 1)
            if 0 <= n - 2 < len(units):
                att_t(n - 2)
            if 0 <= n - 3 < len(units):
                att_v(n - 3)
        b = take()
        for i in range(2):
            m = mm(b.ap[:, 0:T], ones, acc[:, i, :], i == 0, i == 1, cv[i], *b.free)
        i_mu = af(mu, b.ap[:, 0:T], ACT.Copy, m, scale=1.0 / 256)
        give(b, i_mu)
        b = take()
        for i in range(2):
            a = tt(dve, acc[:, i, :], acc[:, i, :], mu, ALU.subtract, i_mu)
            a = af(sqc[:, i, :], acc[:, i, :], ACT.Square, a)
            m = mm(b.ap[:, 0:T], ones, sqc[:, i, :], i == 0, i == 1, a, *b.free)
        r, rd = rsqrt(rsc, b.ap[:, 0:T], 1.0 / 256, 1e-6, m)
        give(b, rd)
        r_m = []
        for i in range(2):
            a = stt(acc[:, i, :], acc[:, i, :], par("conv_ln_g", 0, i=i), rsc, ALU.mult, ALU.mult, r)
            r_m.append(af(mix[:, i, :], acc[:, i, :], ACT.Silu, a, bias=par("conv_ln_b", 0, i=i)))
        for i in range(6):
            r_m.append(r_mix[(i, 1)])
        rh = []
        for n in range(KT):
            b, m = dense(mix, T, KT, "w_out_p", n * P, P, r_m)
            r = tt(dve, hx[:, n, :], b.ap[:, 0:T], hx[:, n, :], ALU.add, m)
            give(b, r)
            rh.append(r)
        rh = ffn(hx, T, ("ffn_norm", 0), ("w_gate_up", 0), ("w_down", 0), 1.0, rh)
        rh = norm(hx, T, ("final_norm",), rh, hx)

        T = T2
        pool.wait(d_m)
        rh = [pool.op(lambda e: e.memset(ms[:, 2695:2696], 0.0), d_m, *rh)] * KT
        rh = ffn(h, T, ("norm_g_2", 0, 0), ("ffn_w_in_2", 0, 0), ("ffn_w_out_2", 0, 0), 0.5, rh)
        xn = hn[:, :, 1:1 + T]
        rn = norm(h, T, ("norm_g_2", 0, 1), rh, xn)

        def big(i):
            return v3(slot(i, 0, KT * T), KT)

        xx, xi, kT, aT, kkT, rT, vT, gT, icT = (big(0), [big(1), big(2)], big(3), big(4), big(5), big(6), big(7),
                                                big(8), big(9))
        Lc = v4(slot(10), KT, NC)
        cc = v4(slot(11), KT, NC)
        bon = big(14)
        lora = ms[:, 0:544]
        i_xx = tt(pool, xx, hn[:, :, 0:T], xn, ALU.subtract, z0, *rn)
        xi_use = [None, None]
        n_x = [0]

        def mixed(j):
            n = n_x[0] % 2
            n_x[0] += 1
            res = [stt(xi[n][:, k, :], xx[:, k, :], par("rk_mix_2", 0, j, i=k), xn[:, k, :], ALU.mult, ALU.add,
                       i_xx, xi_use[n]) for k in range(KT)]
            return xi[n], res, n

        def full(dst, key, x, res, n):
            out_ = []
            for i in range(KT):
                b, m = dense(x, T, KT, key, i * P, P, res)
                r = cp(act, dst[:, i, :], b.ap[:, 0:T], m)
                give(b, r)
                out_.append(r)
            xi_use[n] = m
            return out_

        def lora_up(key, kp, x_, ready, i, split=None):
            b = take()
            if split is None:
                w, ld = st.tile(key, 0, kp, (i * P, P), P)
                m = mm(b.ap[:, 0:T], w, x_, True, True, ld, ready, *b.free)
            else:
                w, ld = st.tile(key, 0, P, (i * P, P), P)
                mm(b.ap[:, 0:T], w, x_[0], True, False, ld, ready, *b.free)
                w, ld = st.tile(key, P, 32, (i * P, P), P)
                m = mm(b.ap[:, 0:T], w, x_[1], False, True, ld)
            return b, m

        x, r, n = mixed(1)
        b, m = dense(x, T, KT, ("rk_w1_2", 0), 0, 64, r)
        xi_use[n] = m
        i = af(lora[0:64, 0:T], b.ap[0:64, 0:T], ACT.Tanh, m)
        give(b, i)
        z1 = pool.op(lambda e: e.memset(Lc[:, :, :, 0:1], 0.0), *rn)
        sw = big(9)
        x2, r2, n2 = mixed(4)
        i_s = []
        for k in range(KT):
            b, m = lora_up(("rk_w2_2", 0), 64, lora[0:64, 0:T], i, k)
            s = af(sw[:, k, :], b.ap[:, 0:T], ACT.Sigmoid, m, bias=par("rk_w0_2", 0, i=k))
            give(b, s)
            i_s.append(s)
        b, m = dense(x2, T, KT, ("rk_a1_2", 0), 0, 64, r2)
        xi_use[n2] = m
        i = cp(act, lora[0:64, T:2 * T], b.ap[0:64, 0:T], m)
        give(b, i)
        z_ones = con("ones", C)
        r_L = []
        for k in range(KT):
            for c in range(NC):
                l = dve.op(lambda e, k=k, c=c: e.tensor_tensor_scan(
                    Lc[:, k, c, 1:C + 1], z_ones, sw[:, k, c * C:c * C + C], 0.0, ALU.mult, ALU.add), i_s[k], z1)
            r_L.append(l)
        i_a = []
        for k in range(KT):
            b, m = lora_up(("rk_a2_2", 0), 64, lora[0:64, T:2 * T], i, k)
            s = af(aT[:, k, :], b.ap[:, 0:T], ACT.Sigmoid, m, bias=par("rk_a0_2", 0, i=k))
            give(b, s)
            i_a.append(s)
        x, r, n = mixed(2)
        r_k = full(kT, ("rk_w_k_2", 0), x, r, n)
        x, r, n = mixed(5)
        b, m0 = dense(x, T, KT, ("rk_g1_2", 0), 0, P, r)
        b2, m = dense(x, T, KT, ("rk_g1_2", 0), P, 32, r)
        xi_use[n] = m
        gl = ms[:, 600:600 + 2 * T]
        g0 = af(gl[:, 0:T], b.ap[:, 0:T], ACT.Sigmoid, m0)
        g1 = af(gl[0:32, T:2 * T], b2.ap[0:32, 0:T], ACT.Sigmoid, m)
        give(b, g0)
        give(b2, g1)
        i_g = []
        for k in range(KT):
            b, m = lora_up(("rk_g2_2", 0), 0, (gl[:, 0:T], gl[0:32, T:2 * T]), g1, k, split=True)
            s = cp(act, gT[:, k, :], b.ap[:, 0:T], m)
            give(b, s)
            i_g.append(s)
        x, r, n = mixed(0)
        r_r = full(rT, ("rk_w_r_2", 0), x, r, n)
        x, r, n = mixed(3)
        r_v = full(vT, ("rk_w_v_2", 0), x, r, n)
        e_c, e_i = [], []
        for k in range(KT):
            e_c.append(af(cc[:, k, :, :], Lc[:, k, :, :], ACT.Exp, r_L[k], z1, scale=-KAPPA))
            e_i.append(af(icT[:, k, :].rearrange("p (c t) -> p c t", c=NC), Lc[:, k, :, 1:C + 1], ACT.Exp, scale=KAPPA))

        def head_sums(src, ready):
            b = take()
            for k in range(KT):
                m = mm(b.ap[0:16, 0:T], EH[:, k, :], src(k), k == 0, k == KT - 1, ready[k], *b.free)
            return b, m

        def spread(src16, k, *ready):
            b = take()
            m = mm(b.ap[:, 0:T], ETH[:, k, :], src16, True, True, *ready, *b.free)
            return b, m

        tmpk = big(1)
        w_kk = []
        ka1 = ms[:, 2600:2608]
        kap = pr[:, PAT[("rk_k_a_2", 0)]:][:, 0:8]
        i_ka = ts(dve, ka1, kap, -1.0, 1.0, ALU.mult, ALU.add)
        r_kk, r_sq = [], []
        for k in range(KT):
            r_kk.append(ts(dve, kkT[:, k, :], kT[:, k, :], par("rk_k_k_2", 0, i=k), None, ALU.mult, None, r_k[k]))
            r_sq.append(af(tmpk[:, k, :], kkT[:, k, :], ACT.Square, r_kk[k], xi_use[0], xi_use[1]))
        b, m = head_sums(lambda k: tmpk[:, k, :], r_sq)
        s16 = ms[0:16, 0:T]
        i = ts(dve, s16, b.ap[0:16, 0:T], 1e-24, None, ALU.max, None, m, m)
        give(b, i)
        i = af(s16, s16, ACT.Sqrt, i)
        i16 = rec(s16, s16, i)
        r_kn = []
        for k in range(KT):
            b, m = spread(s16, k, i16)
            i = tt(dve, kkT[:, k, :], kkT[:, k, :], b.ap[:, 0:T], ALU.mult, m)
            give(b, i)
            r_kn.append(i)
        r_kp, r_p = [], []
        r_sq2 = []
        for k in range(KT):
            i = ts(dve, tmpk[:, k, :], aT[:, k, :], par("rk_k_a_2", 0, i=k), ka1[:, k:k + 1], ALU.mult, ALU.add,
                   i_a[k], i_ka, r_kn[k])
            i = tt(dve, kT[:, k, :], kT[:, k, :], tmpk[:, k, :], ALU.mult, i)
            r_kp.append(i)
            j = stt(tmpk[:, k, :], rT[:, k, :], par("rk_r_k_2", 0, i=k), kT[:, k, :], ALU.mult, ALU.mult, i, r_r[k])
            r_sq2.append(j)
        b, m = head_sums(lambda k: tmpk[:, k, :], r_sq2)
        s16b = ms[0:16, 300:300 + T]
        i16 = cp(dve, s16b, b.ap[0:16, 0:T], m)
        give(b, i16)
        r_bon = []
        for k in range(KT):
            b, m = spread(s16b, k, i16)
            i = tt(dve, bon[:, k, :], vT[:, k, :], b.ap[:, 0:T], ALU.mult, m, r_v[k])
            give(b, i)
            r_bon.append(i)
        pre = []
        for k in range(KT):
            v_ = lambda a: a[:, k, :].rearrange("p (c t) -> p c t", c=NC)
            i = tt(pool, aT[:, k, :], aT[:, k, :], kkT[:, k, :], ALU.mult, r_kn[k], r_kp[k], i_a[k])
            i = tt(pool, aT[:, k, :], aT[:, k, :], icT[:, k, :], ALU.mult, i, e_i[k])
            j = tt(pool, kT[:, k, :], kT[:, k, :], icT[:, k, :], ALU.mult, r_sq2[k])
            l = tt(dve, v_(rT), v_(rT), cc[:, k, :, 1:C + 1], ALU.mult, e_c[k], r_sq2[k])
            o = stt(v_(kkT), v_(kkT), -1.0, cc[:, k, :, 0:C], ALU.mult, ALU.mult, i)
            pre.append((j, l, o))
        p_pool, p_dve = pre[-1][0], pre[-1][2]

        def hm(i, j, n=1088):
            return slot(i, j * 1088, n, C)

        AbT, Dm, DT, Xb, LT0, LT1 = hm(0, 0), hm(0, 1), hm(1, 0), hm(1, 1), hm(2, 0), hm(2, 1)
        BR = slot(9, 0, 2176, C).rearrange("p (h a t) -> p h a t", h=16, a=2)
        KR = slot(10, 0, 2176, C).rearrange("p (h a t) -> p h a t", h=16, a=2)
        AbT, Dm, DT, Xb = (v3(a, 16) for a in (AbT, Dm, DT, Xb))
        LTs = [v3(LT0, 16), v3(LT1, 16)]
        tokA, tokB = slot(12, 0, 1024, C), slot(12, 1024, 1024, C)
        tokK, tokV = slot(13, 0, 1024, C), slot(13, 1024, 1024, C)
        tk = [a.rearrange("p (k f d) -> p k f d", k=8, f=2) for a in (tokA, tokB, tokK, tokV)]
        AkV = v3(hn_[0:C, 0:1024], 16)
        W2 = v3(hn_[0:C, 1024:2048], 16)
        W1T = v3(ms[:, 0:544], 8)
        U = v3(ms[0:C, 544:1568], 16)
        M = v3(ms[:, 1568:2080], 8)
        Mi = v3(ms[:, 2080:2592], 8)
        lv = (2, 4, 8, 16, 32, 64)
        i_M = pool.op(lambda e: e.memset(M[:, :, :], 0.0), *r_bon, g1, p_dve)
        r_y = [None] * NC
        prev_tok = []
        prev_seq = []
        id68 = ident[0:C, 0:C]

        def bc4(ap, n=4):
            return ap.unsqueeze(1).to_broadcast([C, n, ap.shape[-1]])

        def chunk(c, i_M, prev):
            t0 = c * C
            w_prev = list(prev)
            r_t = []
            for n_, src in enumerate((kkT, aT, kT, vT)):
                for hb in range(2):
                    b = take()
                    for k in range(4):
                        m = tr(b.ap[0:C, k * P:k * P + P], src[:, hb * 4 + k, t0:t0 + C], P, p_pool, p_dve, i_M, *b.free)
                    q = act if (n_ + hb) % 2 else dve
                    dst = (tokA, tokB, tokK, tokV)[n_][:, hb * 512:hb * 512 + 512]
                    r = cp(q, dst, b.ap[0:C, :], m, *w_prev)
                    give(b, r)
                    r_t.append(r)
            gr = {}
            for quad in range(4):
                hf, k0 = quad // 2, (quad % 2) * 4
                hs = slice(quad * 4, quad * 4 + 4)
                rows = slice(64 * hf, 64 * hf + 64)
                ra = []
                for src, dst in ((aT, BR), (kT, KR)):
                    for pair in range(2):
                        b = take()
                        for k in range(2):
                            kk_ = k0 + 2 * pair + k
                            for z, rr in enumerate((kkT, rT)):
                                m = mm(b.ap[0:C, k * 136 + z * C:k * 136 + z * C + C], src[rows, kk_, t0:t0 + C],
                                       rr[rows, kk_, t0:t0 + C], True, True, *b.free)
                        h0 = quad * 4 + pair * 2
                        o = dst[:, h0:h0 + 2, :, :].rearrange("p h a t -> p h (a t)")
                        r = tt(dve, o, v3(b.ap[0:C, 0:272], 2), bc4(con("mst", 136, C), 2), ALU.mult, m, *w_prev)
                        give(b, r)
                        ra.append(r)
                b = take()
                for k in range(4):
                    m = mm(b.ap[0:C, k * C:k * C + C], kkT[rows, k0 + k, t0:t0 + C], aT[rows, k0 + k, t0:t0 + C],
                           True, True, *b.free)
                r = tt(dve, Dm[:, hs, :], v3(b.ap[0:C, 0:272], 4), bc4(con("m1", C, C)), ALU.mult, m, *w_prev)
                give(b, r)
                rD = tt(pool, Dm[:, hs, :], Dm[:, hs, :], bc4(id68), ALU.add, r)
                ab = BR[:, hs, 0, :]
                i = tt(pool, DT[:, hs, :], ab, bc4(con("l1", C, C)), ALU.mult, *ra, *w_prev)
                rT_ = tt(pool, DT[:, hs, :], DT[:, hs, :], bc4(id68), ALU.add, i)
                gr[quad] = (rD, rT_, ra)
            use = {}
            rD = {q: gr[q][0] for q in range(4)}
            rT_ = {q: gr[q][1] for q in range(4)}
            rL = {}
            lt_use = [{}, {}]

            def masks(li):
                for quad in range(4):
                    hs = slice(quad * 4, quad * 4 + 4)
                    rL[(li, quad)] = tt(pool, LTs[li % 2][:, hs, :], BR[:, hs, 0, :], bc4(con(f"l{lv[li]}", C, C)),
                                        ALU.mult, *gr[quad][2], lt_use[li % 2].get(quad))
            masks(0)
            for li in range(6):
                if li + 1 < 6:
                    masks(li + 1)
                LT = LTs[li % 2]
                rX = {}
                for quad in range(4):
                    b = take()
                    for k in range(4):
                        hh = quad * 4 + k
                        m = mm(b.ap[0:C, k * C:k * C + C], LT[:, hh, :], Dm[:, hh, :], True, True,
                               rL[(li, quad)], rD[quad], *b.free)
                    lt_use[li % 2][quad] = m
                    rX[quad] = cp(act, Xb[:, quad * 4:quad * 4 + 4, :], v3(b.ap[0:C, 0:272], 4), m, use.get(quad))
                    give(b, rX[quad])
                for quad in range(4):
                    hs = slice(quad * 4, quad * 4 + 4)
                    if li < 5:
                        b = take()
                        for k in range(4):
                            hh = quad * 4 + k
                            m = mm(b.ap[0:C, k * C:k * C + C], DT[:, hh, :], Xb[:, hh, :], True, True,
                                   rX[quad], rT_[quad], *b.free)
                    b2 = take()
                    for k in range(4):
                        hh = quad * 4 + k
                        m2 = mm(b2.ap[0:C, k * C:k * C + C], Xb[:, hh, :], DT[:, hh, :], True, True,
                                rX[quad], rT_[quad], *b2.free)
                    use[quad] = m2
                    if li < 5:
                        rD[quad] = tt(dve, Dm[:, hs, :], v3(b.ap[0:C, 0:272], 4), Dm[:, hs, :], ALU.add, m)
                        give(b, rD[quad])
                    rT_[quad] = tt(dve, DT[:, hs, :], v3(b2.ap[0:C, 0:272], 4), DT[:, hs, :], ALU.add, m2)
                    give(b2, rT_[quad])
            r1, rk_, r2_ = [], {}, {}
            for quad in range(4):
                hf, k0 = quad // 2, (quad % 2) * 4
                b = take()
                for k in range(4):
                    m = mm(b.ap[64 * hf:64 * hf + 64, k * C:k * C + C], tk[0][:, k0 + k, hf, :], DT[:, quad * 4 + k, :],
                           True, True, rT_[quad], *r_t, *b.free)
                r = cp(act, W1T[64 * hf:64 * hf + 64, k0:k0 + 4, :], v3(b.ap[64 * hf:64 * hf + 64, 0:272], 4), m, *w_prev)
                give(b, r)
                r1.append(r)
                b = take()
                for k in range(4):
                    m = mm(b.ap[0:C, k * 64:k * 64 + 64], KR[:, quad * 4 + k, 0, :], tk[3][:, k0 + k, hf, :],
                           True, True, *gr[quad][2], *b.free)
                r = cp(act, AkV[:, quad * 4:quad * 4 + 4, :], v3(b.ap[0:C, 0:256], 4), m, *w_prev)
                give(b, r)
                rk_[quad] = r
            for quad in range(4):
                b = take()
                for k in range(4):
                    m = mm(b.ap[0:C, k * 64:k * 64 + 64], DT[:, quad * 4 + k, :], AkV[:, quad * 4 + k, :],
                           True, True, rk_[quad], *b.free)
                r2_[quad] = cp(act, W2[:, quad * 4:quad * 4 + 4, :], v3(b.ap[0:C, 0:256], 4), m, *w_prev)
                give(b, r2_[quad])
            rU = []
            for hf in range(2):
                b = take()
                for k in range(8):
                    m = mm(b.ap[0:C, k * 64:k * 64 + 64], W1T[64 * hf:64 * hf + 64, k, :], M[64 * hf:64 * hf + 64, k, :],
                           True, True, *r1, i_M, *b.free)
                r = tt(dve, U[:, hf * 8:hf * 8 + 8, :], v3(b.ap[0:C, :], 8), W2[:, hf * 8:hf * 8 + 8, :], ALU.add, m,
                       r2_[3], *w_prev)
                give(b, r)
                rU.append(r)
            ys = []
            for hf in range(2):
                rows = slice(64 * hf, 64 * hf + 64)
                for kb in range(2):
                    b = take()
                    for k in range(kb * 4, kb * 4 + 4):
                        o = b.ap[rows, (k % 4) * C:(k % 4) * C + C]
                        hh = hf * 8 + k
                        mm(o, M[rows, k, :], rT[rows, k, t0:t0 + C], True, False, rU[hf], *b.free)
                        mm(o, U[:, hh, :], BR[:, hh, 1, :], False, False)
                        m = mm(o, tk[3][:, k, hf, :], KR[:, hh, 1, :], False, True)
                    ys.append((b, m, rows, kb))
            b = take()
            for hf in range(2):
                for k in range(8):
                    o = b.ap[64 * hf:64 * hf + 64, k * 64:k * 64 + 64]
                    mm(o, tk[1][:, k, hf, :], U[:, hf * 8 + k, :], True, False, *b.free)
                    m = mm(o, tk[2][:, k, hf, :], tk[3][:, k, hf, :], False, True)
            i = tt(dve, M[:, :, :], v3(b.ap[:, :], 8), M[:, :, :], ALU.add, m, i_M)
            give(b, i)
            i_M = tt(dve, M[:, :, :], M[:, :, :], cc[:, :, c, C:C + 1].to_broadcast([P, 8, 64]), ALU.mult, i)
            ry = []
            for b, m, rows, kb in ys:
                r = cp(act, rT[rows, kb * 4:kb * 4 + 4, t0:t0 + C], v3(b.ap[rows, 0:272], 4), m)
                give(b, r)
                ry.append(r)
            return i_M, [pe.last()], ry[-1]

        prev = []
        for c in range(NC):
            i_M, prev, r_y[c] = chunk(c, i_M, prev)
        y, sq = rT, big(9)
        b, m = head_sums(lambda k: y[:, k, :], [r_y[3]] * KT)
        i16 = ts(dve, s16, b.ap[0:16, 0:T], 1.0 / 64, None, ALU.mult, None, m, i_M)
        give(b, i16)
        r_yc, r_s = [], []
        for k in range(KT):
            b, m = spread(s16, k, i16)
            i = tt(dve, y[:, k, :], y[:, k, :], b.ap[:, 0:T], ALU.subtract, m)
            give(b, i)
            r_yc.append(i)
            r_s.append(af(sq[:, k, :], y[:, k, :], ACT.Square, i))
        b, m = head_sums(lambda k: sq[:, k, :], r_s)
        i16, rd = rsqrt(s16b, b.ap[0:16, 0:T], 1.0 / 64, 64e-5, m)
        give(b, rd)
        r_o = []
        for k in range(KT):
            b, m = spread(s16b, k, i16)
            i = stt(y[:, k, :], y[:, k, :], par("rk_lnx_g_2", 0, i=k), b.ap[:, 0:T], ALU.mult, ALU.mult, m)
            give(b, i)
            i = stt(y[:, k, :], y[:, k, :], par("rk_lnx_b_2", 0, i=k), bon[:, k, :], ALU.add, ALU.add, i)
            r_o.append(tt(dve, y[:, k, :], y[:, k, :], gT[:, k, :], ALU.mult, i, i_g[k]))
        rh = []
        for n in range(KT):
            b, m = dense(y, T, KT, ("rk_w_o_2", 0), n * P, P, r_o)
            r = tt(dve, h[:, n, :], b.ap[:, 0:T], h[:, n, :], ALU.add, m)
            give(b, r)
            rh.append(r)
        zz = pool.op(lambda e: e.memset(hn[:, :, 0:1], 0.0), pe.last())
        rh = ffn(h, T, ("norm_g_2", 0, 2), ("ffn_w_in_2", 0, 1), ("ffn_w_out_2", 0, 1), 0.5, rh)

        rh = ffn(h, T, ("norm_g_2", 1, 0), ("ffn_w_in_2", 1, 0), ("ffn_w_out_2", 1, 0), 0.5, rh)
        rn = norm(h, T, ("norm_g_2", 1, 1), rh, xn)
        Q = big(0)
        K7 = v3(slot(1, 0, 7 * T), 7)
        KK, QI, KI = K7[:, 0:2, :], K7[:, 2:6, :], K7[:, 6:7, :]
        Vt = v3(slot(2, 0, 4 * 264, C), 4)
        oT = big(3)
        tmp = v3(slot(4, 0, 8 * T), 8)
        cosF, sinF = con("cos", T2), con("sin", T2)
        bias = v3(slot(5, 0, 4 * T, C), 4)

        def rope(dst, i, psap, b, m, tmp_i, t_use):
            pass

        jobs = [(KI[:, 0, :], 6, None)] + [(QI[:, i, :], 2 + i, None) for i in range(4)] \
            + [(KK[:, i, :], i, "at_k_g_2") for i in range(2)] + [(Q[:, i, :], 7 + i, "at_q_g_2") for i in range(8)]
        colof = lambda j: ("at_qk", j * P)
        state = {}
        ntmp = [None] * 4
        res_of = {}

        def d1(n):
            dst, j, g = jobs[n]
            b, m = dense(xn, T, KT, "at_qk", j * P, P, rn)
            r = cp(act, dst, b.ap[:, 0:T], m)
            give(b, r)
            state[n] = r

        def d1b(n):
            dst, j, g = jobs[n]
            r = state[n]
            if g is None:
                return
            sq_ = tmp[:, n % 4, :]
            a = af(sq_, dst, ACT.Square, r, ntmp[n % 4])
            b = take()
            m = mm(b.ap[0:16, 0:T], EH[:, 0, :], sq_, True, True, a, *b.free)
            q_ = ms[0:16, (n % 2) * 300:(n % 2) * 300 + T]
            i, rd = rsqrt(q_, b.ap[0:16, 0:T], 1.0 / 64, 1e-6, m)
            give(b, rd)
            b, m = spread(q_, 0, i)
            i = stt(dst, dst, par(g, 0), b.ap[:, 0:T], ALU.mult, ALU.mult, m)
            give(b, i)
            state[n] = i

        def d2(n):
            dst, j, g = jobs[n]
            r = state[n]
            b = take()
            m = mm(b.ap[:, 0:T], con("RT", P), dst, True, True, r, *b.free)
            t_ = tmp[:, 4 + n % 4, :]
            i = tt(dve, t_, b.ap[:, 0:T], sinF, ALU.mult, m)
            give(b, i)
            i2 = tt(dve, dst, dst, cosF, ALU.mult, m)
            i = tt(dve, dst, dst, t_, ALU.add, i, i2)
            ntmp[n % 4] = m
            state[n] = i

        for n in range(len(jobs) + 2):
            if n < len(jobs):
                d1(n)
            if 0 <= n - 1 < len(jobs):
                d1b(n - 1)
            if 0 <= n - 2 < len(jobs):
                d2(n - 2)
        bs = [take() for _ in range(NC)]
        for k in range(KT):
            w, ld = st.tile("at_vw", k * P, P, (0, 264), 264)
            for c in range(NC):
                vl = mm(bs[c].ap[0:C, 0:264], xn[:, k, c * C:c * C + C], w, k == 0, k == KT - 1, ld, rn[k],
                        *(bs[c].free if k == 0 else ()))
        r_v = []
        for c in range(NC):
            a = cp(act, Vt[:, c, 0:256], bs[c].ap[0:C, 0:256], vl)
            a = af(Vt[:, c, 256:264], bs[c].ap[0:C, 256:264], ACT.Copy, vl, scale=float(8 ** -0.5 * 64 ** -0.5))
            give(bs[c], a)
            r_v.append(a)
        sc = v3(slot(9, 0, 1088, C), 4)
        wk = v3(slot(9, 1088, 1088, C), 4)
        rel = v3(slot(10, 0, 1088, C), 4)
        t8 = slot(10, 1100, 64, C)
        eqb, gtb = v3(slot(11, 0, 1088, C), 4), v3(slot(11, 1088, 1088, C), 4)
        csb = v3(slot(12, 0, 1088, C), 4)
        rel_use = [None] * 4
        i_acc = {}
        nr = 0
        for c in (3, 2, 1, 0):
            kw = (c + 1) * C
            for hh in range(8):
                hf = hh % 2
                b = take()
                m = mm(b.ap[0:C, 0:kw], QI[64 * hf:64 * hf + 64, hh // 2, c * C:c * C + C],
                       KI[64 * hf:64 * hf + 64, 0, 0:kw], True, True, state[0], state[1 + hh // 2], *b.free)
                rr = rel[:, nr % 4, 0:kw]
                a = af(rr, b.ap[0:C, 0:kw], ACT.Relu, m, rel_use[nr % 4])
                give(b, a)
                w_ = Vt[:, c, 256 + hh:257 + hh]
                if hh == 0:
                    i = ts(dve, sc[:, c, 0:kw], rr, w_, None, ALU.mult, None, a, r_v[c])
                else:
                    i = stt(sc[:, c, 0:kw], rr, w_, sc[:, c, 0:kw], ALU.mult, ALU.add, a, i)
                rel_use[nr % 4] = i
                nr += 1
            i_acc[c] = tt(dve, sc[:, c, c * C:kw], sc[:, c, c * C:kw], con("cm", C, C), ALU.add, i)
        cur = {}
        for rnd in range(8):
            for c in range(NC):
                kw = (c + 1) * C
                src = sc if rnd == 0 else wk
                i = dve.op(lambda e, c=c, kw=kw, src=src: e.max(t8[:, c * 8:c * 8 + 8], src[:, c, 0:kw]),
                           i_acc[c] if rnd == 0 else cur[c])
                cur[c] = i
            if rnd < 7:
                for c in range(NC):
                    kw = (c + 1) * C
                    src = sc if rnd == 0 else wk
                    cur[c] = dve.op(lambda e, c=c, kw=kw, src=src: e.match_replace(
                        wk[:, c, 0:kw], t8[:, c * 8:c * 8 + 8], src[:, c, 0:kw], -BIG), cur[c])
        r_b = {}
        cnt = slot(10, 1200, 8, C)
        for c in range(NC):
            kw = (c + 1) * C
            th = t8[:, c * 8 + 7:c * 8 + 8]
            S_, e_, g_, q_ = sc[:, c, 0:kw], eqb[:, c, 0:kw], gtb[:, c, 0:kw], csb[:, c, 0:kw]
            cn = cnt[:, c:c + 1]
            i1 = ts(dve, g_, S_, th, None, ALU.is_gt, None, cur[c])
            i2 = ts(dve, e_, S_, th, None, ALU.is_equal, None)
            i3 = dve.op(lambda e, cn=cn, g_=g_: e.tensor_reduce(cn, g_, AX.X, ALU.add), i1)
            i4 = ts(dve, cn, cn, -1.0, 64.0, ALU.mult, ALU.add, i3)
            o_ = con("ones", 1, C).to_broadcast([C, kw])
            i5 = dve.op(lambda e, q_=q_, e_=e_, o_=o_: e.tensor_tensor_scan(q_, o_, e_, 0.0, ALU.mult, ALU.add), i2)
            i6 = stt(q_, q_, cn, e_, ALU.is_le, ALU.mult, i5, i4)
            i7 = tt(dve, q_, q_, g_, ALU.add, i6)
            B_ = bias[:, c, 0:kw]
            i8 = ts(dve, B_, q_, BIG, -BIG, ALU.mult, ALU.add, i7)
            r_b[c] = tt(dve, bias[:, c, c * C:kw], bias[:, c, c * C:kw], con("cm", C, C), ALU.min, i8)
        units = [(c, g) for c in range(NC) for g in range(4)]
        s_use, pt_use, stt_ = [None] * 3, [None] * 2, {}
        r_oT = {}

        def a_s(n):
            c, g = units[n]
            hf, k0, kw = g % 2, (g // 2) * 4, (c + 1) * C
            s = v3(slot((6, 7, 4)[n % 3], 0, 4 * kw, C), 4)
            for k in range(4):
                b = take()
                m = mm(b.ap[0:C, 0:kw], Q[64 * hf:64 * hf + 64, k0 + k, c * C:c * C + C],
                       KK[64 * hf:64 * hf + 64, g // 2, 0:kw], True, True, state[5 + g // 2], state[7 + k0 + k], *b.free)
                i = stt(s[:, k, :], b.ap[0:C, 0:kw], 0.125, bias[:, c, 0:kw], ALU.mult, ALU.add, m, r_b[c],
                        s_use[n % 3])
                give(b, i)
            mx, sm = slot((6, 7, 4)[n % 3], 1100, 4, C), slot((6, 7, 4)[n % 3], 1110, 4, C)
            i = dve.op(lambda e: e.tensor_reduce(mx, s, AX.X, ALU.max, negate=True), i)
            for k in range(4):
                e_ = af(s[:, k, :], s[:, k, :], ACT.Exp, i, bias=mx[:, k:k + 1], acc=sm[:, k:k + 1])
            stt_[n] = (s, sm, e_)

        def a_p(n):
            c, g = units[n]
            s, sm, e_ = stt_[n]
            kw = (c + 1) * C
            i = rec(sm, sm, e_)
            i = tt(dve, s, s, sm.unsqueeze(2).to_broadcast([C, 4, kw]), ALU.mult, i)
            stt_[n] = (s, i)

        def a_t(n):
            c, g = units[n]
            s, i = stt_[n]
            pt = v3(slot(8, (n % 2) * 1088, 1088, C), 4)
            for kc in range(c + 1):
                b = take()
                for k in range(4):
                    m = tr(b.ap[0:C, k * C:k * C + C], s[:, k, kc * C:kc * C + C], C, i, *b.free)
                r = cp(act, pt[:, kc, :], b.ap[0:C, 0:272], m, pt_use[n % 2])
                give(b, r)
            s_use[n % 3] = m
            stt_[n] = (pt, r)

        def a_v(n):
            c, g = units[n]
            pt, r = stt_[n]
            hf, k0 = g % 2, (g // 2) * 4
            b = take()
            for kc in range(c + 1):
                m = mm(b.ap[64 * hf:64 * hf + 64, 0:272], Vt[:, kc, g * 64:g * 64 + 64], pt[:, kc, :], kc == 0,
                       kc == c, r, r_v[kc], *b.free)
            pt_use[n % 2] = m
            i = cp(act, oT[64 * hf:64 * hf + 64, k0:k0 + 4, c * C:c * C + C], v3(b.ap[64 * hf:64 * hf + 64, 0:272], 4), m)
            give(b, i)
            r_oT[(c, g)] = i

        for n in range(len(units) + 3):
            if n < len(units):
                a_s(n)
            if 0 <= n - 1 < len(units):
                a_p(n - 1)
            if 0 <= n - 2 < len(units):
                a_t(n - 2)
            if 0 <= n - 3 < len(units):
                a_v(n - 3)
        ro = [r_oT[(3, 3)]] * KT
        rh = []
        for n in range(KT):
            b, m = dense(oT, T, KT, "at_w_o_p", n * P, P, ro)
            r = tt(dve, h[:, n, :], b.ap[:, 0:T], h[:, n, :], ALU.add, m)
            give(b, r)
            rh.append(r)
        rh = ffn(h, T, ("norm_g_2", 1, 2), ("ffn_w_in_2", 1, 1), ("ffn_w_out_2", 1, 1), 0.5, rh)
        d_o = sp.dma(lambda e: e.dma_start(out, hx), s_out, *rh)
        sp.wait(d_o)

        st.dram = wdecl(st.n)
        counts = {}
        for q in (pe, dve, act, pool, sp):
            q.number(counts)
        block = ctx.enter_context(nc.Block())

        @block.sync
        def _(eng):
            sp.emit(eng)

        @block.scalar
        def _(eng):
            act.emit(eng)

        @block.gpsimd
        def _(eng):
            pool.emit(eng)

        @block.vector
        def _(eng):
            dve.emit(eng)

        @block.tensor
        def _(eng):
            pe.emit(eng)
    return st.plan, st.n


def arrange(inp, plan, n):
    w_in = np.asarray(inp["w_in"])[0]
    q = [w_in[:, 512 + 64 * i:576 + 64 * i] for i in HO1]
    gates = w_in[:, 2816:2852]
    gcol = [h * 3 + br for br in range(3) for h in HO1]
    at = np.asarray(inp["at_w_in_2"])[0]
    wo = np.asarray(inp["w_out"])[0]
    ao = np.asarray(inp["at_w_o_2"])[0]
    w2k = np.asarray(inp["cmp_k_w2"])[0]
    src = {
        ("w_in", 0): np.concatenate([w_in[:, 0:512]] + q + [w_in[:, 1280:]], axis=1),
        "w_vg": np.concatenate([w_in[:, 2048:2304], gates[:, gcol], w_in[:, 2560:2816]], axis=1),
        "cmp_k_w1": np.asarray(inp["cmp_k_w1"])[0].reshape(2048, 256),
        "cmp_v_w1": np.asarray(inp["cmp_v_w1"])[0].reshape(2048, 256),
        "cmp_k_w2d": np.concatenate([w2k, w2k], axis=1),
        "cmp_v_w2": np.asarray(inp["cmp_v_w2"])[0],
        "w_out_p": np.concatenate([wo[0:256]] + [wo[256 + 64 * i:320 + 64 * i] for i in HO1], axis=0),
        "at_qk": np.concatenate([at[:, 1024:1280], at[:, 1536:2048], at[:, 2048:2112], at[:, 2048:2112]]
                                + [at[:, 64 * i:64 * i + 64] for i in HO2], axis=1),
        "at_vw": np.concatenate([at[:, 1280:1536], at[:, 2112:2120]], axis=1),
        "at_w_o_p": np.concatenate([ao[64 * i:64 * i + 64] for i in HO2], axis=0),
    }
    W = np.zeros((n, P, CH), np.float32)
    for c, off, key, k0, kp, (c0, cw), w in plan:
        if key not in src:
            src[key] = np.asarray(inp[key[0]])[key[1:]]
        W[c, 0:kp, off:off + w] = src[key][k0:k0 + kp, c0:c0 + cw]
    return W


def kernel(**inputs):
    import concourse.bacc as _bacc
    from concourse.bass_utils import run_bass_kernel_spmd as _run

    nc = _bacc.Bacc("TRN2", target_bir_lowering=False, num_devices=1)
    carr, cat = consts()
    pat, npar = param_offsets()
    arrays = {}

    def declare(name, a):
        arrays[name] = np.ascontiguousarray(a)
        return nc.dram_tensor(name, arrays[name].shape, F32, kind="ExternalInput").ap()

    cd = declare("consts_dram", carr)
    pd = declare("params_dram", pack_params(inputs))
    x = np.asarray(inputs["x"])[0]
    xd = declare("x_dram", x.T.reshape(KT, P, T1).transpose(1, 0, 2))
    md = declare("meta_dram", np.asarray(inputs["meta_2"]).T.reshape(KT, P, NM).transpose(1, 0, 2))
    out = nc.dram_tensor("out_dram", (P, KT, T1), F32, kind="ExternalOutput").ap()

    def wdecl(n):
        return nc.dram_tensor("w_dram", (n, P, CH), F32, kind="ExternalInput").ap()

    plan, n = build(nc, out, wdecl, cd, pd, xd, md, carr.shape[1], cat, pat, npar)
    arrays["w_dram"] = arrange(inputs, plan, n)
    r = _run(nc, [arrays], core_ids=[0])
    got = r.results[0]["out_dram"]
    return np.ascontiguousarray(got.transpose(1, 0, 2).reshape(1, KT * P, T1).transpose(0, 2, 1))
```

```python
from contextlib import ExitStack

import numpy as np
import concourse.bass as bass
from concourse import mybir

F32 = mybir.dt.float32
F32R = mybir.dt.float32r
ALU = mybir.AluOpType
ACT = mybir.ActivationFunctionType
AX = mybir.AxisListType
P = 128

T1 = 256
T2 = 272
NM = 16
KT = 8
DFF = 2816
MT = DFF // P
CS = (96, 96, 80)
C0 = (0, 96, 192)
NC = 3
C = 96
CH = 1024
NRAW = 3
NSPL = 4
AHEAD = 2
NCH = 436
BIG = 3.0e38
KAPPA = float(np.exp(-0.5))

HO1 = [0, 3, 1, 4, 2, 5, 6, 9, 7, 10, 8, 11]
HO2 = [0, 4, 1, 5, 2, 6, 3, 7, 8, 12, 9, 13, 10, 14, 11, 15]


def slopes12():
    s8 = [2.0 ** (-(i + 1)) for i in range(8)]
    s16 = [2.0 ** (-0.5 * (i + 1)) for i in range(16)]
    return np.asarray(s8 + s16[0::2][:4], dtype=np.float32)


class Ins:

    def __init__(self, q, fn, amount=1, sem=None):
        self.q, self.fn, self.wanted, self.value = q, fn, sem is not None, None
        self.amount, self.sem = amount, sem


class Queue:

    def __init__(self, sem):
        self.sem, self.items = sem, []

    def wait(self, *producers):
        for p in producers:
            if p is not None:
                p.wanted = True
                self.items.append(p)

    def op(self, fn, *producers):
        self.wait(*producers)
        i = Ins(self, fn)
        self.items.append((i,))
        return i

    def dma(self, fn, sem, *producers):
        self.wait(*producers)
        i = Ins(self, fn, 16, sem)
        self.items.append((i,))
        return i

    def last(self):
        for it in reversed(self.items):
            if isinstance(it, tuple):
                return it[0]
        return None

    def number(self, counts):
        for it in self.items:
            if isinstance(it, tuple) and it[0].wanted:
                i = it[0]
                s = i.sem if i.sem is not None else self.sem
                i.sem = s
                counts[s] = counts.get(s, 0) + i.amount
                i.value = counts[s]

    def emit(self, eng):
        seen = {}
        for it in self.items:
            if isinstance(it, tuple):
                i = it[0]
                r = i.fn(eng)
                if i.wanted:
                    r.then_inc(i.sem, i.amount)
            elif seen.get(it.sem, 0) < it.value:
                eng.wait_ge(it.sem, it.value)
                seen[it.sem] = it.value


class Bank:
    def __init__(self, ap):
        self.ap, self.free = ap, []


def consts():
    groups = [([], {}), ([], {}), ([], {}), ([], {})]

    def put(g, name, a):
        parts, at = groups[g]
        a = np.asarray(a, np.float32)
        full = np.zeros((P, a.shape[1]), np.float32)
        full[:a.shape[0]] = a
        at[name] = sum(x.shape[1] for x in parts)
        parts.append(full)

    p = np.arange(P)
    put(0, "ident", np.eye(P))
    put(0, "ones", np.ones((P, P)))
    E = np.zeros((P, KT, 16))
    for k in range(KT):
        E[p, k, 2 * k + p // 64] = 1.0
    put(0, "E", E.reshape(P, -1))
    put(0, "ET", E.transpose(2, 1, 0).reshape(16, -1))
    tq = np.arange(T1).reshape(2, P).T[:, :, None]
    pos = np.arange(T1)[None, None, :]
    put(1, "D", np.where(pos <= tq, tq - pos, BIG).reshape(P, -1))
    sl = slopes12()
    n15 = np.arange(15)[None, None, None, :]
    t4 = tq[:, :, :, None]
    bc = -sl[HO1][None, None, :, None] * (t4 - (16.0 * n15 + 15.5))
    put(1, "Bc", np.where(16 * n15 + 31 <= t4, bc, -BIG).reshape(P, -1))
    s, t = np.arange(C)[:, None], np.arange(C)[None, :]
    put(2, "mst", np.concatenate([(s < t), (s <= t)], axis=1))
    put(2, "m1", ((s % 2 == 1) & (t == s - 1)))
    for lv in (1, 2, 4, 8, 16, 32, 64):
        put(2, f"l{lv}", (s // (2 * lv) == t // (2 * lv)) & (s // lv % 2 == 0) & (t // lv % 2 == 1))
    R = np.zeros((P, P))
    for b in (0, 64):
        for d in range(8):
            R[b + d, b + d + 8] = -1.0
            R[b + d + 8, b + d] = 1.0
    put(3, "RT", R.T)
    inv = (np.float32(500000.0) ** (-np.arange(0, 16, 2, dtype=np.float32) / np.float32(16))).astype(np.float32)
    ang = np.arange(T2, dtype=np.float32)[:, None] * inv[None, :]
    cf, sf = np.ones((P, T2)), np.zeros((P, T2))
    for b in (0, 64):
        for d in range(16):
            cf[b + d] = np.cos(ang[:, d % 8])
            sf[b + d] = np.sin(ang[:, d % 8])
    put(3, "cos", cf)
    put(3, "sin", sf)
    put(3, "cm", np.where(t <= s, 0.0, -BIG))
    return [np.concatenate(parts, axis=1) for parts, _ in groups], [at for _, at in groups]


def params():
    want = [
        ("attn_norm", (0,), "col"), ("ffn_norm", (0,), "col"), ("final_norm", (), "col"),
        ("conv_w", (0,), "rows"), ("conv_b", (0,), "col"), ("conv_ln_g", (0,), "col"), ("conv_ln_b", (0,), "col"),
        ("cmp_k_pe", (0,), "pe"), ("cmp_v_pe", (0,), "pe"),
    ]
    for i in range(2):
        for j in range(3):
            want.append(("norm_g_2", (i, j), "col"))
    for j in range(6):
        want.append(("rk_mix_2", (0, j), "col"))
    for nm in ("rk_w0_2", "rk_a0_2", "rk_k_k_2", "rk_k_a_2", "rk_lnx_g_2", "rk_lnx_b_2"):
        want.append((nm, (0,), "col"))
    want.append(("rk_r_k_2", (0,), "col"))
    want.append(("at_q_g_2", (0,), "dup"))
    want.append(("at_k_g_2", (0,), "dup"))
    return want


PW = {"conv_w": 62, "conv_b": 2, "conv_ln_g": 2, "conv_ln_b": 2, "cmp_k_pe": 16, "cmp_v_pe": 16,
      "at_q_g_2": 1, "at_k_g_2": 1}


def param_offsets():
    at, n = {}, 0
    for name, idx, kind in params():
        at[(name,) + idx] = n
        n += PW.get(name, 8)
    return at, n


def pack_params(inp):
    out = []
    for name, idx, kind in params():
        a = np.asarray(inp[name])[idx]
        if kind == "col":
            a = a.reshape(-1, P).T
        elif kind == "rows":
            a = a.reshape(31, 2, P).transpose(2, 1, 0).reshape(P, 62)
        elif kind == "pe":
            a = a.reshape(16, P).T
        else:
            a = np.concatenate([a, a]).reshape(P, 1)
        out.append(a)
    return np.ascontiguousarray(np.concatenate(out, axis=1))


class Stream:

    def __init__(self, raw, hi, lo, sync, pe, act, dve, sems):
        self.raw, self.hi, self.lo = raw, hi, lo
        self.sync, self.pe, self.act, self.dve, self.sems = sync, pe, act, dve, sems
        self.plan, self.n, self.pos = [], 0, CH
        self.split, self.last_use, self.landed = [], [], []
        self.dram = None

    def fetch(self, c):
        s = c % NRAW
        before = [self.split[c - NRAW][1], self.split[c - NRAW][0]] if c >= NRAW else []
        self.landed.append(self.sync.dma(
            lambda e: e.dma_start(self.raw[:, s * CH:(s + 1) * CH], self.dram[c]), self.sems[s], *before))

    def part(self, c):
        s, d = c % NRAW, c % NSPL
        raw = self.raw[:, s * CH:(s + 1) * CH]
        hi, lo = self.hi[:, d * CH:(d + 1) * CH], self.lo[:, d * CH:(d + 1) * CH]
        used = self.last_use[c - NSPL] if c >= NSPL else None
        a = self.act.op(lambda e: e.activation(hi, raw, ACT.Copy), self.landed[c], used)
        b = self.dve.op(lambda e: e.tensor_tensor(lo, raw, hi.bitcast(F32), ALU.subtract), a, used)
        self.split.append((a, b))
        if c + NRAW < NCH:
            self.fetch(c + NRAW)

    def tile(self, key, k0, kp, cols, w):
        if self.pos + w > CH:
            if self.n:
                self.last_use.append(self.pe.last())
            else:
                for c in range(NRAW):
                    self.fetch(c)
            self.n += 1
            self.pos = 0
            while len(self.split) < min(self.n + AHEAD, NCH):
                self.part(len(self.split))
        off = self.pos
        self.pos += w
        c = self.n - 1
        self.plan.append((c, off, key, k0, kp, cols, w))
        o = c % NSPL * CH + off
        return self.hi[0:kp, o:o + w], self.lo[0:kp, o:o + w], self.split[c]


def build(nc, out, wdecl, cdram, pdram, xdram, mdram, CW, CAT, PAT, NPAR):
    with ExitStack() as ctx:
        def alloc(scope, name, n, dt=F32):
            return scope.enter_context(nc.sbuf_tensor(name, [P, n], dt))

        def sem(name):
            return ctx.enter_context(nc.semaphore(name))

        h = alloc(ctx, "h", KT * T2)[:, :].rearrange("p (k t) -> p k t", k=KT)
        cs0 = alloc(ctx, "cs0", CW[0])
        pr = alloc(ctx, "pr", NPAR)
        rs_ = alloc(ctx, "rs", 2 * T2)
        sq_ = alloc(ctx, "sq", 3 * T2)
        small = alloc(ctx, "small", 16)
        raw = alloc(ctx, "w_raw", NRAW * CH)
        whi = alloc(ctx, "w_hi", NSPL * CH, F32R)
        wlo = alloc(ctx, "w_lo", NSPL * CH, F32R)
        psum = [ctx.enter_context(nc.psum_tensor(f"ps{i}", [P, 512], F32)) for i in range(8)]

        pe, dve, act, pool, sp = (Queue(sem(n)) for n in ("s_pe", "s_dve", "s_act", "s_pool", "s_sp"))
        st = Stream(raw, whi, wlo, sp, pe, act, dve, [sem(f"s_raw{i}") for i in range(NRAW)])
        s_in = [sem(f"s_in{i}") for i in range(7)]
        s_x = [sem(f"s_cx{i}") for i in range(8)]
        s_out = sem("s_out")
        hx = h[:, :, NM:T2]
        csg = {0: cs0}

        def v3(ap, a):
            return ap.rearrange("p (a b) -> p a b", a=a)

        def v4(ap, a, b):
            return ap.rearrange("p (a b c) -> p a b c", a=a, b=b)

        def con(g, name, n, rows=P):
            return csg[g][0:rows, CAT[g][name]:CAT[g][name] + n]

        def par(*key, i=0, rows=P, n=1):
            o = PAT[key] + i
            return pr[0:rows, o:o + n]

        ident = con(0, "ident", P)
        ones = con(0, "ones", P)
        EH = v3(con(0, "E", 128), KT)
        ETH = v3(con(0, "ET", 1024, 16), KT)
        free = [Bank(p) for p in psum]

        def take():
            return free.pop(0)

        def give(b, *readers):
            b.free = list(readers)
            free.append(b)

        def mm(o, lhsT, rhs, start, stop, *w):
            return pe.op(lambda e: e.matmul(o, lhsT, rhs, start=start, stop=stop), *w)

        def tr(o, a, n, *w):
            return pe.op(lambda e: e.transpose(o, a, ident[0:n, 0:n]), *w)

        def tt(q, o, a, b, op, *w):
            return q.op(lambda e: e.tensor_tensor(o, a, b, op), *w)

        def stt(o, a, s, b, op0, op1, *w):
            return dve.op(lambda e: e.scalar_tensor_tensor(out=o, in0=a, scalar=s, in1=b, op0=op0, op1=op1), *w)

        def ts(q, o, a, s1, s2, op0, op1, *w):
            if op1 is None:
                return q.op(lambda e: e.tensor_scalar(o, a, s1, None, op0), *w)
            return q.op(lambda e: e.tensor_scalar(o, a, s1, s2, op0, op1), *w)

        def cp(q, o, a, *w):
            if q is act:
                return q.op(lambda e: e.activation(o, a, ACT.Copy), *w)
            return q.op(lambda e: e.tensor_copy(o, a), *w)

        def af(o, a, f, *w, bias=0.0, scale=1.0, acc=None):
            if acc is None:
                return act.op(lambda e: e.activation(o, a, f, bias=bias, scale=scale), *w)
            return act.op(lambda e: e.activation(o, a, f, bias=bias, scale=scale, accum_out=acc), *w)

        def rec(o, a, *w):
            return dve.op(lambda e: e.reciprocal(o, a), *w)

        def red(o, a, op, *w, negate=False):
            return dve.op(lambda e: e.tensor_reduce(o, a, AX.X, op, negate=negate), *w)

        def rsqrt(dst, src, scale, eps, *w):
            a = ts(dve, dst, src, scale, eps, ALU.mult, ALU.add, *w)
            b = af(dst, dst, ACT.Sqrt, a)
            return rec(dst, dst, b), a

        class Pair:

            def __init__(self, scope, name, n):
                self.hi = alloc(scope, name + "_hi", n, F32R)
                self.lo = alloc(scope, name + "_lo", n, F32R)
                self.ready = {}

            def at(self, off, n, rows=P):
                return self.hi[0:rows, off:off + n], self.lo[0:rows, off:off + n]

            def put(self, k, off, src, *w, rows=P, after=()):
                shape = src.shape[-1]
                hi, lo = self.at(off, shape, rows)
                a = af(hi, src, ACT.Copy, *w, *after)
                b = tt(dve, lo, src, hi.bitcast(F32), ALU.subtract, a)
                self.ready[k] = (a, b)
                return b

            def put_scaled(self, k, off, src, col, *w, after=()):
                hi, lo = self.at(off, src.shape[-1])
                a = af(hi, src, ACT.Copy, *w, *after, scale=col)
                b = stt(lo, src, col, hi.bitcast(F32), ALU.mult, ALU.subtract, a)
                self.ready[k] = (a, b)
                return b

        def mm3(o, lhs, rhs, start, stop, *w):
            mm(o, lhs[0], rhs[0], start, False, *w)
            mm(o, lhs[0], rhs[1], False, False)
            return mm(o, lhs[1], rhs[0], False, stop)

        i_c0 = act.dma(lambda e: e.dma_start(cs0[:, :], cdram[0]), s_in[0])
        i_p = act.dma(lambda e: e.dma_start(pr[:, :], pdram), s_in[1])
        i_x = sp.dma(lambda e: e.dma_start(hx, xdram), s_in[2])
        i_m = act.dma(lambda e: e.dma_start(h[:, :, 0:NM], mdram), s_in[3])

        n_stat = [0]
        rs_use = [[], []]
        sq_use = [[], [], []]

        def stats(src, T, ready, q):
            j = n_stat[0] % 2
            n_stat[0] += 1
            acc = sq_[:, 0:T]
            i = af(acc, src[:, 0, :], ACT.Square, ready[0], *sq_use[0])
            for k in range(1, KT):
                s = 1 + k % 2
                t_ = sq_[:, s * T2:s * T2 + T]
                a = af(t_, src[:, k, :], ACT.Square, ready[k], *sq_use[s])
                i = tt(q, acc, acc, t_, ALU.add, a, i)
                sq_use[s] = [i]
            b = take()
            m = mm(b.ap[:, 0:T], ones, acc, True, True, i, i_c0, *b.free)
            sq_use[0] = [m]
            rs = rs_[:, j * T2:j * T2 + T]
            r, rd = rsqrt(rs, b.ap[:, 0:T], 1.0 / 1024, 1e-6, m, *rs_use[j])
            give(b, rd)
            return rs, r

        def scaled(X, src, T, key, ready, after):
            for k in range(KT):
                X.put_scaled(k, k * T2, src[:, k, :], par(*key, i=k), ready[k], i_p, after=after if k == 0 else ())

        def dense(X, T, kt, key, n0, nw, kp=P, xo=0, xk=0):
            b = take()
            for k in range(kt):
                wh, wl, ld = st.tile(key, k * P, kp, (n0, nw), nw)
                m = mm3(b.ap[0:nw, 0:T], (wh, wl), X.at(xo + k * T2, T, kp), k == 0, k == kt - 1, *ld,
                        *X.ready[xk + k], *(b.free if k == 0 else ()))
            return b, m

        def ffn(X, hv, T, nkey, w1, w2, scale, ready, x_free):
            rs, r_rs = stats(hv, T, ready, pool)
            scaled(X, hv, T, nkey, ready, x_free)
            with ExitStack() as sc:
                n_ = f"f{n_stat[0]}"
                PR = Pair(sc, n_ + "_prod", MT * T2)
                tmp = v3(alloc(sc, n_ + "_tmp", 9 * T2)[:, :], 9)
                late = []
                p_use = [None] * 3
                for m in range(MT):
                    o = m % 3 * 3
                    t1, t2, t3 = (tmp[:, o + z, 0:T] for z in range(3))
                    bg, g = dense(X, T, KT, w1, m * P, P)
                    i1 = tt(dve, t1, bg.ap[:, 0:T], rs, ALU.mult, g, r_rs, p_use[m % 3])
                    give(bg, i1)
                    s = af(t2, t1, ACT.Silu, i1)
                    bu, u = dense(X, T, KT, w1, DFF + m * P, P)
                    i2 = tt(dve, t1, bu.ap[:, 0:T], rs, ALU.mult, u, s)
                    give(bu, i2)
                    i3 = tt(pool, t3, t1, t2, ALU.mult, i2, s)
                    if late:
                        late.pop()()

                    def low(m=m, t3=t3, i3=i3):
                        p_use[m % 3] = PR.put(m, m * T2, t3, i3)
                    late.append(low)
                    x_last = u
                late.pop()()
                rs_use[(n_stat[0] - 1) % 2] = [i2]
                res = []
                for n in range(KT):
                    b, i = dense(PR, T, MT, w2, n * P, P)
                    r = stt(hv[:, n, :], b.ap[:, 0:T], scale, hv[:, n, :], ALU.mult, ALU.add, i)
                    give(b, r)
                    res.append(r)
            return res, [x_last]

        def barrier():
            ends = [q.last() for q in (pe, dve, act, pool)]
            for q in (pe, dve, act, pool):
                q.wait(*[e for e in ends if e is not None and e.q is not q])

        T = T1
        scX = ctx.enter_context(ExitStack())
        X = Pair(scX, "x1", KT * T2)
        sc = ctx.enter_context(ExitStack())
        csg[1] = alloc(sc, "cs1", CW[1])
        i_c1 = act.dma(lambda e: e.dma_start(csg[1][:, :], cdram[1]), s_in[4])
        rs, r_rs = stats(hx, T, [i_x] * KT, dve)
        scaled(X, hx, T, ("attn_norm", 0), [i_x] * KT, ())
        mix = v3(alloc(sc, "mix", KT * T)[:, :], KT)
        qT = v3(alloc(sc, "qT", 6 * T)[:, :], 6)
        ksT, kwT, kcT, vcT = (v3(alloc(sc, n, 512)[:, :], 2) for n in ("ksT", "kwT", "kcT", "vcT"))
        V = v4(alloc(sc, "V", 1024)[:, :], 2, 2)
        G = v3(alloc(sc, "G", 72)[:, :], 2)
        yp = v3(alloc(sc, "yp", 572)[:, :], 2)
        Xc = [v3(alloc(sc, f"Xc{j}", 1024)[:, :], 4) for j in range(2)]
        XW = alloc(sc, "XW", 960)
        XP = [Pair(sc, f"xw{j}", 960) for j in range(2)]
        hcP = [Pair(sc, f"hc{j}", 120) for j in range(2)]
        hcs = alloc(sc, "hcs", 512)
        kcc = alloc(sc, "kcc", 60)[:, :]
        vcc = v3(alloc(sc, "vcc", 256)[0:15, :], 4)
        rsT = alloc(sc, "rsT", 2)
        acc = v3(alloc(sc, "cacc", 512)[:, :], 2)
        sqc = v3(alloc(sc, "csq", 512)[:, :], 2)
        sg = v3(alloc(sc, "csg", 512)[:, :], 2)
        mu = alloc(sc, "cmu", 256)[:, :]
        rsc = alloc(sc, "crs", 256)[:, :]
        sC = alloc(sc, "sC", 480)
        PcT = v4(alloc(sc, "PcT", 3072)[0:15, :], 2, 12)
        sR = alloc(sc, "sR", 3 * 520)
        ptR = alloc(sc, "ptR", 3 * 512)
        zy = pool.op(lambda e: e.memset(yp[:, :, 0:30], 0.0))

        def proj(dst, n0, nt, scale=1.0):
            res = []
            for i in range(nt):
                b, m = dense(X, T, KT, ("w_in", 0), n0 + i * P, P)
                r = stt(dst[:, i, :], b.ap[:, 0:T], scale, rs, ALU.mult, ALU.mult, m, r_rs)
                give(b, r)
                res.append(r)
            return res

        i_y = []
        for i in range(2):
            bv, v = dense(X, T, KT, ("w_in", 0), 256 + i * P, P)
            s = tt(dve, sg[:, i, :], bv.ap[:, 0:T], rs, ALU.mult, v, r_rs)
            give(bv, s)
            s = af(sg[:, i, :], sg[:, i, :], ACT.Sigmoid, s)
            bu, u = dense(X, T, KT, ("w_in", 0), i * P, P)
            a = tt(dve, yp[:, i, 30:286], bu.ap[:, 0:T], rs, ALU.mult, u)
            give(bu, a)
            i_y.append(tt(dve, yp[:, i, 30:286], yp[:, i, 30:286], sg[:, i, :], ALU.mult, s, a))
        cv = [None, None]
        taps = [(j, i) for j in range(31) for i in range(2)]

        def conv(n):
            for _ in range(n):
                if not taps:
                    return
                j, i = taps.pop(0)
                w = par("conv_w", 0, i=i * 31 + j)
                if j == 0:
                    cv[i] = ts(dve, acc[:, i, :], yp[:, i, 0:256], w, par("conv_b", 0, i=i), ALU.mult, ALU.add, zy, *i_y)
                else:
                    cv[i] = stt(acc[:, i, :], yp[:, i, j:j + 256], w, acc[:, i, :], ALU.mult, ALU.add, cv[i])

        r_c = []
        for j, dst in enumerate((kcT, vcT)):
            r_c.append(proj(dst, 1280 + 256 * j, 2))
            conv(6)
        r_x = []
        for j, src in enumerate((kcT, vcT)):
            ds = []
            for gp in range(2):
                for pr_ in range(2):
                    n = T - pr_
                    ds.append(act.dma(
                        lambda e, j=j, gp=gp, pr_=pr_, n=n, src=src: e.dma_start(
                            Xc[j].rearrange("p (a b) t -> p a b t", b=2)[64 * pr_:64 * pr_ + 64, :, gp, 0:n],
                            src[64 * gp:64 * gp + 64, :, pr_:pr_ + n]),
                        s_x[4 * j + 2 * gp + pr_], *r_c[j]))
            r_x.append(ds)
        b = take()
        for t in range(2):
            m = tr(b.ap[:, t * P:t * P + P], rs[:, t * P:t * P + P], P, r_rs, *b.free)
        i_rsT = cp(dve, rsT[:, 0:2], b.ap[:, 0:256:P], m)
        give(b, i_rsT)
        r_q = []
        for z in range(6):
            r_q += proj(qT[:, z:z + 1, :], 512 + z * P, 1, scale=0.125)
            conv(5)
            if z in (1, 2):
                j = z - 1
                pecol = par(("cmp_k_pe", "cmp_v_pe")[j], 0, n=16)
                XW4 = XW[:, :].rearrange("p (l g n) -> p l g n", l=16, g=4)
                ws = []
                for g in range(4):
                    for hf in range(2):
                        src = Xc[j][:, g, 16 * hf:16 * hf + 240].rearrange("p (n l) -> p l n", l=16)[:, 0:16:2, :]
                        ws.append(tt(pool, XW4[:, 8 * hf:8 * hf + 8, g, :], src,
                                     pecol[:, 8 * hf:8 * hf + 8].unsqueeze(2).to_broadcast([P, 8, 15]), ALU.add,
                                     *r_x[j], i_p, *(XP[0].ready[0] if j else ())))
                XP[j].put(0, 0, XW[:, :], *ws)
        r_ks = proj(ksT, 1792, 2)
        conv(7)
        r_kw = proj(kwT, 2304, 2)
        conv(7)
        bs = [[take(), take()] for _ in range(2)]
        for k in range(KT):
            wh, wl, ld = st.tile("w_vg", k * P, P, (0, 548), 548)
            xh, xl = X.at(k * T2, T)
            for t in range(2):
                x_ = (xh[:, t * P:t * P + P], xl[:, t * P:t * P + P])
                mm3(bs[t][0].ap[:, 0:292], x_, (wh[:, 0:292], wl[:, 0:292]), k == 0, k == KT - 1, *ld,
                    *((bs[t][0].free + bs[t][1].free) if k == 0 else ()))
                vl = mm3(bs[t][1].ap[:, 0:256], x_, (wh[:, 292:548], wl[:, 292:548]), k == 0, k == KT - 1)
        r_v, r_g = [], []
        for t in range(2):
            col = rsT[:, t:t + 1]
            a = af(V[:, t, 0, :], bs[t][0].ap[:, 0:256], ACT.Copy, vl, i_rsT, scale=col)
            g_ = af(G[:, t, :], bs[t][0].ap[:, 256:292], ACT.Sigmoid, scale=col)
            c_ = af(V[:, t, 1, :], bs[t][1].ap[:, 0:256], ACT.Copy, scale=col)
            give(bs[t][0], g_)
            give(bs[t][1], c_)
            r_v.append(c_)
            r_g.append(g_)
        x_last = vl
        conv(99)
        for j in range(2):
            nm = ("cmp_k", "cmp_v")[j]
            b = take()
            for l2 in range(16):
                wh, wl, ld = st.tile(nm + "_w1", l2 * P, P, (0, 256), 256)
                m = mm3(b.ap[0:60, 0:256], XP[j].at(l2 * 60, 60), (wh, wl), l2 == 0, l2 == 15, *ld,
                        *XP[j].ready[0], *(b.free if l2 == 0 else ()))
            hs_ = hcs[0:60, 256 * j:256 * j + 256]
            i = af(hs_, b.ap[0:60, 0:256], ACT.Silu, m)
            give(b, i)
            b = take()
            for ht in range(2):
                m = tr(b.ap[:, ht * 60:ht * 60 + 60], hs_[:, ht * P:ht * P + P], 60, i, *b.free)
            a = af(hcP[j].hi[:, :], b.ap[:, 0:120], ACT.Copy, m)
            c_ = tt(dve, hcP[j].lo[:, :], b.ap[:, 0:120], hcP[j].hi[:, :].bitcast(F32), ALU.subtract, a)
            give(b, c_)
            b = take()
            if j == 0:
                for ht in range(2):
                    wh, wl, ld = st.tile(nm + "_w2d", ht * P, P, (0, P), P)
                    m = mm3(b.ap[:, 0:60], (wh, wl), hcP[j].at(ht * 60, 60), ht == 0, ht == 1, *ld, a, c_, *b.free)
                r_kc = cp(dve, kcc, b.ap[:, 0:60], m)
                give(b, r_kc)
            else:
                wt = [st.tile(nm + "_w2", ht * P, P, (0, 64), 64) for ht in range(2)]
                for g in range(4):
                    for ht in range(2):
                        m = mm3(b.ap[0:15, g * 64:g * 64 + 64], hcP[j].at(ht * 60 + g * 15, 15), wt[ht][0:2],
                                ht == 0, ht == 1, *wt[ht][2], a, c_, *b.free)
                r_vc = cp(dve, vcc, v3(b.ap[0:15, 0:256], 4), m)
                give(b, r_vc)
        comp = {}

        def comp_a(t):
            bb = [take(), take()]
            for p in range(12):
                hf, g = p % 2, HO1[p] // 3
                m = mm(bb[hf].ap[:, p // 2 * 15:p // 2 * 15 + 15], qT[64 * hf:64 * hf + 64, p // 2, t * P:t * P + P],
                       kcc[64 * hf:64 * hf + 64, g * 15:g * 15 + 15], True, True, r_q[p // 2], r_kc,
                       *bb[hf].free)
            s4 = sC[:, t * 240:t * 240 + 180].rearrange("p (a f n) -> p a f n", a=6, f=2)
            B4 = con(1, "Bc", 360)[:, t * 180:t * 180 + 180].rearrange("p (a f n) -> p a f n", a=6, f=2)
            r = []
            for hf in range(2):
                r.append(tt(dve, s4[:, :, hf, :], v3(bb[hf].ap[:, 0:90], 6), B4[:, :, hf, :], ALU.add, m, i_c1))
                give(bb[hf], r[-1])
            s3 = v3(sC[:, t * 240:t * 240 + 180], 12)
            mx = sC[:, t * 240 + 180:t * 240 + 192]
            i = red(mx, s3, ALU.max, *r)
            i = ts(dve, mx, mx, -1e35, None, ALU.max, None, i)
            i = tt(dve, s3, s3, mx.unsqueeze(2).to_broadcast([P, 12, 15]), ALU.subtract, i)
            comp[t] = af(s3, s3, ACT.Exp, i)

        def comp_b(t):
            s3 = v3(sC[:, t * 240:t * 240 + 180], 12)
            cf = sC[:, t * 240 + 200:t * 240 + 212]
            i = red(cf, s3, ALU.add, comp[t])
            i = ts(dve, cf, cf, 1e-30, None, ALU.max, None, i)
            i = rec(cf, cf, i)
            i = tt(dve, cf, cf, G[:, t, 0:12], ALU.mult, i, r_g[t])
            comp[t] = tt(dve, s3, s3, cf.unsqueeze(2).to_broadcast([P, 12, 15]), ALU.mult, i)

        r_pc = {}

        def comp_c(t):
            s3 = v3(sC[:, t * 240:t * 240 + 180], 12)
            for q3 in range(3):
                b = take()
                for p in range(4):
                    m = tr(b.ap[0:15, p * P:p * P + P], s3[:, q3 * 4 + p, :], P, comp[t], *b.free)
                c_ = cp(act, PcT[:, t, q3 * 4:q3 * 4 + 4, :], v3(b.ap[0:15, :], 4), m)
                give(b, c_)
            r_pc[t] = c_

        sl = slopes12()
        units = [(t, p) for t in range(2) for p in range(12)]
        obank = {}
        s_use, pt_use = [None] * 3, [None] * 3
        stt_ = {}
        r_mix = {}

        def att_s(n):
            t, p = units[n]
            hf, g, kw = p % 2, HO1[p] // 3, P * (t + 1)
            b = take()
            q_ = qT[64 * hf:64 * hf + 64, p // 2, t * P:t * P + P]
            for br, kk_ in enumerate((ksT, kwT)):
                m = mm(b.ap[:, br * kw:br * kw + kw], q_, kk_[64 * hf:64 * hf + 64, g // 2, 0:kw], True, True,
                       r_q[p // 2], r_ks[g // 2], r_kw[g // 2], *b.free)
            o = n % 3 * 520
            s = v3(sR[:, o:o + 2 * kw], 2)
            D_ = con(1, "D", 512)[:, t * 256:t * 256 + kw].unsqueeze(1).to_broadcast([P, 2, kw])
            a = stt(s, D_, -float(sl[HO1[p]]), v3(b.ap[:, 0:2 * kw], 2), ALU.mult, ALU.add, m, i_c1, s_use[n % 3])
            give(b, a)
            mx, sm = sR[:, o + 512:o + 514], sR[:, o + 514:o + 516]
            i = red(mx, s, ALU.max, a, negate=True)
            for br in range(2):
                e_ = af(s[:, br, :], s[:, br, :], ACT.Exp, i, bias=mx[:, br:br + 1], acc=sm[:, br:br + 1])
            stt_[n] = (s, sm, e_)

        def att_p(n):
            t, p = units[n]
            s, sm, e_ = stt_[n]
            kw = P * (t + 1)
            i = ts(dve, sm, sm, 1e-30, None, ALU.max, None, e_)
            i = rec(sm, sm, i)
            i = tt(dve, sm, sm, G[:, t, 12 + p:36:12], ALU.mult, i, r_g[t])
            i = tt(dve, s, s, sm.unsqueeze(2).to_broadcast([P, 2, kw]), ALU.mult, i)
            stt_[n] = (s, i)

        def att_t(n):
            t, p = units[n]
            s, i = stt_[n]
            b = take()
            for br in range(2):
                for kc in range(t + 1):
                    m = tr(b.ap[:, (br * (t + 1) + kc) * P:][:, 0:P], s[:, br, kc * P:kc * P + P], P, i, *b.free)
            s_use[n % 3] = m
            n_ = 2 * (t + 1) * P
            pt = ptR[:, n % 3 * 512:n % 3 * 512 + n_]
            c_ = cp(act, pt, b.ap[:, 0:n_], m, pt_use[n % 3])
            give(b, c_)
            stt_[n] = (pt, c_)

        def att_v(n):
            t, p = units[n]
            hf, g = p % 2, HO1[p] // 3
            pt, c_ = stt_[n]
            if hf == 0:
                obank[n // 2] = take()
            b = obank[n // 2]
            o = b.ap[64 * hf:64 * hf + 64, 0:P]
            mm(o, vcc[:, g, :], PcT[:, t, p, :], True, False, r_vc, r_pc[t], c_, r_v[0], r_v[1], *b.free)
            for br in range(2):
                for kc in range(t + 1):
                    m = mm(o, V[:, kc, br, g * 64:g * 64 + 64], pt[:, (br * (t + 1) + kc) * P:][:, 0:P], False,
                           br == 1 and kc == t)
            pt_use[n % 3] = m
            if hf == 1:
                r = cp(act, mix[:, 2 + p // 2, t * P:t * P + P], b.ap[:, 0:P], m)
                give(b, r)
                r_mix[(p // 2, t)] = r
                if t == 1:
                    X.put(2 + p // 2, (2 + p // 2) * T2, mix[:, 2 + p // 2, :], r, x_last)

        b = take()
        for i in range(2):
            m = mm(b.ap[:, 0:T], ones, acc[:, i, :], i == 0, i == 1, cv[i], *b.free)
        i_mu = af(mu, b.ap[:, 0:T], ACT.Copy, m, scale=1.0 / 256)
        give(b, i_mu)
        comp_a(0)
        att_s(0)
        comp_a(1)
        att_s(1)
        b = take()
        for i in range(2):
            a = tt(dve, acc[:, i, :], acc[:, i, :], mu, ALU.subtract, i_mu)
            a = af(sqc[:, i, :], acc[:, i, :], ACT.Square, a)
            m = mm(b.ap[:, 0:T], ones, sqc[:, i, :], i == 0, i == 1, a, *b.free)
        r, rd = rsqrt(rsc, b.ap[:, 0:T], 1.0 / 256, 1e-6, m)
        give(b, rd)
        for i in range(2):
            a = stt(acc[:, i, :], acc[:, i, :], par("conv_ln_g", 0, i=i), rsc, ALU.mult, ALU.mult, r)
            a = af(mix[:, i, :], acc[:, i, :], ACT.Silu, a, bias=par("conv_ln_b", 0, i=i))
            X.put(i, i * T2, mix[:, i, :], a, x_last)
        for n in range(len(units) + 3):
            if 2 <= n < len(units):
                att_s(n)
            if n == 0:
                comp_b(0)
            if n == 1:
                comp_c(0)
                comp_b(1)
            if n == 3:
                comp_c(1)
            if 0 <= n - 1 < len(units):
                att_p(n - 1)
            if 0 <= n - 2 < len(units):
                att_t(n - 2)
            if 0 <= n - 3 < len(units):
                att_v(n - 3)
        rh = []
        for n in range(KT):
            b, m = dense(X, T, KT, "w_out_p", n * P, P)
            r = tt(dve, hx[:, n, :], b.ap[:, 0:T], hx[:, n, :], ALU.add, m)
            give(b, r)
            rh.append(r)
        sc.close()
        rh, xf = ffn(X, hx, T, ("ffn_norm", 0), ("w_gate_up", 0), ("w_down", 0), 1.0, rh, [m])
        rs, r_rs = stats(hx, T, rh, pool)
        rh = [stt(hx[:, k, :], hx[:, k, :], par("final_norm", i=k), rs, ALU.mult, ALU.mult, r_rs, i_m) for k in range(KT)]
        rs_use[(n_stat[0] - 1) % 2] = [rh[-1]]

        T = T2
        rh, xf = ffn(X, h, T, ("norm_g_2", 0, 0), ("ffn_w_in_2", 0, 0), ("ffn_w_out_2", 0, 0), 0.5, rh, xf)
        rs, r_rs = stats(h, T, rh, pool)
        scX.close()
        sB = ctx.enter_context(ExitStack())
        barrier()
        csg[2] = alloc(sB, "cs2", CW[2])
        i_c2 = act.dma(lambda e: e.dma_start(csg[2][:, :], cdram[2]), s_in[5])
        hn_ = alloc(sB, "hn", KT * (T2 + 1))
        hn = v3(hn_[:, :], KT)
        kT, aT, kkT, rT, vT = (v3(alloc(sB, n, KT * T2)[:, :], KT) for n in ("kT", "aT", "kkT", "rT", "vT"))
        Lc = alloc(sB, "Lc", KT * (T2 + NC))[:, :].rearrange("p (k t) -> p k t", k=KT)
        ms = alloc(sB, "rkms", 3 * T2 + 560)
        s16, s16b = ms[0:16, 0:T2], ms[0:16, T2:2 * T2]
        ka1 = ms[:, 3 * T2 + 544:3 * T2 + 552]
        gl = ms[:, 2 * T2:4 * T2]
        LO = [c0 + i for i, c0 in enumerate(C0)]

        def Lcol(k, c, off, n):
            return Lc[:, k, LO[c] + off:LO[c] + off + n]

        xn = hn[:, :, 1:1 + T]
        z0 = pool.op(lambda e: e.memset(hn[:, :, 0:1], 0.0))
        rn = [stt(xn[:, k, :], h[:, k, :], par("norm_g_2", 0, 1, i=k), rs, ALU.mult, ALU.mult, r_rs, rh[k])
              for k in range(KT)]
        rs_use[(n_stat[0] - 1) % 2] = [rn[-1]]
        sP = ctx.enter_context(ExitStack())
        xx = v3(alloc(sP, "xx", KT * T2)[:, :], KT)
        sw = v3(alloc(sP, "sw", KT * T2)[:, :], KT)
        xr = v3(alloc(sP, "xraw", 3 * T2)[:, :], 3)
        XS = [Pair(sP, f"xs{i}", KT * T2) for i in range(2)]
        LP = Pair(sP, "lora", 2 * T2)
        lo_ = alloc(sP, "loraf", 2 * T2)
        i_xx = [tt(pool, xx[:, k, :], hn[:, k, 0:T], xn[:, k, :], ALU.subtract, z0, rn[k]) for k in range(KT)]
        x_use = [[], []]
        n_x = [0]
        xr_use = [None] * 3

        def mixed(j):
            n = n_x[0] % 2
            n_x[0] += 1
            for k in range(KT):
                s = (n_x[0] * KT + k) % 3
                i = stt(xr[:, s, :], xx[:, k, :], par("rk_mix_2", 0, j, i=k), xn[:, k, :], ALU.mult, ALU.add,
                        i_xx[k], xr_use[s])
                xr_use[s] = XS[n].put(k, k * T2, xr[:, s, :], i, after=x_use[n])
            return n

        def full(dst, key, n, evac):
            out_ = []
            for i in range(KT):
                b, m = dense(XS[n], T, KT, key, i * P, P)
                r = evac(i, b, m)
                give(b, r)
                out_.append(r)
            x_use[n] = [m]
            return out_

        def plain(dst):
            return lambda i, b, m: cp(act, dst[:, i, :], b.ap[:, 0:T], m)

        zL = [pool.op(lambda e, c=c: e.memset(Lc[:, :, LO[c]:LO[c] + 1], 0.0)) for c in range(NC)]
        n1 = mixed(1)
        n2 = mixed(4)
        b, m = dense(XS[n1], T, KT, ("rk_w1_2", 0), 0, 64)
        x_use[n1] = [m]
        i = af(lo_[0:64, 0:T], b.ap[0:64, 0:T], ACT.Tanh, m)
        give(b, i)
        LP.put(0, 0, lo_[0:64, 0:T], i, rows=64)
        b, m = dense(XS[n2], T, KT, ("rk_a1_2", 0), 0, 64)
        x_use[n2] = [m]
        i = cp(act, lo_[0:64, T:2 * T], b.ap[0:64, 0:T], m)
        give(b, i)
        LP.put(1, T2, lo_[0:64, T:2 * T], i, rows=64)
        n1 = mixed(2)
        i_s = []
        for k in range(KT):
            b, m = dense(LP, T, 1, ("rk_w2_2", 0), k * P, P, kp=64)
            s = af(sw[:, k, :], b.ap[:, 0:T], ACT.Sigmoid, m, bias=par("rk_w0_2", 0, i=k))
            give(b, s)
            i_s.append(s)
        i_a = []
        for k in range(KT):
            b, m = dense(LP, T, 1, ("rk_a2_2", 0), k * P, P, kp=64, xo=T2, xk=1)
            s = af(aT[:, k, :], b.ap[:, 0:T], ACT.Sigmoid, m, bias=par("rk_a0_2", 0, i=k))
            give(b, s)
            i_a.append(s)
        r_k = full(kT, ("rk_w_k_2", 0), n1, plain(kT))
        n2 = mixed(0)
        r_L = []
        for k in range(KT):
            for c in range(NC):
                n = CS[c]
                l = dve.op(lambda e, k=k, c=c, n=n: e.tensor_tensor_scan(
                    Lcol(k, c, 1, n), ones[:, 0:n], sw[:, k, C0[c]:C0[c] + n], 0.0, ALU.mult, ALU.add), i_s[k], *zL)
            r_L.append(l)
        r_r = full(rT, ("rk_w_r_2", 0), n2, plain(rT))
        e_i, e_c = [], []
        for k in range(KT):
            for c in range(NC):
                a = af(sw[:, k, C0[c]:C0[c] + CS[c]], Lcol(k, c, 1, CS[c]), ACT.Exp, r_L[k], scale=KAPPA)
            e_i.append(a)
            e_c.append(af(Lc[:, k, :], Lc[:, k, :], ACT.Exp, a, scale=-KAPPA))
        n1 = mixed(3)
        r_v = full(vT, ("rk_w_v_2", 0), n1, plain(vT))
        n2 = mixed(5)
        b, m0 = dense(XS[n2], T, KT, ("rk_g1_2", 0), 0, P)
        b2, m = dense(XS[n2], T, KT, ("rk_g1_2", 0), P, 32)
        g0 = af(gl[:, 0:T], b.ap[:, 0:T], ACT.Sigmoid, m0)
        g1 = af(gl[0:32, T:2 * T], b2.ap[0:32, 0:T], ACT.Sigmoid, m)
        give(b, g0)
        give(b2, g1)

        def head_sums(src, ready):
            b = take()
            for k in range(KT):
                m = mm(b.ap[0:16, 0:T], EH[:, k, :], src(k), k == 0, k == KT - 1, ready[k], *b.free)
            return b, m

        def spread(src16, k, *ready):
            b = take()
            m = mm(b.ap[:, 0:T], ETH[:, k, :], src16, True, True, *ready, *b.free)
            return b, m

        i_ka = ts(dve, ka1, par("rk_k_a_2", 0, n=8), -1.0, 1.0, ALU.mult, ALU.add)
        r_sq = []
        for k in range(KT):
            i = ts(dve, kkT[:, k, :], kT[:, k, :], par("rk_k_k_2", 0, i=k), None, ALU.mult, None, r_k[k])
            r_sq.append(af(xx[:, k, :], kkT[:, k, :], ACT.Square, i, *xr_use))
        b, m = head_sums(lambda k: xx[:, k, :], r_sq)
        i = ts(dve, s16, b.ap[0:16, 0:T], 1e-24, None, ALU.max, None, m)
        give(b, i)
        i = af(s16, s16, ACT.Sqrt, i)
        i16 = rec(s16, s16, i)
        r_kn = []
        for k in range(KT):
            b, m = spread(s16, k, i16)
            i = tt(dve, kkT[:, k, :], kkT[:, k, :], b.ap[:, 0:T], ALU.mult, m)
            give(b, i)
            r_kn.append(i)
        r_sq2 = []
        for k in range(KT):
            i = ts(dve, xx[:, k, :], aT[:, k, :], par("rk_k_a_2", 0, i=k), ka1[:, k:k + 1], ALU.mult, ALU.add,
                   i_a[k], i_ka, r_kn[0])
            i = tt(dve, kT[:, k, :], kT[:, k, :], xx[:, k, :], ALU.mult, i)
            r_sq2.append(stt(xx[:, k, :], rT[:, k, :], par("rk_r_k_2", 0, i=k), kT[:, k, :], ALU.mult, ALU.mult, i,
                             r_r[k]))
        b, m = head_sums(lambda k: xx[:, k, :], r_sq2)
        i_bon = cp(dve, s16b, b.ap[0:16, 0:T], m)
        give(b, i_bon)
        for k in range(KT):
            i = tt(pool, aT[:, k, :], aT[:, k, :], kkT[:, k, :], ALU.mult, r_kn[k], r_sq2[k])
            i = tt(pool, aT[:, k, :], aT[:, k, :], sw[:, k, :], ALU.mult, i, e_i[k])
            p_pool = tt(pool, kT[:, k, :], kT[:, k, :], sw[:, k, :], ALU.mult)
            for c in range(NC):
                s_, n = C0[c], CS[c]
                tt(dve, rT[:, k, s_:s_ + n], rT[:, k, s_:s_ + n], Lcol(k, c, 1, n), ALU.mult, e_c[k], r_sq2[k])
                p_dve = stt(kkT[:, k, s_:s_ + n], kkT[:, k, s_:s_ + n], -1.0, Lcol(k, c, 0, n), ALU.mult, ALU.mult, i)
        sP.close()
        sK = ctx.enter_context(ExitStack())
        barrier()
        Dm, DT, Xb, LT = (v3(alloc(sK, n, 16 * C)[0:C, :], 16) for n in ("Dm", "DT", "Xb", "LT"))
        BR, KR = (v4(alloc(sK, n, 32 * C)[0:C, :], 16, 2) for n in ("BR", "KR"))
        toks = [alloc(sK, n, 1024) for n in ("tokA", "tokB", "tokK", "tokV")]
        tk = [v4(a[:, :], 8, 2) for a in toks]
        AkV = v3(hn_[:, 0:1024], 16)
        W2 = v3(hn_[:, 1024:2048], 16)
        W1T = v3(alloc(sK, "W1T", 8 * C)[:, :], 8)
        U = v3(alloc(sK, "Ub", 1024)[:, :], 16)
        M = v3(alloc(sK, "Mst", 512)[:, :], 8)
        lv = (2, 4, 8, 16, 32, 64)
        i_M = pool.op(lambda e: e.memset(M[:, :, :], 0.0))
        r_y = [None] * NC

        def chunk(c, i_M, prev):
            t0, n = C0[c], CS[c]

            def bc(ap, w):
                return ap[0:n].unsqueeze(1).to_broadcast([n, w, ap.shape[-1]])

            def msk(name, rows=None):
                return con(2, name, n, n)

            mst = con(2, "mst", 2 * C, n).rearrange("p (a t) -> p a t", a=2)[:, :, 0:n]
            w_prev = list(prev)
            r_t = []
            for n_, src in enumerate((kkT, aT, kT, vT)):
                for hb in range(2):
                    b = take()
                    for k in range(4):
                        m = tr(b.ap[0:n, k * P:k * P + P], src[:, hb * 4 + k, t0:t0 + n], P, *b.free)
                    r = cp(act, toks[n_][0:n, hb * 512:hb * 512 + 512], b.ap[0:n, :], m, *w_prev)
                    give(b, r)
                    r_t.append(r)
            gr = {}
            for quad in range(4):
                hf, k0 = quad // 2, (quad % 2) * 4
                hs = slice(quad * 4, quad * 4 + 4)
                rows = slice(64 * hf, 64 * hf + 64)
                ra = []
                for src, dst in ((aT, BR), (kT, KR)):
                    for pair in range(2):
                        b = take()
                        for k in range(2):
                            kk_ = k0 + 2 * pair + k
                            for z, rr in enumerate((kkT, rT)):
                                m = mm(b.ap[0:n, (2 * k + z) * n:(2 * k + z) * n + n], src[rows, kk_, t0:t0 + n],
                                       rr[rows, kk_, t0:t0 + n], True, True, *b.free)
                        h0 = quad * 4 + pair * 2
                        for k in range(2):
                            r = tt(dve, dst[0:n, h0 + k, :, 0:n], v3(b.ap[0:n, 2 * k * n:2 * k * n + 2 * n], 2), mst,
                                   ALU.mult, m, i_c2, *w_prev)
                        give(b, r)
                        ra.append(r)
                b = take()
                for k in range(4):
                    m = mm(b.ap[0:n, k * n:k * n + n], kkT[rows, k0 + k, t0:t0 + n], aT[rows, k0 + k, t0:t0 + n],
                           True, True, *b.free)
                r = tt(dve, Dm[0:n, hs, 0:n], v3(b.ap[0:n, 0:4 * n], 4), bc(msk("m1"), 4), ALU.mult, m, *w_prev)
                give(b, r)
                rD = tt(pool, Dm[0:n, hs, 0:n], Dm[0:n, hs, 0:n], bc(ident[0:n, 0:n], 4), ALU.add, r)
                i = tt(pool, DT[0:n, hs, 0:n], BR[0:n, hs, 0, 0:n], bc(msk("l1"), 4), ALU.mult, *ra, *w_prev)
                rT_ = tt(pool, DT[0:n, hs, 0:n], DT[0:n, hs, 0:n], bc(ident[0:n, 0:n], 4), ALU.add, i)
                gr[quad] = (rD, rT_, ra)
            rD = {q: gr[q][0] for q in range(4)}
            rT_ = {q: gr[q][1] for q in range(4)}
            use, rL, lt_use = {}, {}, {}

            def masks(li, quad):
                hs = slice(quad * 4, quad * 4 + 4)
                rL[quad] = tt(pool, LT[0:n, hs, 0:n], BR[0:n, hs, 0, 0:n], bc(msk(f"l{lv[li]}"), 4), ALU.mult,
                              *gr[quad][2], lt_use.get(quad), *w_prev)

            for quad in range(4):
                masks(0, quad)
            for li in range(6):
                rX = {}
                for quad in range(4):
                    b = take()
                    for k in range(4):
                        hh = quad * 4 + k
                        m = mm(b.ap[0:n, k * n:k * n + n], LT[0:n, hh, 0:n], Dm[0:n, hh, 0:n], True, True,
                               rL[quad], rD[quad], *b.free)
                    lt_use[quad] = m
                    rX[quad] = cp(act, Xb[0:n, quad * 4:quad * 4 + 4, 0:n], v3(b.ap[0:n, 0:4 * n], 4), m,
                                  use.get(quad), *w_prev)
                    give(b, rX[quad])
                    if li + 1 < 6:
                        masks(li + 1, quad)
                for quad in range(4):
                    hs = slice(quad * 4, quad * 4 + 4)
                    if li < 5:
                        b = take()
                        for k in range(4):
                            hh = quad * 4 + k
                            m = mm(b.ap[0:n, k * n:k * n + n], DT[0:n, hh, 0:n], Xb[0:n, hh, 0:n], True, True,
                                   rX[quad], rT_[quad], *b.free)
                    b2 = take()
                    for k in range(4):
                        hh = quad * 4 + k
                        m2 = mm(b2.ap[0:n, k * n:k * n + n], Xb[0:n, hh, 0:n], DT[0:n, hh, 0:n], True, True,
                                rX[quad], rT_[quad], *b2.free)
                    use[quad] = m2
                    if li < 5:
                        rD[quad] = tt(dve, Dm[0:n, hs, 0:n], v3(b.ap[0:n, 0:4 * n], 4), Dm[0:n, hs, 0:n], ALU.add, m)
                        give(b, rD[quad])
                    rT_[quad] = tt(dve, DT[0:n, hs, 0:n], v3(b2.ap[0:n, 0:4 * n], 4), DT[0:n, hs, 0:n], ALU.add, m2)
                    give(b2, rT_[quad])
            r1, rk_, r2_ = [], {}, {}
            for quad in range(4):
                hf, k0 = quad // 2, (quad % 2) * 4
                rows = slice(64 * hf, 64 * hf + 64)
                b = take()
                for k in range(4):
                    m = mm(b.ap[0:n, k * 64:k * 64 + 64], KR[0:n, quad * 4 + k, 0, 0:n], tk[3][0:n, k0 + k, hf, :],
                           True, True, *gr[quad][2], *r_t, *b.free)
                r = cp(act, AkV[0:n, quad * 4:quad * 4 + 4, :], v3(b.ap[0:n, 0:256], 4), m, *w_prev)
                give(b, r)
                rk_[quad] = r
            for quad in range(4):
                hf, k0 = quad // 2, (quad % 2) * 4
                rows = slice(64 * hf, 64 * hf + 64)
                b = take()
                for k in range(4):
                    m = mm(b.ap[rows, k * n:k * n + n], tk[0][0:n, k0 + k, hf, :], DT[0:n, quad * 4 + k, 0:n],
                           True, True, rT_[quad], *b.free)
                r = cp(act, W1T[rows, k0:k0 + 4, 0:n], v3(b.ap[rows, 0:4 * n], 4), m, *w_prev)
                give(b, r)
                r1.append(r)
            for quad in range(4):
                b = take()
                for k in range(4):
                    m = mm(b.ap[0:n, k * 64:k * 64 + 64], DT[0:n, quad * 4 + k, 0:n], AkV[0:n, quad * 4 + k, :],
                           True, True, rk_[quad], *b.free)
                r2_[quad] = cp(act, W2[0:n, quad * 4:quad * 4 + 4, :], v3(b.ap[0:n, 0:256], 4), m, *w_prev)
                give(b, r2_[quad])
            rU = []
            for hf in range(2):
                b = take()
                for k in range(8):
                    m = mm(b.ap[0:n, k * 64:k * 64 + 64], W1T[64 * hf:64 * hf + 64, k, 0:n],
                           M[64 * hf:64 * hf + 64, k, :], True, True, *r1, i_M, *b.free)
                r = tt(dve, U[0:n, hf * 8:hf * 8 + 8, :], v3(b.ap[0:n, :], 8), W2[0:n, hf * 8:hf * 8 + 8, :], ALU.add,
                       m, r2_[3], *w_prev)
                give(b, r)
                rU.append(r)
            ys = []
            for hf in range(2):
                rows = slice(64 * hf, 64 * hf + 64)
                for kb in range(2):
                    b = take()
                    for k in range(kb * 4, kb * 4 + 4):
                        o = b.ap[rows, (k % 4) * n:(k % 4) * n + n]
                        hh = hf * 8 + k
                        mm(o, M[rows, k, :], rT[rows, k, t0:t0 + n], True, False, rU[hf], *b.free)
                        mm(o, U[0:n, hh, :], BR[0:n, hh, 1, 0:n], False, False)
                        m = mm(o, tk[3][0:n, k, hf, :], KR[0:n, hh, 1, 0:n], False, True)
                    ys.append((b, m, rows, kb))
            if c + 1 < NC:
                b = take()
                for hf in range(2):
                    for k in range(8):
                        o = b.ap[64 * hf:64 * hf + 64, k * 64:k * 64 + 64]
                        mm(o, tk[1][0:n, k, hf, :], U[0:n, hf * 8 + k, :], True, False, *b.free)
                        m = mm(o, tk[2][0:n, k, hf, :], tk[3][0:n, k, hf, :], False, True)
                i = tt(dve, M[:, :, :], v3(b.ap[:, :], 8), M[:, :, :], ALU.add, m, i_M)
                give(b, i)
                i_M = tt(dve, M[:, :, :], M[:, :, :], Lc[:, :, LO[c] + n:LO[c] + n + 1].to_broadcast([P, 8, 64]),
                         ALU.mult, i)
            ry = []
            for b, m, rows, kb in ys:
                r = cp(act, rT[rows, kb * 4:kb * 4 + 4, t0:t0 + n], v3(b.ap[rows, 0:4 * n], 4), m)
                give(b, r)
                ry.append(r)
            return i_M, [pe.last()], ry[-1]

        prev = []
        for c in range(NC):
            i_M, prev, r_y[c] = chunk(c, i_M, prev)
        sK.close()
        sQ = ctx.enter_context(ExitStack())
        barrier()
        YP = Pair(sQ, "yp2", KT * T2)
        GP = Pair(sQ, "gp", 2 * T2)
        y, sq = rT, v3(alloc(sQ, "ysq", KT * T2)[:, :], KT)
        bonT = v3(alloc(sQ, "bon", 2 * T2)[:, :], 2)
        s16c = alloc(sQ, "s16c", T2)[0:16, :]
        GP.put(0, 0, gl[:, 0:T], g1)
        GP.put(1, T2, gl[0:32, T:2 * T], rows=32)
        b, m = head_sums(lambda k: y[:, k, :], [r_y[NC - 1]] * KT)
        i16 = ts(dve, s16, b.ap[0:16, 0:T], 1.0 / 64, None, ALU.mult, None, m)
        give(b, i16)
        r_s = []
        for k in range(KT):
            b, m = spread(s16, k, i16)
            i = tt(dve, y[:, k, :], y[:, k, :], b.ap[:, 0:T], ALU.subtract, m)
            give(b, i)
            r_s.append(af(sq[:, k, :], y[:, k, :], ACT.Square, i))
        i_g = []
        for k in range(KT):
            b = take()
            wh, wl, ld = st.tile(("rk_g2_2", 0), 0, P, (k * P, P), P)
            mm3(b.ap[:, 0:T], (wh, wl), GP.at(0, T), True, False, *ld, *GP.ready[0], *GP.ready[1], *b.free)
            wh, wl, ld = st.tile(("rk_g2_2", 0), P, 32, (k * P, P), P)
            m = mm3(b.ap[:, 0:T], (wh, wl), GP.at(T2, T, 32), False, True, *ld)
            s = cp(act, aT[:, k, :], b.ap[:, 0:T], m)
            give(b, s)
            i_g.append(s)
        b, m = head_sums(lambda k: sq[:, k, :], r_s)
        i16, rd = rsqrt(s16c, b.ap[0:16, 0:T], 1.0 / 64, 64e-5, m)
        give(b, rd)
        bu_ = [None, None]
        i_b = []
        for k in range(KT):
            b, m = spread(s16b, k)
            i = tt(dve, kT[:, k, :], vT[:, k, :], b.ap[:, 0:T], ALU.mult, m)
            give(b, i)
            i_b.append(i)
        for k in range(KT):
            b, m = spread(s16c, k, i16)
            i = stt(y[:, k, :], y[:, k, :], par("rk_lnx_g_2", 0, i=k), b.ap[:, 0:T], ALU.mult, ALU.mult, m)
            give(b, i)
            i = stt(y[:, k, :], y[:, k, :], par("rk_lnx_b_2", 0, i=k), kT[:, k, :], ALU.add, ALU.add, i, i_b[k])
            i = tt(pool, y[:, k, :], y[:, k, :], aT[:, k, :], ALU.mult, i, i_g[k])
            YP.put(k, k * T2, y[:, k, :], i)
        rh = []
        for n in range(KT):
            b, m = dense(YP, T, KT, ("rk_w_o_2", 0), n * P, P)
            r = tt(dve, h[:, n, :], b.ap[:, 0:T], h[:, n, :], ALU.add, m)
            give(b, r)
            rh.append(r)
        sQ.close()
        sB.close()
        X = Pair(ctx, "x2", KT * T2)
        rh, xf = ffn(X, h, T, ("norm_g_2", 0, 2), ("ffn_w_in_2", 0, 1), ("ffn_w_out_2", 0, 1), 0.5, rh, [m])

        rh, xf = ffn(X, h, T, ("norm_g_2", 1, 0), ("ffn_w_in_2", 1, 0), ("ffn_w_out_2", 1, 0), 0.5, rh, xf)
        rs, r_rs = stats(h, T, rh, pool)
        scaled(X, h, T, ("norm_g_2", 1, 1), rh, xf)
        sD = ctx.enter_context(ExitStack())
        csg[3] = alloc(sD, "cs3", CW[3])
        Q = v3(alloc(sD, "Q", KT * T2)[:, :], KT)
        KK = v3(alloc(sD, "KK", 2 * T2)[:, :], 2)
        QI = v3(alloc(sD, "QI", 4 * T2)[:, :], 4)
        KI = v3(alloc(sD, "KI", T2)[:, :], 1)
        Vt = v3(alloc(sD, "Vt", NC * 264)[:, :], NC)
        rsT = alloc(sD, "rsT2", NC)
        oT = v3(alloc(sD, "oT", KT * T2)[:, :], KT)
        tmp = v3(alloc(sD, "rtmp", 4 * T2)[:, :], 4)
        sqr = v3(alloc(sD, "sqr", 3 * T2)[:, :], 3)
        f16 = alloc(sD, "f16", 2 * T2)
        bias = v3(alloc(sD, "bias", NC * T2)[:, :], NC)
        sR2 = alloc(sD, "sR2", 3 * (4 * T2 + 16))
        pt2 = alloc(sD, "pt2", 2 * NC * 4 * C)
        scr = v3(alloc(sD, "scr", NC * T2)[:, :], NC)
        wk = v3(alloc(sD, "wk", NC * T2)[:, :], NC)
        rel = v3(alloc(sD, "rel", 4 * T2)[:, :], 4)
        t8 = alloc(sD, "t8", 32)
        eqb, gtb, csb = (v3(alloc(sD, n, NC * T2)[:, :], NC) for n in ("eqb", "gtb", "csb"))
        barrier_tok = [q.last() for q in (pe, dve, act, pool)]
        i_c3 = sp.dma(lambda e: e.dma_start(csg[3][:, :], cdram[3]), s_in[6], *barrier_tok)
        cosF, sinF = con(3, "cos", T2), con(3, "sin", T2)
        st_ = {}
        r_ki = []
        for n in range(5):
            dst = KI[:, 0, :] if n == 0 else QI[:, n - 1, :]
            b, m = dense(X, T, KT, "at_i", n * P, P)
            r = tt(dve, dst, b.ap[:, 0:T], rs, ALU.mult, m, r_rs)
            give(b, r)
            st_[n] = r
        b = take()
        for c in range(NC):
            m = tr(b.ap[0:CS[c], c * P:c * P + P], rs[:, C0[c]:C0[c] + CS[c]], P, r_rs, *b.free)
        for c in range(NC):
            i_rsT = cp(dve, rsT[0:CS[c], c:c + 1], b.ap[0:CS[c], c * P:c * P + 1], m)
        give(b, i_rsT)
        bs = [take() for _ in range(NC)]
        for k in range(KT):
            wh, wl, ld = st.tile("at_vw", k * P, P, (0, 264), 264)
            xh, xl = X.at(k * T2, T)
            for c in range(NC):
                s_, n = C0[c], CS[c]
                vl = mm3(bs[c].ap[0:n, 0:264], (xh[:, s_:s_ + n], xl[:, s_:s_ + n]), (wh, wl), k == 0, k == KT - 1,
                         *ld, *(bs[c].free if k == 0 else ()))
        r_v = []
        for c in range(NC):
            n = CS[c]
            a = af(Vt[0:n, c, :], bs[c].ap[0:n, 0:264], ACT.Copy, vl, i_rsT, scale=rsT[0:n, c:c + 1])
            give(bs[c], a)
            r_v.append(ts(dve, Vt[0:n, c, 256:264], Vt[0:n, c, 256:264], float(8 ** -0.5 * 64 ** -0.5), None, ALU.mult,
                          None, a))
        rt_use = [None] * 4

        def rope(dst, n, r):
            b = take()
            m = mm(b.ap[:, 0:T], con(3, "RT", P), dst, True, True, r, i_c3, *b.free)
            t_ = tmp[:, n % 4, :]
            i = tt(dve, t_, b.ap[:, 0:T], sinF, ALU.mult, m, rt_use[n % 4])
            give(b, i)
            i2 = tt(pool, dst, dst, cosF, ALU.mult, m)
            i = tt(pool, dst, dst, t_, ALU.add, i, i2)
            rt_use[n % 4] = i
            return i

        for n in range(5):
            st_[n] = rope(KI[:, 0, :] if n == 0 else QI[:, n - 1, :], n, st_[n])
        jobs = [(KK[:, i, :], "at_k_g_2") for i in range(2)] + [(Q[:, i, :], "at_q_g_2") for i in range(8)]
        sq_free = [None] * 3
        zk = {}
        hb = {}

        def qk_dense(n):
            dst, g = jobs[n]
            b, m = dense(X, T, KT, "at_qk", n * P, P)
            r = cp(act, dst, b.ap[:, 0:T], m)
            give(b, r)
            s_ = sqr[:, n % 3, :]
            a = af(s_, dst, ACT.Square, r, sq_free[n % 3])
            zk[n] = (r, a)
            return m

        def qk_sum(n):
            if n in (0, 2):
                hb[n] = take()
            first = 0 if n < 2 else 2
            b = hb[first]
            m = mm(b.ap[0:16, 0:T], EH[:, n - first, :], sqr[:, n % 3, :], n == first, n in (1, 9), zk[n][1], *b.free)
            sq_free[n % 3] = m
            zk[n] = (zk[n][0], m)

        def qk_factor(first, last):
            o = 0 if first == 0 else T2
            f = f16[0:16, o:o + T]
            b = hb[first]
            i = stt(f, b.ap[0:16, 0:T], 1.0 / 64, rs[0:16, :], ALU.mult, ALU.mult, zk[last][1])
            give(b, i)
            i = tt(dve, f, f, rs[0:16, :], ALU.mult, i)
            i = ts(dve, f, f, 1e-6, None, ALU.add, None, i)
            i = af(f, f, ACT.Sqrt, i)
            i = rec(f, f, i)
            return f, tt(dve, f, f, rs[0:16, :], ALU.mult, i)

        rel_use = [None] * 4
        i_acc = {}
        idx = [(c, hh) for c in (2, 1, 0) for hh in range(8)]

        def index(n):
            c, hh = idx[n]
            nq, kw, hf = CS[c], C0[c] + CS[c], hh % 2
            b = take()
            m = mm(b.ap[0:nq, 0:kw], QI[64 * hf:64 * hf + 64, hh // 2, C0[c]:kw],
                   KI[64 * hf:64 * hf + 64, 0, 0:kw], True, True, st_[0], st_[1 + hh // 2], *b.free)
            rr = rel[0:nq, n % 4, 0:kw]
            a = af(rr, b.ap[0:nq, 0:kw], ACT.Relu, m, rel_use[n % 4])
            give(b, a)
            w_ = Vt[0:nq, c, 256 + hh:257 + hh]
            o = scr[0:nq, c, 0:kw]
            if hh == 0:
                i = ts(dve, o, rr, w_, None, ALU.mult, None, a, r_v[c])
            else:
                i = stt(o, rr, w_, o, ALU.mult, ALU.add, a, i_acc[c])
            rel_use[n % 4] = i
            if hh == 7:
                d = scr[0:nq, c, C0[c]:kw]
                i = tt(dve, d, d, con(3, "cm", nq, nq), ALU.add, i)
            i_acc[c] = i

        def best(c):
            nq, kw = CS[c], C0[c] + CS[c]
            cur = i_acc[c]
            for rnd in range(8):
                src = (scr if rnd == 0 else wk)[0:nq, c, 0:kw]
                m8, w_ = t8[0:nq, c * 8:c * 8 + 8], wk[0:nq, c, 0:kw]
                cur = dve.op(lambda e, m8=m8, src=src: e.max(m8, src), cur)
                if rnd < 7:
                    cur = dve.op(lambda e, m8=m8, src=src, w_=w_: e.match_replace(w_, m8, src, -BIG), cur)
                yield cur

        r_b = {}

        def choose(c, cur):
            nq, kw = CS[c], C0[c] + CS[c]
            th, cn = t8[0:nq, c * 8 + 7:c * 8 + 8], t8[0:nq, 24 + c:25 + c]
            S_, e_, g_, q_ = (a[0:nq, c, 0:kw] for a in (scr, eqb, gtb, csb))
            i1 = ts(dve, g_, S_, th, None, ALU.is_gt, None, cur)
            i2 = ts(dve, e_, S_, th, None, ALU.is_equal, None)
            i3 = red(cn, g_, ALU.add, i1)
            o_ = ones[0:nq, 0:1].to_broadcast([nq, kw])
            i5 = dve.op(lambda e: e.tensor_tensor_scan(q_, o_, e_, 0.0, ALU.mult, ALU.add), i2)
            i4 = ts(dve, cn, cn, -1.0, 64.0, ALU.mult, ALU.add, i3)
            i6 = stt(q_, q_, cn, e_, ALU.is_le, ALU.mult, i5, i4)
            i7 = tt(dve, q_, q_, g_, ALU.add, i6)
            i8 = ts(dve, bias[0:nq, c, 0:kw], q_, BIG, -BIG, ALU.mult, ALU.add, i7)
            d = bias[0:nq, c, C0[c]:kw]
            r_b[c] = tt(dve, d, d, con(3, "cm", nq, nq), ALU.min, i8)

        for n in range(10):
            x_last = qk_dense(n)
            if n >= 1:
                qk_sum(n - 1)
            for z in range(6 * n, min(6 * n + 6, 24)):
                index(z)
            if n == 4:
                gens = [best(c) for c in range(NC)]
                cur = [None] * NC
            if n >= 4:
                for _ in range(2):
                    for c in range(NC):
                        v_ = next(gens[c], None)
                        cur[c] = v_ if v_ is not None else cur[c]
        qk_sum(9)
        fk, ik = qk_factor(0, 1)
        fq, iq = qk_factor(2, 9)
        rs_use[(n_stat[0] - 1) % 2] = [iq]
        r_kq = {}
        for n in range(11):
            if n < 10:
                dst, g = jobs[n]
                b, m = spread(fk if n < 2 else fq, n if n < 2 else n - 2, ik if n < 2 else iq)
                i = stt(dst, dst, par(g, 0), b.ap[:, 0:T], ALU.mult, ALU.mult, m, zk[n][0])
                give(b, i)
                r_kq[n] = i
            if n >= 1:
                r_kq[n - 1] = rope(jobs[n - 1][0], n - 1, r_kq[n - 1])
        for c in range(NC):
            choose(c, cur[c])
        units = [(c, g) for c in range(NC) for g in range(4)]
        s_use, pt_use, stt_ = [None] * 3, [None] * 2, {}
        r_oT = {}

        def a_s(n):
            c, g = units[n]
            nq, kw, hf, k0 = CS[c], C0[c] + CS[c], g % 2, (g // 2) * 4
            o = n % 3 * (4 * T2 + 16)
            s = v3(sR2[0:nq, o:o + 4 * kw], 4)
            for k in range(4):
                b = take()
                m = mm(b.ap[0:nq, 0:kw], Q[64 * hf:64 * hf + 64, k0 + k, C0[c]:kw],
                       KK[64 * hf:64 * hf + 64, g // 2, 0:kw], True, True, r_kq[g // 2], r_kq[2 + k0 + k], *b.free)
                i = stt(s[:, k, :], b.ap[0:nq, 0:kw], 0.125, bias[0:nq, c, 0:kw], ALU.mult, ALU.add, m, r_b[c],
                        s_use[n % 3])
                give(b, i)
            mx, sm = sR2[0:nq, o + 4 * T2:o + 4 * T2 + 4], sR2[0:nq, o + 4 * T2 + 8:o + 4 * T2 + 12]
            i = red(mx, s, ALU.max, i, negate=True)
            for k in range(4):
                e_ = af(s[:, k, :], s[:, k, :], ACT.Exp, i, bias=mx[:, k:k + 1], acc=sm[:, k:k + 1])
            stt_[n] = (s, sm, e_)

        def a_p(n):
            c, g = units[n]
            s, sm, e_ = stt_[n]
            nq, kw = CS[c], C0[c] + CS[c]
            i = rec(sm, sm, e_)
            i = tt(dve, s, s, sm.unsqueeze(2).to_broadcast([nq, 4, kw]), ALU.mult, i)
            stt_[n] = (s, i)

        def a_t(n):
            c, g = units[n]
            s, i = stt_[n]
            nq = CS[c]
            pt = v3(pt2[:, n % 2 * NC * 4 * C:(n % 2 + 1) * NC * 4 * C], NC)
            for kc in range(c + 1):
                b = take()
                nk = CS[kc]
                for k in range(4):
                    m = tr(b.ap[0:nk, k * nq:k * nq + nq], s[:, k, C0[kc]:C0[kc] + nk], nq, i, *b.free)
                r = cp(act, pt[0:nk, kc, 0:4 * nq], b.ap[0:nk, 0:4 * nq], m, pt_use[n % 2])
                give(b, r)
            s_use[n % 3] = m
            stt_[n] = (pt, r)

        def a_v(n):
            c, g = units[n]
            pt, r = stt_[n]
            nq, hf, k0 = CS[c], g % 2, (g // 2) * 4
            rows = slice(64 * hf, 64 * hf + 64)
            b = take()
            for kc in range(c + 1):
                nk = CS[kc]
                m = mm(b.ap[rows, 0:4 * nq], Vt[0:nk, kc, g * 64:g * 64 + 64], pt[0:nk, kc, 0:4 * nq], kc == 0,
                       kc == c, r, r_v[kc], *b.free)
            pt_use[n % 2] = m
            i = cp(act, oT[rows, k0:k0 + 4, C0[c]:C0[c] + nq], v3(b.ap[rows, 0:4 * nq], 4), m)
            give(b, i)
            r_oT[(c, g)] = i

        for n in range(len(units) + 3):
            if n < len(units):
                a_s(n)
            if 0 <= n - 1 < len(units):
                a_p(n - 1)
            if 0 <= n - 2 < len(units):
                a_t(n - 2)
            if 0 <= n - 3 < len(units):
                a_v(n - 3)
        for k in range(KT):
            X.put(k, k * T2, oT[:, k, :], r_oT[(2, 1 if k < 4 else 3)], x_last)
        rh = []
        for n in range(KT):
            b, m = dense(X, T, KT, "at_w_o_p", n * P, P)
            r = tt(dve, h[:, n, :], b.ap[:, 0:T], h[:, n, :], ALU.add, m)
            give(b, r)
            rh.append(r)
        sD.close()
        rh, xf = ffn(X, h, T, ("norm_g_2", 1, 2), ("ffn_w_in_2", 1, 1), ("ffn_w_out_2", 1, 1), 0.5, rh, [m])
        i_o = sp.dma(lambda e: e.dma_start(out, hx), s_out, *rh)
        sp.wait(i_o)

        assert st.n == NCH, st.n
        st.dram = wdecl(st.n)
        counts = {}
        for q in (pe, dve, act, pool, sp):
            q.number(counts)
        block = ctx.enter_context(nc.Block())

        @block.sync
        def _(eng):
            sp.emit(eng)

        @block.scalar
        def _(eng):
            act.emit(eng)

        @block.gpsimd
        def _(eng):
            pool.emit(eng)

        @block.vector
        def _(eng):
            dve.emit(eng)

        @block.tensor
        def _(eng):
            pe.emit(eng)
    return st.plan, st.n


def arrange(inp, plan, n):
    w_in = np.asarray(inp["w_in"])[0]
    q = [w_in[:, 512 + 64 * i:576 + 64 * i] for i in HO1]
    gates = w_in[:, 2816:2852]
    gcol = [h * 3 + br for br in range(3) for h in HO1]
    at = np.asarray(inp["at_w_in_2"])[0]
    wo = np.asarray(inp["w_out"])[0]
    ao = np.asarray(inp["at_w_o_2"])[0]
    w2k = np.asarray(inp["cmp_k_w2"])[0]
    src = {
        ("w_in", 0): np.concatenate([w_in[:, 0:512]] + q + [w_in[:, 1280:]], axis=1),
        "w_vg": np.concatenate([w_in[:, 2048:2304], gates[:, gcol], w_in[:, 2560:2816]], axis=1),
        "cmp_k_w1": np.asarray(inp["cmp_k_w1"])[0].reshape(2048, 256),
        "cmp_v_w1": np.asarray(inp["cmp_v_w1"])[0].reshape(2048, 256),
        "cmp_k_w2d": np.concatenate([w2k, w2k], axis=1),
        "cmp_v_w2": np.asarray(inp["cmp_v_w2"])[0],
        "w_out_p": np.concatenate([wo[0:256]] + [wo[256 + 64 * i:320 + 64 * i] for i in HO1], axis=0),
        "at_i": np.concatenate([at[:, 2048:2112], at[:, 2048:2112], at[:, 1536:2048]], axis=1),
        "at_qk": np.concatenate([at[:, 1024:1280]] + [at[:, 64 * i:64 * i + 64] for i in HO2], axis=1),
        "at_vw": np.concatenate([at[:, 1280:1536], at[:, 2112:2120]], axis=1),
        "at_w_o_p": np.concatenate([ao[64 * i:64 * i + 64] for i in HO2], axis=0),
    }
    W = np.zeros((n, P, CH), np.float32)
    for c, off, key, k0, kp, (c0, cw), w in plan:
        if key not in src:
            src[key] = np.asarray(inp[key[0]])[key[1:]]
        W[c, 0:kp, off:off + w] = src[key][k0:k0 + kp, c0:c0 + cw]
    return W


def kernel(**inputs):
    import concourse.bacc as _bacc
    from concourse.bass_utils import run_bass_kernel_spmd as _run

    nc = _bacc.Bacc("TRN2", target_bir_lowering=False, num_devices=1)
    carr, cat = consts()
    pat, npar = param_offsets()
    arrays = {}

    def declare(name, a):
        arrays[name] = np.ascontiguousarray(a)
        return nc.dram_tensor(name, arrays[name].shape, F32, kind="ExternalInput").ap()

    cd = [declare(f"consts{i}_dram", a) for i, a in enumerate(carr)]
    pd = declare("params_dram", pack_params(inputs))
    x = np.asarray(inputs["x"])[0]
    xd = declare("x_dram", x.T.reshape(KT, P, T1).transpose(1, 0, 2))
    md = declare("meta_dram", np.asarray(inputs["meta_2"]).T.reshape(KT, P, NM).transpose(1, 0, 2))
    out = nc.dram_tensor("out_dram", (P, KT, T1), F32, kind="ExternalOutput").ap()

    def wdecl(n):
        return nc.dram_tensor("w_dram", (n, P, CH), F32, kind="ExternalInput").ap()

    plan, n = build(nc, out, wdecl, cd, pd, xd, md, [a.shape[1] for a in carr], cat, pat, npar)
    arrays["w_dram"] = arrange(inputs, plan, n)
    r = _run(nc, [arrays], core_ids=[0])
    got = r.results[0]["out_dram"]
    return np.ascontiguousarray(got.transpose(1, 0, 2).reshape(1, KT * P, T1).transpose(0, 2, 1))
```

```python
from contextlib import ExitStack

import numpy as np
import concourse.bass as bass
from concourse import mybir

F32 = mybir.dt.float32
F32R = mybir.dt.float32r
ALU = mybir.AluOpType
ACT = mybir.ActivationFunctionType
AX = mybir.AxisListType
P = 128

T1 = 256
T2 = 272
NM = 16
KT = 8
DFF = 2816
MT = DFF // P
CS = (96, 96, 80)
C0 = (0, 96, 192)
NC = 3
C = 96
CH = 1024
NRAW = 4
NSPL = 4
AHEAD = 2
NCH = 434
BIG = 3.0e38
KAPPA = float(np.exp(-0.5))

HO1 = [0, 3, 1, 4, 2, 5, 6, 9, 7, 10, 8, 11]
HO2 = [0, 4, 1, 5, 2, 6, 3, 7, 8, 12, 9, 13, 10, 14, 11, 15]


def slopes12():
    s8 = [2.0 ** (-(i + 1)) for i in range(8)]
    s16 = [2.0 ** (-0.5 * (i + 1)) for i in range(16)]
    return np.asarray(s8 + s16[0::2][:4], dtype=np.float32)


class Ins:

    def __init__(self, q, fn, amount=1, sem=None):
        self.q, self.fn, self.wanted, self.value = q, fn, sem is not None, None
        self.amount, self.sem = amount, sem


class Queue:

    def __init__(self, sem):
        self.sem, self.items = sem, []

    def wait(self, *producers):
        for p in producers:
            if p is not None:
                p.wanted = True
                self.items.append(p)

    def op(self, fn, *producers):
        self.wait(*producers)
        i = Ins(self, fn)
        self.items.append((i,))
        return i

    def dma(self, fn, sem, *producers):
        self.wait(*producers)
        i = Ins(self, fn, 16, sem)
        self.items.append((i,))
        return i

    def last(self):
        for it in reversed(self.items):
            if isinstance(it, tuple):
                return it[0]
        return None

    def number(self, counts):
        for it in self.items:
            if isinstance(it, tuple) and it[0].wanted:
                i = it[0]
                s = i.sem if i.sem is not None else self.sem
                i.sem = s
                counts[s] = counts.get(s, 0) + i.amount
                i.value = counts[s]

    def emit(self, eng):
        seen = {}
        for it in self.items:
            if isinstance(it, tuple):
                i = it[0]
                r = i.fn(eng)
                if i.wanted:
                    r.then_inc(i.sem, i.amount)
            elif seen.get(it.sem, 0) < it.value:
                eng.wait_ge(it.sem, it.value)
                seen[it.sem] = it.value


class Bank:
    def __init__(self, ap):
        self.ap, self.free = ap, []


def consts():
    groups = [([], {}), ([], {}), ([], {}), ([], {})]

    def put(g, name, a):
        parts, at = groups[g]
        a = np.asarray(a, np.float32)
        full = np.zeros((P, a.shape[1]), np.float32)
        full[:a.shape[0]] = a
        at[name] = sum(x.shape[1] for x in parts)
        parts.append(full)

    p = np.arange(P)
    put(0, "ident", np.eye(P))
    put(0, "ones", np.ones((P, P)))
    E = np.zeros((P, KT, 16))
    for k in range(KT):
        E[p, k, 2 * k + p // 64] = 1.0
    put(0, "E", E.reshape(P, -1))
    put(0, "ET", E.transpose(2, 1, 0).reshape(16, -1))
    tq = np.arange(T1).reshape(2, P).T[:, :, None]
    pos = np.arange(T1)[None, None, :]
    put(1, "D", np.where(pos <= tq, tq - pos, BIG).reshape(P, -1))
    sl = slopes12()
    n15 = np.arange(15)[None, None, None, :]
    t4 = tq[:, :, :, None]
    bc = -sl[HO1][None, None, :, None] * (t4 - (16.0 * n15 + 15.5))
    put(1, "Bc", np.where(16 * n15 + 31 <= t4, bc, -BIG).reshape(P, -1))
    s, t = np.arange(C)[:, None], np.arange(C)[None, :]
    put(2, "mst", np.concatenate([(s < t), (s <= t)], axis=1))
    for lv in (1, 2, 4, 8, 16, 32, 64):
        put(2, f"l{lv}", (s // (2 * lv) == t // (2 * lv)) & (s // lv % 2 == 0) & (t // lv % 2 == 1))
    R = np.zeros((P, P))
    for b in (0, 64):
        for d in range(8):
            R[b + d, b + d + 8] = -1.0
            R[b + d + 8, b + d] = 1.0
    put(3, "RT", R.T)
    inv = (np.float32(500000.0) ** (-np.arange(0, 16, 2, dtype=np.float32) / np.float32(16))).astype(np.float32)
    ang = np.arange(T2, dtype=np.float32)[:, None] * inv[None, :]
    cf, sf = np.ones((P, T2)), np.zeros((P, T2))
    for b in (0, 64):
        for d in range(16):
            cf[b + d] = np.cos(ang[:, d % 8])
            sf[b + d] = np.sin(ang[:, d % 8])
    put(3, "cos", cf)
    put(3, "sin", sf)
    put(3, "cm", np.where(t <= s, 0.0, -BIG))
    return [np.concatenate(parts, axis=1) for parts, _ in groups], [at for _, at in groups]


def params():
    want = [
        ("attn_norm", (0,), "col"), ("ffn_norm", (0,), "col"), ("final_norm", (), "col"),
        ("conv_w", (0,), "rows"), ("conv_b", (0,), "col"), ("conv_ln_g", (0,), "col"), ("conv_ln_b", (0,), "col"),
        ("cmp_k_pe", (0,), "pe"), ("cmp_v_pe", (0,), "pe"),
    ]
    for i in range(2):
        for j in range(3):
            want.append(("norm_g_2", (i, j), "col"))
    for j in range(6):
        want.append(("rk_mix_2", (0, j), "col"))
    for nm in ("rk_w0_2", "rk_a0_2", "rk_k_k_2", "rk_k_a_2", "rk_lnx_g_2", "rk_lnx_b_2"):
        want.append((nm, (0,), "col"))
    want.append(("rk_r_k_2", (0,), "col"))
    want.append(("at_q_g_2", (0,), "dup"))
    want.append(("at_k_g_2", (0,), "dup"))
    return want


PW = {"conv_w": 62, "conv_b": 2, "conv_ln_g": 2, "conv_ln_b": 2, "cmp_k_pe": 16, "cmp_v_pe": 16,
      "at_q_g_2": 1, "at_k_g_2": 1}


def param_offsets():
    at, n = {}, 0
    for name, idx, kind in params():
        at[(name,) + idx] = n
        n += PW.get(name, 8)
    return at, n


def pack_params(inp):
    out = []
    for name, idx, kind in params():
        a = np.asarray(inp[name])[idx]
        if kind == "col":
            a = a.reshape(-1, P).T
        elif kind == "rows":
            a = a.reshape(31, 2, P).transpose(2, 1, 0).reshape(P, 62)
        elif kind == "pe":
            a = a.reshape(16, P).T
        else:
            a = np.concatenate([a, a]).reshape(P, 1)
        out.append(a)
    return np.ascontiguousarray(np.concatenate(out, axis=1))


class Stream:

    def __init__(self, raw, hi, lo, sync, pe, act, dve, sems):
        self.raw, self.hi, self.lo = raw, hi, lo
        self.sync, self.pe, self.act, self.dve, self.sems = sync, pe, act, dve, sems
        self.plan, self.n, self.pos = [], 0, CH
        self.upper, self.split, self.last_use, self.landed = [], [], [], []
        self.dram = None

    def fetch(self, c):
        s = c % NRAW
        before = [self.split[c - NRAW][1], self.split[c - NRAW][0]] if c >= NRAW else []
        self.landed.append(self.sync.dma(
            lambda e: e.dma_start(self.raw[:, s * CH:(s + 1) * CH], self.dram[c]), self.sems[s], *before))

    def part_hi(self, c):
        s, d = c % NRAW, c % NSPL
        raw, hi = self.raw[:, s * CH:(s + 1) * CH], self.hi[:, d * CH:(d + 1) * CH]
        used = self.last_use[c - NSPL] if c >= NSPL else None
        self.upper.append(self.act.op(lambda e: e.activation(hi, raw, ACT.Copy), self.landed[c], used))

    def part_lo(self, c):
        s, d = c % NRAW, c % NSPL
        raw = self.raw[:, s * CH:(s + 1) * CH]
        hi, lo = self.hi[:, d * CH:(d + 1) * CH], self.lo[:, d * CH:(d + 1) * CH]
        used = self.last_use[c - NSPL] if c >= NSPL else None
        b = self.dve.op(lambda e: e.tensor_tensor(lo, raw, hi.bitcast(F32), ALU.subtract), self.upper[c], used)
        self.split.append((self.upper[c], b))
        if c + NRAW < NCH:
            self.fetch(c + NRAW)


    def ahead(self):
        while len(self.split) < min(self.n + AHEAD, NCH):
            while len(self.upper) < min(len(self.split) + 2, NCH):
                self.part_hi(len(self.upper))
            self.part_lo(len(self.split))

    def tile(self, key, k0, kp, cols, w):
        if self.pos + w > CH:
            if self.n:
                self.last_use.append(self.pe.last())
            self.n += 1
            self.pos = 0
            self.ahead()
        off = self.pos
        self.pos += w
        c = self.n - 1
        self.plan.append((c, off, key, k0, kp, cols, w))
        o = c % NSPL * CH + off
        return self.hi[0:kp, o:o + w], self.lo[0:kp, o:o + w], self.split[c]


def build(nc, out, wdecl, cdram, pdram, xdram, mdram, CW, CAT, PAT, NPAR):
    with ExitStack() as ctx:
        def alloc(scope, name, n, dt=F32, side="left"):
            return scope.enter_context(nc.sbuf_tensor(name, [P, n], dt, side=side))

        def sem(name):
            return ctx.enter_context(nc.semaphore(name))

        h = alloc(ctx, "h", KT * T2)[:, :].rearrange("p (k t) -> p k t", k=KT)
        cs0 = alloc(ctx, "cs0", CW[0])
        pr = alloc(ctx, "pr", NPAR)
        rs_ = alloc(ctx, "rs", 2 * T2)
        sq_ = alloc(ctx, "sq", 3 * T2)
        small = alloc(ctx, "small", 16)
        raw = alloc(ctx, "w_raw", NRAW * CH)
        whi = alloc(ctx, "w_hi", NSPL * CH, F32R)
        wlo = alloc(ctx, "w_lo", NSPL * CH, F32R)
        psum = [ctx.enter_context(nc.psum_tensor(f"ps{i}", [P, 512], F32)) for i in range(8)]

        pe, dve, act, pool, sp = (Queue(sem(n)) for n in ("s_pe", "s_dve", "s_act", "s_pool", "s_sp"))
        st = Stream(raw, whi, wlo, sp, pe, act, dve, [sem(f"s_raw{i}") for i in range(NRAW)])
        s_in = [sem(f"s_in{i}") for i in range(10)]
        s_x = [sem(f"s_cx{i}") for i in range(8)]
        s_out = sem("s_out")
        hx = h[:, :, NM:T2]
        csg = {0: cs0}

        def v3(ap, a):
            return ap.rearrange("p (a b) -> p a b", a=a)

        def v4(ap, a, b):
            return ap.rearrange("p (a b c) -> p a b c", a=a, b=b)

        def con(g, name, n, rows=P):
            return csg[g][0:rows, CAT[g][name]:CAT[g][name] + n]

        def par(*key, i=0, rows=P, n=1):
            o = PAT[key] + i
            return pr[0:rows, o:o + n]

        ident = con(0, "ident", P)
        ones = con(0, "ones", P)
        EH = v3(con(0, "E", 128), KT)
        ETH = v3(con(0, "ET", 1024, 16), KT)
        free = [Bank(p) for p in psum]

        def take():
            return free.pop(0)

        def give(b, *readers):
            b.free = list(readers)
            free.append(b)

        def mm(o, lhsT, rhs, start, stop, *w):
            return pe.op(lambda e: e.matmul(o, lhsT, rhs, start=start, stop=stop), *w)

        def tr(o, a, n, *w):
            return pe.op(lambda e: e.transpose(o, a, ident[0:n, 0:n]), *w)

        def tt(q, o, a, b, op, *w):
            return q.op(lambda e: e.tensor_tensor(o, a, b, op), *w)

        def stt(o, a, s, b, op0, op1, *w):
            return dve.op(lambda e: e.scalar_tensor_tensor(out=o, in0=a, scalar=s, in1=b, op0=op0, op1=op1), *w)

        def ts(q, o, a, s1, s2, op0, op1, *w):
            if op1 is None:
                return q.op(lambda e: e.tensor_scalar(o, a, s1, None, op0), *w)
            return q.op(lambda e: e.tensor_scalar(o, a, s1, s2, op0, op1), *w)

        def cp(q, o, a, *w):
            if q is act:
                return q.op(lambda e: e.activation(o, a, ACT.Copy), *w)
            return q.op(lambda e: e.tensor_copy(o, a), *w)

        def af(o, a, f, *w, bias=0.0, scale=1.0, acc=None):
            if acc is None:
                return act.op(lambda e: e.activation(o, a, f, bias=bias, scale=scale), *w)
            return act.op(lambda e: e.activation(o, a, f, bias=bias, scale=scale, accum_out=acc), *w)

        def rec(o, a, *w):
            return dve.op(lambda e: e.reciprocal(o, a), *w)

        def red(o, a, op, *w, negate=False):
            return dve.op(lambda e: e.tensor_reduce(o, a, AX.X, op, negate=negate), *w)

        def rsqrt(dst, src, scale, eps, *w):
            a = ts(dve, dst, src, scale, eps, ALU.mult, ALU.add, *w)
            b = af(dst, dst, ACT.Sqrt, a)
            return rec(dst, dst, b), a

        class Pair:

            def __init__(self, scope, name, n, side="left"):
                if name is None:
                    self.hi, self.lo = n
                else:
                    self.hi = alloc(scope, name + "_hi", n, F32R, side)
                    self.lo = alloc(scope, name + "_lo", n, F32R, side)
                self.ready = {}

            def at(self, off, n, rows=P):
                return self.hi[0:rows, off:off + n], self.lo[0:rows, off:off + n]

            def put(self, k, off, src, *w, rows=P, after=()):
                shape = src.shape[-1]
                hi, lo = self.at(off, shape, rows)
                a = af(hi, src, ACT.Copy, *w, *after)
                b = tt(dve, lo, src, hi.bitcast(F32), ALU.subtract, a)
                self.ready[k] = (a, b)
                return b

            def put_late(self, k, off, src, *w, rows=P, after=(), q=dve):
                hi, lo = self.at(off, src.shape[-1], rows)
                a = af(hi, src, ACT.Copy, *w, *after)

                def low():
                    b = tt(q, lo, src, hi.bitcast(F32), ALU.subtract, a)
                    self.ready[k] = (a, b)
                    return b
                return low

            def put_scaled(self, k, off, src, col, *w, after=()):
                hi, lo = self.at(off, src.shape[-1])
                a = af(hi, src, ACT.Copy, *w, *after, scale=col)
                b = stt(lo, src, col, hi.bitcast(F32), ALU.mult, ALU.subtract, a)
                self.ready[k] = (a, b)
                return b

        def mm3(o, lhs, rhs, start, stop, *w):
            mm(o, lhs[0], rhs[0], start, False, *w)
            mm(o, lhs[0], rhs[1], False, False)
            return mm(o, lhs[1], rhs[0], False, stop)

        i_p = act.dma(lambda e: e.dma_start(pr[:, :], pdram), s_in[1])
        i_x = []
        for k, s in enumerate((s_in[2], s_in[7], s_in[8], s_in[9])):
            i_x.append(sp.dma(lambda e, k=k: e.dma_start(hx[:, 2 * k:2 * k + 2, :], xdram[:, 2 * k:2 * k + 2, :]), s))
            if k == 0:
                st.fetch(0)
        st.fetch(1)
        i_c0 = sp.dma(lambda e: e.dma_start(cs0[:, :], cdram[0]), s_in[0])
        st.fetch(2)
        st.fetch(3)
        i_m = sp.dma(lambda e: e.dma_start(h[:, :, 0:NM], mdram), s_in[3])

        n_stat = [0]
        rs_use = [[], []]
        jq_use = [None] * 3
        sq_use = [[], [], []]

        def tile_squares(src, T, q, X=None, key=None, after=()):
            j = n_stat[0] % 2
            n_stat[0] += 1
            acc = sq_[:, 0:T]
            v = {"low": None, "acc": None}

            def flush():
                if v["low"] is not None:
                    v["low"]()
                    v["low"] = None

            def step(k, ready, parts=(0, 1)):
                s = 1 + k % 2
                t_ = acc if k == 0 else sq_[:, s * T2:s * T2 + T]
                if X is not None and 0 in parts:
                    hi, lo = X.at(k * T2, T)
                    a = af(hi, src[:, k, :], ACT.Copy, ready, i_p, *(after if k == 0 else ()), scale=par(*key, i=k))
                    flush()

                    def low():
                        b = stt(lo, src[:, k, :], par(*key, i=k), hi.bitcast(F32), ALU.mult, ALU.subtract, a)
                        X.ready[k] = (a, b)
                    v["low"] = low
                if 1 not in parts:
                    return
                i = af(t_, src[:, k, :], ACT.Square, ready, *sq_use[0 if k == 0 else s])
                if k:
                    i = tt(q, acc, acc, t_, ALU.add, i, v["acc"])
                    sq_use[s] = [i]
                v["acc"] = i

            def finish():
                flush()
                b = take()
                m = mm(b.ap[:, 0:T], ones, acc, True, True, v["acc"], i_c0, *b.free)
                sq_use[0] = [m]
                rs = rs_[:, j * T2:j * T2 + T]
                r, rd = rsqrt(rs, b.ap[:, 0:T], 1.0 / 1024, 1e-6, m, *rs_use[j])
                give(b, rd)
                return rs, r
            return step, flush, finish

        def joint_squares(X, after):
            n_stat[0] += 2
            acc, acc2 = sq_[:, 0:T1], jq[:, 0, 0:T2]
            v = {"low": None, "a": None, "b": None, "meta": []}
            key = ("norm_g_2", 0, 0)
            hm = h[:, :, 0:NM]
            i_gg = tt(dve, gg, par("final_norm", n=8), par(*key, n=8), ALU.mult, i_p)
            for k in range(KT):
                hi, lo = X.at(k * T2, NM)
                a = af(hi, h[:, k, 0:NM], ACT.Copy, i_m, i_p, *(after if k == 0 else ()), scale=par(*key, i=k))
                v["meta"].append((a, hi, lo))
            for k, (a, hi, lo) in enumerate(v["meta"]):
                last = stt(lo, h[:, k, 0:NM], par(*key, i=k), hi.bitcast(F32), ALU.mult, ALU.subtract, a)
            t_ = jq[:, 1, 0:NM * KT]
            i = af(v3(t_, KT), hm, ACT.Square, i_m)
            i_mq = red(acc2[:, 0:NM], t_.rearrange("p (k t) -> p t k", k=KT), ALU.add, i)

            def flush():
                if v["low"] is not None:
                    v["low"]()
                    v["low"] = None

            def step(k, ready):
                s = 1 + k % 2
                hi, lo = X.at(k * T2 + NM, T1)
                a = af(hi, hx[:, k, :], ACT.Copy, ready, i_gg, scale=gg[:, k:k + 1])
                flush()

                def low():
                    b = stt(lo, hx[:, k, :], gg[:, k:k + 1], hi.bitcast(F32), ALU.mult, ALU.subtract, a)
                    X.ready[k] = (a, b)
                v["low"] = low
                t1 = acc if k == 0 else sq_[:, s * T2:s * T2 + T1]
                t2 = acc2[:, NM:T2] if k == 0 else jq[:, s, 0:T1]
                i1 = af(t1, hx[:, k, :], ACT.Square, ready, *sq_use[0 if k == 0 else s])
                i2 = af(t2, hx[:, k, :], ACT.Square, ready, jq_use[s] if k else i_mq, scale=par("final_norm", i=k))
                if k:
                    i1 = tt(pool, acc, acc, t1, ALU.add, i1, v["a"])
                    i2 = tt(pool, acc2[:, NM:T2], acc2[:, NM:T2], t2, ALU.add, i2, v["b"])
                    sq_use[s] = [i1]
                    jq_use[s] = i2
                v["a"], v["b"] = i1, i2

            def finish():
                flush()
                b = take()
                m = mm(b.ap[:, 0:T1], ones, acc, True, True, v["a"], i_mq, *b.free)
                sq_use[0] = [m]
                rs1, rs2 = rs_[:, 0:T1], rs_[:, T2:2 * T2]
                r1, rd = rsqrt(rs1, b.ap[:, 0:T1], 1.0 / 1024, 1e-6, m, *rs_use[0])
                give(b, rd)
                b = take()
                m = mm(b.ap[:, 0:T2], ones, acc2, True, True, v["b"], *b.free)
                x_ = jq[:, 1, 0:T1]
                r = tt(dve, x_, b.ap[:, NM:T2], rs1, ALU.mult, m, r1)
                r = tt(dve, rs2[:, NM:T2], x_, rs1, ALU.mult, r, *rs_use[1])
                r = cp(dve, rs2[:, 0:NM], b.ap[:, 0:NM])
                give(b, r)
                r, _ = rsqrt(rs2, rs2, 1.0 / 1024, 1e-6, r)
                r = tt(dve, rs2[:, NM:T2], rs2[:, NM:T2], rs1, ALU.mult, r)
                rs_use[0] = []
                return rs1, rs2, r
            return step, flush, finish

        def dense(X, T, kt, key, n0, nw, kp=P, xo=0, xk=0):
            b = take()
            for k in range(kt):
                wh, wl, ld = st.tile(key, k * P, kp, (n0, nw), nw)
                m = mm3(b.ap[0:nw, 0:T], (wh, wl), X.at(xo + k * T2, T, kp), k == 0, k == kt - 1, *ld,
                        *X.ready[xk + k], *(b.free if k == 0 else ()))
            return b, m

        def ffn(X, hv, T, fin, w1, w2, scale, nxt, ups=()):
            with ExitStack() as sc:
                n_ = f"f{n_stat[0]}"
                PR = Pair(sc, n_ + "_prod", MT * T2)
                tmp = v3(alloc(sc, n_ + "_tmp", 9 * T2)[:, :], 9)
                late = []
                p_use = [None] * 3
                for m in range(MT):
                    o = m % 3 * 3
                    t1, t2, t3 = (tmp[:, o + z, 0:T] for z in range(3))
                    bg, g = dense(X, T, KT, w1, m * P, P)
                    if m == 0:
                        rs, r_rs = fin()
                    elif m - 1 < len(ups):
                        ups[m - 1]()
                    i1 = tt(dve, t1, bg.ap[:, 0:T], rs, ALU.mult, g, r_rs, p_use[m % 3])
                    give(bg, i1)
                    s = af(t2, t1, ACT.Silu, i1)
                    bu, u = dense(X, T, KT, w1, DFF + m * P, P)
                    i2 = tt(dve, t1, bu.ap[:, 0:T], rs, ALU.mult, u, s)
                    give(bu, i2)
                    i3 = tt(pool, t3, t1, t2, ALU.mult, i2, s)
                    if late:
                        late.pop()()

                    low_ = PR.put_late(m, m * T2, t3, i3)

                    def low(m=m, low_=low_):
                        p_use[m % 3] = low_()
                    late.append(low)
                    x_last = u
                late.pop()()
                rs_use[(n_stat[0] - 1) % 2] = [i2]
                step, flush, fin = nxt([x_last])
                res = []
                for n in range(KT):
                    b, i = dense(PR, T, MT, w2, n * P, P)
                    r = stt(hv[:, n, :], b.ap[:, 0:T], scale, hv[:, n, :], ALU.mult, ALU.add, i)
                    give(b, r)
                    res.append(r)
                    if step is not None:
                        step(n, r)
                if step is not None:
                    flush()
            return res, [x_last], fin

        def barrier():
            ends = [q.last() for q in (pe, dve, act, pool)]
            for q in (pe, dve, act, pool):
                q.wait(*[e for e in ends if e is not None and e.q is not q])

        T = T1
        scX = ctx.enter_context(ExitStack())
        X = Pair(scX, "x1", KT * T2)
        X2 = Pair(scX, "x1b", KT * T2)
        jq = v3(alloc(scX, "jq", 3 * T2)[:, :], 3)
        gg = alloc(scX, "gg", 8)[:, :]
        sc = ctx.enter_context(ExitStack())
        csg[1] = alloc(sc, "cs1", CW[1])
        i_c1 = sp.dma(lambda e: e.dma_start(csg[1][:, :], cdram[1]), s_in[4])
        step, flush, fin = tile_squares(hx, T, dve, X, ("attn_norm", 0))
        for k in range(KT):
            step(k, i_x[k // 2], parts=(0,))
            if k == 1:
                st.part_hi(0)
            if k == 2:
                st.part_lo(0)
        flush()
        for k in range(KT):
            step(k, i_x[k // 2], parts=(1,))
        mix = v3(alloc(sc, "mix", KT * T)[:, :], KT)
        qT = v3(alloc(sc, "qT", 6 * T)[:, :], 6)
        ksT, kwT, kcT, vcT = (v3(alloc(sc, n, 512)[:, :], 2) for n in ("ksT", "kwT", "kcT", "vcT"))
        V = v4(alloc(sc, "V", 1024)[:, :], 2, 2)
        G = v3(alloc(sc, "G", 72)[:, :], 2)
        yp = v3(alloc(sc, "yp", 572)[:, :], 2)
        Xc = [v3(alloc(sc, f"Xc{j}", 1024)[:, :], 4) for j in range(2)]
        XW = alloc(sc, "XW", 960)
        XP = [Pair(sc, None, (t_[:, 0:960], t_[:, 960:1920])) for t_ in (X2.hi, X2.lo)]
        hcP = [Pair(sc, f"hc{j}", 120) for j in range(2)]
        hcs = alloc(sc, "hcs", 512)
        kcc = alloc(sc, "kcc", 60)[:, :]
        vcc = v3(alloc(sc, "vcc", 256)[0:15, :], 4)
        rsT = alloc(sc, "rsT", 2)
        acc = v3(alloc(sc, "cacc", 512)[:, :], 2)
        sqc = v3(alloc(sc, "csq", 512)[:, :], 2)
        sg = v3(alloc(sc, "csg", 512)[:, :], 2)
        tap = v3(alloc(sc, "ctap", 1024)[:, :], 4)
        mu = alloc(sc, "cmu", 256)[:, :]
        rsc = alloc(sc, "crs", 256)[:, :]
        sC = alloc(sc, "sC", 480)
        PcT = v4(alloc(sc, "PcT", 3072)[0:15, :], 2, 12)
        sR = alloc(sc, "sR", 4 * 520)
        ptR = alloc(sc, "ptR", 4 * 512)
        zy = pool.op(lambda e: e.memset(yp[:, :, 0:30], 0.0))

        def proj(dst, n0, nt, scale=1.0):
            res = []
            for i in range(nt):
                b, m = dense(X, T, KT, ("w_in", 0), n0 + i * P, P)
                r = stt(dst[:, i, :], b.ap[:, 0:T], scale, rs, ALU.mult, ALU.mult, m, r_rs)
                give(b, r)
                res.append(r)
            return res

        i_y = []
        for i in range(2):
            bv, v = dense(X, T, KT, ("w_in", 0), 256 + i * P, P)
            if i == 0:
                rs, r_rs = fin()
            s = tt(dve, sg[:, i, :], bv.ap[:, 0:T], rs, ALU.mult, v, r_rs)
            give(bv, s)
            s = af(sg[:, i, :], sg[:, i, :], ACT.Sigmoid, s)
            bu, u = dense(X, T, KT, ("w_in", 0), i * P, P)
            a = tt(dve, yp[:, i, 30:286], bu.ap[:, 0:T], rs, ALU.mult, u)
            give(bu, a)
            i_y.append(tt(dve, yp[:, i, 30:286], yp[:, i, 30:286], sg[:, i, :], ALU.mult, s, a))
        cv, tap_use = [None] * 3, [None] * 4
        NT = 20
        taps = []
        for j in range(31):
            taps += [(j, 0)] + ([(j, 2)] if j < NT else []) + ([(j + NT, 1)] if j + NT < 31 else [])

        def conv(n):
            for _ in range(n):
                if not taps:
                    break
                j, i = taps.pop(0)
                w = par("conv_w", 0, i=min(i, 1) * 31 + j)
                a_, y_ = acc[:, min(i, 1), :], yp[:, min(i, 1), j:j + 256]
                if i == 2:
                    t_ = tap[:, 3 if j == 0 else j % 3, :]
                    u = af(t_, y_, ACT.Copy, tap_use[j % 3], *i_y, zy, scale=w)
                    if j:
                        u = tap_use[j % 3] = tt(pool, tap[:, 3, :], tap[:, 3, :], t_, ALU.add, u, cv[2])
                    cv[2] = u
                elif cv[i] is None:
                    cv[i] = ts(dve, a_, y_, w, par("conv_b", 0, i=i), ALU.mult, ALU.add, zy, *i_y)
                else:
                    cv[i] = stt(a_, y_, w, a_, ALU.mult, ALU.add, cv[i])
            if not taps and cv[2] is not None:
                cv[1] = tt(dve, acc[:, 1, :], acc[:, 1, :], tap[:, 3, :], ALU.add, cv[1], cv[2])
                cv[2] = None

        r_c = []
        for j, dst in enumerate((kcT, vcT)):
            r_c.append(proj(dst, 1280 + 256 * j, 2))
            conv(6)
        r_x = []
        for j, src in enumerate((kcT, vcT)):
            ds = []
            for gp in range(2):
                for pr_ in range(2):
                    n = T - pr_
                    ds.append(act.dma(
                        lambda e, j=j, gp=gp, pr_=pr_, n=n, src=src: e.dma_start(
                            Xc[j].rearrange("p (a b) t -> p a b t", b=2)[64 * pr_:64 * pr_ + 64, :, gp, 0:n],
                            src[64 * gp:64 * gp + 64, :, pr_:pr_ + n]),
                        s_x[4 * j + 2 * gp + pr_], *r_c[j]))
            r_x.append(ds)
        b = take()
        for t in range(2):
            m = tr(b.ap[:, t * P:t * P + P], rs[:, t * P:t * P + P], P, r_rs, *b.free)
        i_rsT = cp(dve, rsT[:, 0:2], b.ap[:, 0:256:P], m)
        give(b, i_rsT)
        x2_free = []
        bc_, wt_ = {}, {}

        def cmp_1(j):
            b = take()
            for l2 in range(16):
                wh, wl, ld = st.tile(("cmp_k", "cmp_v")[j] + "_w1", l2 * P, P, (0, 256), 256)
                m = mm3(b.ap[0:60, 0:256], XP[j].at(l2 * 60, 60), (wh, wl), l2 == 0, l2 == 15, *ld,
                        *XP[j].ready[0], *(b.free if l2 == 0 else ()))
                if l2 % 4 == 3 and l2 < 15:
                    yield
            hs_ = hcs[0:60, 256 * j:256 * j + 256]
            i = af(hs_, b.ap[0:60, 0:256], ACT.Silu, m)
            give(b, i)
            bc_[j] = (hs_, i)
            x2_free.append(m)

        def cmp_2(j):
            hs_, i = bc_[j]
            b = take()
            for ht in range(2):
                m = tr(b.ap[:, ht * 60:ht * 60 + 60], hs_[:, ht * P:ht * P + P], 60, i, *b.free)
            a = af(hcP[j].hi[:, :], b.ap[:, 0:120], ACT.Copy, m)
            c_ = tt(dve, hcP[j].lo[:, :], b.ap[:, 0:120], hcP[j].hi[:, :].bitcast(F32), ALU.subtract, a)
            give(b, c_)
            bc_[j] = (a, c_)

        def cmp_3(j):
            a, c_ = bc_[j]
            b = take()
            if j == 0:
                for ht in range(2):
                    wh, wl, ld = st.tile("cmp_k_w2d", ht * P, P, (0, P), P)
                    m = mm3(b.ap[:, 0:60], (wh, wl), hcP[j].at(ht * 60, 60), ht == 0, ht == 1, *ld, a, c_, *b.free)
                r = cp(dve, kcc, b.ap[:, 0:60], m)
            else:
                wt = [st.tile("cmp_v_w2", ht * P, P, (0, 64), 64) for ht in range(2)]
                for g in range(4):
                    for ht in range(2):
                        m = mm3(b.ap[0:15, g * 64:g * 64 + 64], hcP[j].at(ht * 60 + g * 15, 15), wt[ht][0:2],
                                ht == 0, ht == 1, *wt[ht][2], a, c_, *b.free)
                r = cp(dve, vcc, v3(b.ap[0:15, 0:256], 4), m)
            give(b, r)
            return r

        c0_, c1_ = cmp_1(0), cmp_1(1)
        r_q = []
        for z in range(6):
            r_q += proj(qT[:, z:z + 1, :], 512 + z * P, 1, scale=0.125)
            conv(5)
            if z in (1, 4):
                j = int(z == 4)
                pecol = par(("cmp_k_pe", "cmp_v_pe")[j], 0, n=16)
                XW4 = XW[:, :].rearrange("p (l g n) -> p l g n", l=16, g=4)
                ws = []
                for g in range(4):
                    for hf in range(2):
                        src = Xc[j][:, g, 16 * hf:16 * hf + 240].rearrange("p (n l) -> p l n", l=16)[:, 0:16:2, :]
                        ws.append(tt(pool, XW4[:, 8 * hf:8 * hf + 8, g, :], src,
                                     pecol[:, 8 * hf:8 * hf + 8].unsqueeze(2).to_broadcast([P, 8, 15]), ALU.add,
                                     *r_x[j], i_p, *(XP[0].ready[0] if j else ())))
            if z == 3:
                XP[0].put(0, 0, XW[:, :], *ws)
            if z == 4:
                next(c0_)
        next(c0_)
        r_ks = proj(ksT, 1792, 1)
        XP[1].put(0, 0, XW[:, :], *ws)
        conv(6)
        next(c0_)
        r_ks += proj(ksT[:, 1:2, :], 1792 + P, 1)
        conv(6)
        next(c0_, None)
        r_kw = proj(kwT, 2304, 1)
        conv(99)
        cmp_2(0)
        next(c1_)
        b = take()
        for i in range(2):
            m = mm(b.ap[:, 0:T], ones, acc[:, i, :], i == 0, i == 1, cv[i], *b.free)
        i_mu = af(mu, b.ap[:, 0:T], ACT.Copy, m, scale=1.0 / 256)
        give(b, i_mu)
        r_kw += proj(kwT[:, 1:2, :], 2304 + P, 1)
        next(c1_)
        r_kc = cmp_3(0)
        b = take()
        for i in range(2):
            a = tt(dve, acc[:, i, :], acc[:, i, :], mu, ALU.subtract, i_mu)
            a = af(sqc[:, i, :], acc[:, i, :], ACT.Square, a)
            m = mm(b.ap[:, 0:T], ones, sqc[:, i, :], i == 0, i == 1, a, *b.free)
        r, rd = rsqrt(rsc, b.ap[:, 0:T], 1.0 / 256, 1e-6, m)
        give(b, rd)
        comp = {}

        def comp_a(t):
            bb = [take(), take()]
            for p in range(12):
                hf, g = p % 2, HO1[p] // 3
                m = mm(bb[hf].ap[:, p // 2 * 15:p // 2 * 15 + 15], qT[64 * hf:64 * hf + 64, p // 2, t * P:t * P + P],
                       kcc[64 * hf:64 * hf + 64, g * 15:g * 15 + 15], True, True, r_q[p // 2], r_kc,
                       *bb[hf].free)
            s4 = sC[:, t * 240:t * 240 + 180].rearrange("p (a f n) -> p a f n", a=6, f=2)
            B4 = con(1, "Bc", 360)[:, t * 180:t * 180 + 180].rearrange("p (a f n) -> p a f n", a=6, f=2)
            r = []
            for hf in range(2):
                r.append(tt(dve, s4[:, :, hf, :], v3(bb[hf].ap[:, 0:90], 6), B4[:, :, hf, :], ALU.add, m, i_c1))
                give(bb[hf], r[-1])
            s3 = v3(sC[:, t * 240:t * 240 + 180], 12)
            mx = sC[:, t * 240 + 180:t * 240 + 192]
            i = red(mx, s3, ALU.max, *r)
            i = ts(dve, mx, mx, -1e35, None, ALU.max, None, i)
            i = tt(dve, s3, s3, mx.unsqueeze(2).to_broadcast([P, 12, 15]), ALU.subtract, i)
            comp[t] = i

        def comp_e(t):
            s3 = v3(sC[:, t * 240:t * 240 + 180], 12)
            comp[t] = af(s3, s3, ACT.Exp, comp[t])

        def comp_b(t):
            s3 = v3(sC[:, t * 240:t * 240 + 180], 12)
            cf = sC[:, t * 240 + 200:t * 240 + 212]
            i = red(cf, s3, ALU.add, comp[t])
            i = ts(dve, cf, cf, 1e-30, None, ALU.max, None, i)
            i = rec(cf, cf, i)
            i = tt(dve, cf, cf, G[:, t, 0:12], ALU.mult, i, r_g[t])
            comp[t] = tt(dve, s3, s3, cf.unsqueeze(2).to_broadcast([P, 12, 15]), ALU.mult, i)

        r_pc = {}

        def comp_c(t):
            s3 = v3(sC[:, t * 240:t * 240 + 180], 12)
            for q3 in range(3):
                b = take()
                for p in range(4):
                    m = tr(b.ap[0:15, p * P:p * P + P], s3[:, q3 * 4 + p, :], P, comp[t], *b.free)
                c_ = cp(act, PcT[:, t, q3 * 4:q3 * 4 + 4, :], v3(b.ap[0:15, :], 4), m)
                give(b, c_)
            r_pc[t] = c_

        sl = slopes12()
        units = [(t, p) for t in range(2) for p in range(12)]
        s_use, pt_use = [None] * 4, [None] * 4
        stt_ = {}

        def att_s(n, before=True):
            t, p = units[n]
            hf, g, kw = p % 2, HO1[p] // 3, P * (t + 1)
            b = take()
            q_ = qT[64 * hf:64 * hf + 64, p // 2, t * P:t * P + P]
            for br, kk_ in enumerate((ksT, kwT)):
                m = mm(b.ap[:, br * kw:br * kw + kw], q_, kk_[64 * hf:64 * hf + 64, g // 2, 0:kw], True, True,
                       r_q[p // 2], r_ks[g // 2], r_kw[g // 2], *b.free)
            o = n % 4 * 520
            s = v3(sR[:, o:o + 2 * kw], 2)
            D_ = con(1, "D", 512)[:, t * 256:t * 256 + kw].unsqueeze(1).to_broadcast([P, 2, kw])
            a = stt(s, D_, -float(sl[HO1[p]]), v3(b.ap[:, 0:2 * kw], 2), ALU.mult, ALU.add, m, i_c1, s_use[n % 4])
            give(b, a)
            mx, sm = sR[:, o + 512:o + 514], sR[:, o + 514:o + 516]
            p = att_p(n - 1) if before else None
            i = red(mx, s, ALU.max, a, negate=True)
            if p:
                p()
            for br in range(2):
                e_ = af(s[:, br, :], s[:, br, :], ACT.Exp, i, bias=mx[:, br:br + 1], acc=sm[:, br:br + 1])
            stt_[n] = (s, sm, e_)

        def att_p(n):
            t, p = units[n]
            s, sm, e_ = stt_[n]
            kw = P * (t + 1)
            i0 = ts(dve, sm, sm, 1e-30, None, ALU.max, None, e_)

            def more():
                i = rec(sm, sm, i0)
                i = tt(dve, sm, sm, G[:, t, 12 + p:36:12], ALU.mult, i, r_g[t])
                i = tt(pool, s, s, sm.unsqueeze(2).to_broadcast([P, 2, kw]), ALU.mult, i)
                stt_[n] = (s, i)
            return more

        def att_t(n):
            t, p = units[n]
            s, i = stt_[n]
            b = take()
            for br in range(2):
                for kc in range(t + 1):
                    m = tr(b.ap[:, (br * (t + 1) + kc) * P:][:, 0:P], s[:, br, kc * P:kc * P + P], P, i, *b.free)
            s_use[n % 4] = m
            n_ = 2 * (t + 1) * P
            pt = ptR[:, n % 4 * 512:n % 4 * 512 + n_]
            c_ = cp(act, pt, b.ap[:, 0:n_], m, pt_use[n % 4])
            give(b, c_)
            stt_[n] = (pt, c_)

        def att_v(n):
            t, p = units[n]
            b = take()
            o = [b.ap[64 * hf:64 * hf + 64, 0:P] for hf in range(2)]
            w = (r_vc, r_pc[t], stt_[n][1], stt_[n + 1][1], *r_v, *b.free)
            g = [HO1[p + hf] // 3 for hf in range(2)]
            for hf in range(2):
                mm(o[hf], vcc[:, g[hf], :], PcT[:, t, p + hf, :], True, False, *w)
            for br in range(2):
                for kc in range(t + 1):
                    for hf in range(2):
                        m = mm(o[hf], V[:, kc, br, g[hf] * 64:g[hf] * 64 + 64],
                               stt_[n + hf][0][:, (br * (t + 1) + kc) * P:][:, 0:P], False, br == 1 and kc == t)
            pt_use[n % 4] = pt_use[(n + 1) % 4] = m
            r = cp(act, mix[:, 2 + p // 2, t * P:t * P + P], b.ap[:, 0:P], m)
            give(b, r)
            if t == 1:
                X.put(2 + p // 2, (2 + p // 2) * T2, mix[:, 2 + p // 2, :], r, x_last)

        next(c1_)
        comp_a(0)
        comp_a(1)
        next(c1_, None)
        a_ = [None] * 2
        for i in range(2):
            a = stt(acc[:, i, :], acc[:, i, :], par("conv_ln_g", 0, i=i), rsc, ALU.mult, ALU.mult, r)
            a_[i] = af(mix[:, i, :], acc[:, i, :], ACT.Silu, a, bias=par("conv_ln_b", 0, i=i))
        comp_e(0)
        comp_e(1)
        att_s(0, False)
        att_s(1, False)
        cmp_2(1)
        bs = [[take(), take()] for _ in range(2)]
        for k in range(KT):
            xh, xl = X.at(k * T2, T)
            for z, (o, w) in enumerate(((0, 292), (292, 256))):
                wh, wl, ld = st.tile("w_vg", k * P, P, (o, w), w)
                for t in range(2):
                    vl = mm3(bs[t][z].ap[:, 0:w], (xh[:, t * P:t * P + P], xl[:, t * P:t * P + P]), (wh, wl), k == 0,
                             k == KT - 1, *ld, *(bs[t][z].free if k == 0 else ()))
        r_v, r_g = [], []
        for t in range(2):
            r_g.append(af(G[:, t, :], bs[t][0].ap[:, 256:292], ACT.Sigmoid, vl, i_rsT, scale=rsT[:, t:t + 1]))
        for t in range(2):
            col = rsT[:, t:t + 1]
            a = af(V[:, t, 0, :], bs[t][0].ap[:, 0:256], ACT.Copy, scale=col)
            c_ = ts(dve, V[:, t, 1, :], bs[t][1].ap[:, 0:256], col, None, ALU.mult, None, vl)
            give(bs[t][0], a)
            give(bs[t][1], c_)
            r_v += [a, c_]
        x_last = vl
        r_vc = cmp_3(1)
        att_p(0)()
        comp_b(0)
        for n in range(2, len(units) + 5):
            if n == 4:
                comp_c(0)
                comp_b(1)
                for i in range(2):
                    X.put(i, i * T2, mix[:, i, :], a_[i], x_last)
            if n == 6:
                comp_c(1)
            if n < len(units):
                att_s(n)
            elif n == len(units):
                att_p(n - 1)()
            if n >= 3 and n - 3 < len(units):
                att_t(n - 3)
            if n >= 5 and n % 2:
                att_v(n - 5)
        nrm = tile_squares(hx, T, pool, X2, ("ffn_norm", 0), x2_free)
        for n in range(KT):
            b, m = dense(X, T, KT, "w_out_p", n * P, P)
            r = tt(dve, hx[:, n, :], b.ap[:, 0:T], hx[:, n, :], ALU.add, m)
            give(b, r)
            nrm[0](n, r)
        nrm[1]()
        sc.close()
        rh, xf, fin = ffn(X2, hx, T, nrm[2], ("w_gate_up", 0), ("w_down", 0), 1.0,
                          lambda xf: joint_squares(X, [m, *xf]))

        T = T2
        joint = []

        def both():
            rs1, rs2, r = fin_j()
            joint.extend((rs1, r))
            return rs2, r

        def rescale(k):
            rh[k] = stt(hx[:, k, :], hx[:, k, :], par("final_norm", i=k), joint[0], ALU.mult, ALU.mult, joint[1])
            rs_use[0] = [rh[k]]

        fin_j = fin
        rh, xf, fin = ffn(X, h, T, both, ("ffn_w_in_2", 0, 0), ("ffn_w_out_2", 0, 0), 0.5,
                          lambda xf: tile_squares(h, T2, pool), ups=[lambda k=k: rescale(k) for k in range(KT)])
        rs, r_rs = fin()
        scX.close()
        sB = ctx.enter_context(ExitStack())
        barrier()
        sE = ctx.enter_context(ExitStack())
        csg[2] = alloc(sB, "cs2", CW[2])
        i_c2 = act.dma(lambda e: e.dma_start(csg[2][:, :], cdram[2]), s_in[5])
        hn_ = alloc(sB, "hn", KT * (T2 + 1))
        hn = v3(hn_[:, :], KT)
        aT, rT, vT = (v3(alloc(sB, n, KT * T2)[:, :], KT) for n in ("aT", "rT", "vT"))
        kkT, kT = (v3(alloc(sE, n, KT * T2, side="right")[:, :], KT) for n in ("kkT", "kT"))
        Lc = alloc(sB, "Lc", KT * (T2 + NC))[:, :].rearrange("p (k t) -> p k t", k=KT)
        ms = alloc(sB, "rkms", 3 * T2 + 560)
        s16, s16b = ms[0:16, 0:T2], ms[0:16, T2:2 * T2]
        ka1 = ms[:, 3 * T2 + 544:3 * T2 + 552]
        gl = ms[:, 2 * T2:4 * T2]
        LO = [c0 + i for i, c0 in enumerate(C0)]

        def Lcol(k, c, off, n):
            return Lc[:, k, LO[c] + off:LO[c] + off + n]

        xn = hn[:, :, 1:1 + T]
        z0 = pool.op(lambda e: e.memset(hn[:, :, 0:1], 0.0))
        rn = [stt(xn[:, k, :], h[:, k, :], par("norm_g_2", 0, 1, i=k), rs, ALU.mult, ALU.mult, r_rs, rh[k])
              for k in range(KT)]
        rs_use[(n_stat[0] - 1) % 2] = [rn[-1]]
        sP = ctx.enter_context(ExitStack())
        xx = v3(alloc(sP, "xx", KT * T2)[:, :], KT)
        sw = v3(alloc(sP, "sw", KT * T2)[:, :], KT)
        xr = v3(alloc(sP, "xraw", 3 * T2)[:, :], 3)
        XS = [Pair(sP, f"xs{i}", KT * T2) for i in range(2)]
        LP = Pair(sP, "lora", 2 * T2)
        lo_ = alloc(sP, "loraf", 2 * T2)
        i_xx = [tt(pool, xx[:, k, :], hn[:, k, 0:T], xn[:, k, :], ALU.subtract, z0, rn[k]) for k in range(KT)]
        x_use = [[], []]
        n_x = [0]
        xr_use = [None] * 3

        def mixing(j):
            n = n_x[0] % 2
            n_x[0] += 1
            late = None
            for k in range(KT):
                s = (n_x[0] * KT + k) % 3
                i = stt(xr[:, s, :], xx[:, k, :], par("rk_mix_2", 0, j, i=k), xn[:, k, :], ALU.mult, ALU.add,
                        i_xx[k], xr_use[s])
                low = XS[n].put_late(k, k * T2, xr[:, s, :], i, after=x_use[n], q=pool if k % 2 else dve)
                if late is not None:
                    xr_use[late[0]] = late[1]()
                late = (s, low)
                if k == KT - 1:
                    xr_use[s] = low()
                yield n

        def mixed(j):
            for n in mixing(j):
                pass
            return n

        def both_of(a, b):
            for _ in a:
                next(b, None)
                yield
            yield from b

        def full(dst, key, n, evac, between=None, out_=None):
            out_ = [] if out_ is None else out_
            for i in range(KT):
                b, m = dense(XS[n], T, KT, key, i * P, P)
                r = evac(i, b, m)
                give(b, r)
                out_.append(r)
                if between is not None:
                    next(between, None)
            x_use[n] = [m]
            return out_

        def plain(dst):
            return lambda i, b, m: cp(act, dst[:, i, :], b.ap[:, 0:T], m)

        zL = [pool.op(lambda e, c=c: e.memset(Lc[:, :, LO[c]:LO[c] + 1], 0.0)) for c in range(NC)]
        kr = v3(alloc(sP, "kr", 3 * T2)[:, :], 3)
        kr2 = v3(alloc(sP, "kr2", 2 * T2)[:, :], 2)
        e_i, e_c, r_k = [], [], []
        def head_sums(src, ready):
            b = take()
            for k in range(KT):
                m = mm(b.ap[0:16, 0:T], EH[:, k, :], src(k), k == 0, k == KT - 1, ready[k], *b.free)
            return b, m

        def spread(src16, k, *ready):
            b = take()
            m = mm(b.ap[:, 0:T], ETH[:, k, :], src16, True, True, *ready, *b.free)
            return b, m

        i_ka = ts(dve, ka1, par("rk_k_a_2", 0, n=8), -1.0, 1.0, ALU.mult, ALU.add)

        def by_chunk(x, k, off=None):
            if off is None:
                return v3(x[:, k, 0:2 * C], 2), x[:, k, 2 * C:T2]
            return v3(x[:, k, 0:2 * C + 2], 2)[:, :, off:off + C], Lcol(k, 2, off, CS[2])

        norm = {}

        def keys(r_k):
            b = take()
            use = [None] * 2
            m = None
            for k in range(KT):
                z = k % 2
                i = af(kkT[:, k, :], kT[:, k, :], ACT.Copy, r_k[k], scale=par("rk_k_k_2", 0, i=k))
                i = tt(dve, kr[:, z, :], kkT[:, k, :], kkT[:, k, :], ALU.mult, i, use[z])
                yield
                use[z] = m = mm(b.ap[0:16, 0:T], EH[:, k, :], kr[:, z, :], k == 0, k == KT - 1, i, *b.free)
            i = ts(dve, s16, b.ap[0:16, 0:T], 1e-24, None, ALU.max, None, m)
            give(b, i)
            norm["sqrt"] = af(s16, s16, ACT.Sqrt, i)
            norm["use"] = use

        def exps():
            for k in range(KT):
                for o, i in zip(by_chunk(sw, k), by_chunk(Lc, k, 1)):
                    a = af(o, i, ACT.Exp, r_L[k], scale=KAPPA)
                e_i.append(a)
                e_c.append(af(Lc[:, k, :], Lc[:, k, :], ACT.Exp, a, scale=-KAPPA))
                yield

        r_kp, r_B = [], []

        def factors():
            i16 = rec(s16, s16, norm["sqrt"])
            use = [*norm["use"], None]
            ex = exps()
            for k in range(KT):
                b, m = spread(s16, k, i16)
                n_ = tt(dve, kkT[:, k, :], kkT[:, k, :], b.ap[:, 0:T], ALU.mult, m)
                give(b, n_)
                z = k % 3
                i = ts(pool, kr[:, z, :], aT[:, k, :], par("rk_k_a_2", 0, i=k), ka1[:, k:k + 1], ALU.mult, ALU.add,
                       i_a[k], i_ka, use[z])
                i = use[z] = tt(dve, kT[:, k, :], kT[:, k, :], kr[:, z, :], ALU.mult, i)
                r_kp.append(i)
                r_B.append(tt(pool, aT[:, k, :], aT[:, k, :], kkT[:, k, :], ALU.mult, i))
                next(ex)
                yield

        def final(r_r):
            b16 = take()
            use2 = [None] * 2
            for k in range(KT):
                tt(pool, aT[:, k, :], aT[:, k, :], sw[:, k, :], ALU.mult, r_B[k], e_i[k])
                z = k % 2
                i = stt(kr2[:, z, :], rT[:, k, :], par("rk_r_k_2", 0, i=k), kT[:, k, :], ALU.mult, ALU.mult,
                        r_kp[k], r_r[k], use2[z])
                tt(pool, kT[:, k, :], kT[:, k, :], sw[:, k, :], ALU.mult, i)
                for o, l in zip(by_chunk(rT, k), by_chunk(Lc, k, 1)):
                    tt(dve, o, o, l, ALU.mult, e_c[k], i)
                for o, l in zip(by_chunk(kkT, k), by_chunk(Lc, k, 0)):
                    stt(o, o, -1.0, l, ALU.mult, ALU.mult, r_B[k])
                yield
                use2[z] = m = mm(b16.ap[0:16, 0:T], EH[:, k, :], kr2[:, z, :], k == 0, k == KT - 1, i, *b16.free)
            give(b16, cp(dve, s16b, b16.ap[0:16, 0:T], m))

        n1 = mixed(2)
        n2 = mixed(1)
        ck = keys(r_k)
        full(kT, ("rk_w_k_2", 0), n1, plain(kT), ck, r_k)
        n1 = mixed(4)
        b, m = dense(XS[n2], T, KT, ("rk_w1_2", 0), 0, 64)
        x_use[n2] = [m]
        i = af(lo_[0:64, 0:T], b.ap[0:64, 0:T], ACT.Tanh, m)
        give(b, i)
        LP.put(0, 0, lo_[0:64, 0:T], i, rows=64)
        n2 = mixed(0)
        b, m = dense(XS[n1], T, KT, ("rk_a1_2", 0), 0, 64)
        x_use[n1] = [m]
        i = cp(act, lo_[0:64, T:2 * T], b.ap[0:64, 0:T], m)
        give(b, i)
        LP.put(1, T2, lo_[0:64, T:2 * T], i, rows=64)
        i_s = []
        for k in range(KT):
            b, m = dense(LP, T, 1, ("rk_w2_2", 0), k * P, P, kp=64)
            s = af(sw[:, k, :], b.ap[:, 0:T], ACT.Sigmoid, m, bias=par("rk_w0_2", 0, i=k))
            give(b, s)
            i_s.append(s)
        i_a = []
        for k in range(KT):
            b, m = dense(LP, T, 1, ("rk_a2_2", 0), k * P, P, kp=64, xo=T2, xk=1)
            s = af(aT[:, k, :], b.ap[:, 0:T], ACT.Sigmoid, m, bias=par("rk_a0_2", 0, i=k))
            give(b, s)
            i_a.append(s)
        r_L = []
        for k in range(KT):
            for c in range(NC):
                n = CS[c]
                l = dve.op(lambda e, k=k, c=c, n=n: e.tensor_tensor_scan(
                    Lcol(k, c, 1, n), ones[:, 0:n], sw[:, k, C0[c]:C0[c] + n], 0.0, ALU.mult, ALU.add), i_s[k], *zL)
            r_L.append(l)

        n1 = 1 - n2
        for _ in ck:
            pass
        r_r = full(rT, ("rk_w_r_2", 0), n2, plain(rT), both_of(mixing(3), factors()))
        chain = both_of(final(r_r), mixing(5))
        r_v = full(vT, ("rk_w_v_2", 0), n1, plain(vT), chain)
        for _ in chain:
            pass
        b, m0 = dense(XS[n2], T, KT, ("rk_g1_2", 0), 0, P)
        b2, m = dense(XS[n2], T, KT, ("rk_g1_2", 0), P, 32)
        g0 = af(gl[:, 0:T], b.ap[:, 0:T], ACT.Sigmoid, m0)
        g1 = af(gl[0:32, T:2 * T], b2.ap[0:32, 0:T], ACT.Sigmoid, m)
        give(b, g0)
        give(b2, g1)
        sP.close()
        sK = ctx.enter_context(ExitStack())
        barrier()
        Dm, DT, Xb, LT = (v3(alloc(sK, n, 16 * C)[0:C, :], 16) for n in ("Dm", "DT", "Xb", "LT"))
        BR, KR = (v4(alloc(sK, n, 32 * C)[0:C, :], 16, 2) for n in ("BR", "KR"))
        toks = [alloc(sK, n, 1024) for n in ("tokA", "tokB", "tokK", "tokV")]
        tk = [v4(a[:, :], 8, 2) for a in toks]
        AkV = v3(hn_[:, 0:1024], 16)
        W2 = v3(hn_[:, 1024:2048], 16)
        W1T = v3(alloc(sK, "W1T", 8 * C)[:, :], 8)
        U = Xb.rearrange("p a b -> p (a b)")[:, 0:1024].rearrange("p (a b) -> p a b", a=16)
        M = v3(alloc(sK, "Mst", 1024)[:, :], 8)
        lv = (2, 4, 8, 16, 32, 64)
        i_M = [pool.op(lambda e: e.memset(M[:, :, :], 0.0))]
        r_y = [None] * NC

        def chunk(c, i_M, prev):
            t0, n = C0[c], CS[c]

            def bc(ap, w):
                return ap[0:n].unsqueeze(1).to_broadcast([n, w, ap.shape[-1]])

            def msk(name, rows=None):
                return con(2, name, n, n)

            mst = con(2, "mst", 2 * C, n).rearrange("p (a t) -> p a t", a=2)[:, :, 0:n]
            w_prev = list(prev)
            if n < C:
                w_prev += [pool.op(lambda e, a=a: e.memset(a[64:C, :, :], 0.0), *prev) for a in (Dm, DT)]
            r_b, r_kr, rT_, rD, rL, lt_use = {}, {}, {}, {}, {}, {}

            def gram(quad, src, dst, res):
                hf, k0 = quad // 2, (quad % 2) * 4
                rows = slice(64 * hf, 64 * hf + 64)
                res[quad] = []
                for pair in range(2):
                    b = take()
                    for k in range(2):
                        kk_ = k0 + 2 * pair + k
                        for z, rr in enumerate((kkT, rT)):
                            m = mm(b.ap[0:n, (2 * k + z) * n:(2 * k + z) * n + n], src[rows, kk_, t0:t0 + n],
                                   rr[rows, kk_, t0:t0 + n], True, True, *b.free)
                    h0 = quad * 4 + pair * 2
                    for k in range(2):
                        r = tt(dve, dst[0:n, h0 + k, :, 0:n], v3(b.ap[0:n, 2 * k * n:2 * k * n + 2 * n], 2), mst,
                               ALU.mult, m, i_c2, *w_prev)
                    give(b, r)
                    res[quad].append(r)

            def masks(li, quad):
                hs = slice(quad * 4, quad * 4 + 4)
                rL[quad] = tt(pool, LT[0:n, hs, 0:n], BR[0:n, hs, 0, 0:n], bc(msk(f"l{lv[li]}"), 4), ALU.mult,
                              *r_b[quad], lt_use.get(quad), *w_prev)

            def turn(quad):
                b = take()
                for k in range(4):
                    m = tr(b.ap[0:n, k * n:k * n + n], DT[0:n, quad * 4 + k, 0:n], n, rT_[quad], *b.free)
                rD[quad] = cp(act, Dm[0:n, quad * 4:quad * 4 + 4, 0:n], v3(b.ap[0:n, 0:4 * n], 4), m, *w_prev)
                give(b, rD[quad])

            for quad in range(4):
                gram(quad, aT, BR, r_b)
                hs = slice(quad * 4, quad * 4 + 4)
                q = dve if quad % 2 else pool
                i = tt(q, DT[0:n, hs, 0:n], BR[0:n, hs, 0, 0:n], bc(msk("l1"), 4), ALU.mult, *r_b[quad], *w_prev)
                rT_[quad] = tt(q, DT[0:n, hs, 0:n], DT[0:n, hs, 0:n], bc(ident[0:n, 0:n], 4), ALU.add, i)
                masks(0, quad)
            r_t = []
            for n_, src in enumerate((kkT, aT, kT, vT)):
                for hb in range(2):
                    b = take()
                    for k in range(4):
                        m = tr(b.ap[0:n, k * P:k * P + P], src[:, hb * 4 + k, t0:t0 + n], P, *b.free)
                    r = cp(act, toks[n_][0:n, hb * 512:hb * 512 + 512], b.ap[0:n, :], m, *w_prev)
                    give(b, r)
                    r_t.append(r)
            for quad in range(4):
                gram(quad, kT, KR, r_kr)
                if quad:
                    turn(quad - 1)
            turn(3)
            use = {}

            for li in range(6):
                rX = {}
                for quad in range(4):
                    b = take()
                    for k in range(4):
                        hh = quad * 4 + k
                        m = mm(b.ap[0:n, k * n:k * n + n], LT[0:C, hh, 0:n], Dm[0:C, hh, 0:n], True, True,
                               rL[quad], rD[quad], *b.free)
                    lt_use[quad] = m
                    rX[quad] = cp(act, Xb[0:n, quad * 4:quad * 4 + 4, 0:n], v3(b.ap[0:n, 0:4 * n], 4), m,
                                  use.get(quad), *w_prev)
                    give(b, rX[quad])
                    if li + 1 < 6:
                        masks(li + 1, quad)
                for quad in range(4):
                    hs = slice(quad * 4, quad * 4 + 4)
                    b2 = take()
                    for k in range(4):
                        hh = quad * 4 + k
                        m2 = mm(b2.ap[0:n, k * n:k * n + n], Xb[0:C, hh, 0:n], DT[0:C, hh, 0:n], True, True,
                                rX[quad], rT_[quad], *b2.free)
                    use[quad] = m2
                    rT_[quad] = tt(dve, DT[0:n, hs, 0:n], v3(b2.ap[0:n, 0:4 * n], 4), DT[0:n, hs, 0:n], ALU.add, m2)
                    give(b2, rT_[quad])
                    if li < 5 and quad >= 2:
                        turn(quad - 2)
                if li < 5:
                    turn(2)
                    turn(3)
            r1, rk_, r2_ = [], {}, {}
            for quad in range(4):
                hf, k0 = quad // 2, (quad % 2) * 4
                b = take()
                for k in range(4):
                    m = mm(b.ap[0:n, k * 64:k * 64 + 64], KR[0:n, quad * 4 + k, 0, 0:n], tk[3][0:n, k0 + k, hf, :],
                           True, True, *r_kr[quad], *r_t, *b.free)
                r = cp(act, AkV[0:n, quad * 4:quad * 4 + 4, :], v3(b.ap[0:n, 0:256], 4), m, *w_prev)
                give(b, r)
                rk_[quad] = r
            for kb in range(2):
                b = take()
                for k in range(kb * 4, kb * 4 + 4):
                    for hf in range(2):
                        m = mm(b.ap[64 * hf:64 * hf + 64, (k % 4) * n:(k % 4) * n + n], tk[0][0:n, k, hf, :],
                               DT[0:n, hf * 8 + k, 0:n], True, True, rT_[2 * hf + kb], *b.free)
                r = cp(act, W1T[:, kb * 4:kb * 4 + 4, 0:n], v3(b.ap[:, 0:4 * n], 4), m, *w_prev)
                give(b, r)
                r1.append(r)
            ys = [take() for _ in range(2)]

            def y_at(k, hf):
                return ys[k // 4].ap[64 * hf:64 * hf + 64, (k % 4) * n:(k % 4) * n + n]

            for k in range(8):
                for hf in range(2):
                    mm(y_at(k, hf), tk[3][0:n, k, hf, :], KR[0:n, hf * 8 + k, 1, 0:n], k % 4 == 0, False, *ys[k // 4].free)
            for quad in range(4):
                b = take()
                for k in range(4):
                    m = mm(b.ap[0:n, k * 64:k * 64 + 64], DT[0:n, quad * 4 + k, 0:n], AkV[0:n, quad * 4 + k, :],
                           True, True, rk_[quad], *b.free)
                r2_[quad] = cp(act, W2[0:n, quad * 4:quad * 4 + 4, :], v3(b.ap[0:n, 0:256], 4), m, *w_prev)
                give(b, r2_[quad])
            if c + 1 < NC:
                ms_ = take()
                for k in range(8):
                    for hf in range(2):
                        mm(ms_.ap[64 * hf:64 * hf + 64, k * 64:k * 64 + 64], tk[2][0:n, k, hf, :],
                           tk[3][0:n, k, hf, :], k == 0, False, *ms_.free)
            rU = []
            for kb in range(2):
                b = take()
                for k in range(4):
                    m = mm(b.ap[0:n, k * P:k * P + P], W1T[:, kb * 4 + k, 0:n], M[:, kb * 4 + k, :], True, True,
                           r1[kb], *i_M, *b.free)
                for hf in range(2):
                    h0 = hf * 8 + kb * 4
                    r = tt(dve, U[0:n, h0:h0 + 4, :], v3(b.ap[0:n, :], 4)[:, :, 64 * hf:64 * hf + 64],
                           W2[0:n, h0:h0 + 4, :], ALU.add, m, r2_[2 * hf + kb], *w_prev)
                give(b, r)
                rU.append(r)
            for k in range(8):
                mm(ys[k // 4].ap[:, (k % 4) * n:(k % 4) * n + n], M[:, k, :], rT[:, k, t0:t0 + n], False, False)
            if c + 1 < NC:
                for k in range(8):
                    for hf in range(2):
                        m = mm(ms_.ap[64 * hf:64 * hf + 64, k * 64:k * 64 + 64], tk[1][0:n, k, hf, :],
                               U[0:n, hf * 8 + k, :], False, k == 7, rU[k // 4])
                new = []
                for hf in range(2):
                    Mh = M[64 * hf:64 * hf + 64, :, 64 * hf:64 * hf + 64]
                    i = tt(dve, Mh, v3(ms_.ap[64 * hf:64 * hf + 64, :], 8), Mh, ALU.add, m, *i_M)
                    new.append(tt(dve, Mh, Mh, Lc[64 * hf:64 * hf + 64, :, LO[c] + n:LO[c] + n + 1].to_broadcast(
                        [64, 8, 64]), ALU.mult, i))
                give(ms_, i)
                i_M = new
            ry = []
            for kb in range(2):
                for k in range(kb * 4, kb * 4 + 4):
                    for hf in range(2):
                        m = mm(y_at(k, hf), U[0:n, hf * 8 + k, :], BR[0:n, hf * 8 + k, 1, 0:n], False, k % 4 == 3, *rU)
                r = cp(act, rT[:, kb * 4:kb * 4 + 4, t0:t0 + n], v3(ys[kb].ap[:, 0:4 * n], 4), m)
                give(ys[kb], r)
                ry.append(r)
            return i_M, [pe.last()], ry[-1]

        prev = []
        for c in range(NC):
            i_M, prev, r_y[c] = chunk(c, i_M, prev)
        sK.close()
        sQ = ctx.enter_context(ExitStack())
        barrier()
        YP = Pair(sQ, "yp2", KT * T2)
        GP = Pair(sQ, "gp", 2 * T2)
        y, sq = rT, v3(alloc(sQ, "ysq", KT * T2)[:, :], KT)
        bonT = v3(alloc(sQ, "bon", 2 * T2)[:, :], 2)
        s16c = alloc(sQ, "s16c", T2)[0:16, :]
        GP.put(0, 0, gl[:, 0:T], g1)
        GP.put(1, T2, gl[0:32, T:2 * T], rows=32)
        b, m = head_sums(lambda k: y[:, k, :], [r_y[NC - 1]] * KT)
        i16 = ts(dve, s16, b.ap[0:16, 0:T], 1.0 / 64, None, ALU.mult, None, m)
        give(b, i16)
        r_s = []
        for k in range(KT):
            b, m = spread(s16, k, i16)
            i = tt(dve, y[:, k, :], y[:, k, :], b.ap[:, 0:T], ALU.subtract, m)
            give(b, i)
            r_s.append(af(sq[:, k, :], y[:, k, :], ACT.Square, i))
        i_g = []
        for k in range(KT):
            b = take()
            wh, wl, ld = st.tile(("rk_g2_2", 0), 0, P, (k * P, P), P)
            mm3(b.ap[:, 0:T], (wh, wl), GP.at(0, T), True, False, *ld, *GP.ready[0], *GP.ready[1], *b.free)
            wh, wl, ld = st.tile(("rk_g2_2", 0), P, 32, (k * P, P), P)
            m = mm3(b.ap[:, 0:T], (wh, wl), GP.at(T2, T, 32), False, True, *ld)
            s = cp(act, aT[:, k, :], b.ap[:, 0:T], m)
            give(b, s)
            i_g.append(s)
        b, m = head_sums(lambda k: sq[:, k, :], r_s)
        i16, rd = rsqrt(s16c, b.ap[0:16, 0:T], 1.0 / 64, 64e-5, m)
        give(b, rd)
        bu_ = [None, None]
        i_b = []
        for k in range(KT):
            b, m = spread(s16b, k)
            i = tt(dve, kT[:, k, :], vT[:, k, :], b.ap[:, 0:T], ALU.mult, m)
            give(b, i)
            i_b.append(i)
        late = []
        for k in range(KT):
            b, m = spread(s16c, k, i16)
            i = stt(y[:, k, :], y[:, k, :], par("rk_lnx_g_2", 0, i=k), b.ap[:, 0:T], ALU.mult, ALU.mult, m)
            give(b, i)
            i = stt(y[:, k, :], y[:, k, :], par("rk_lnx_b_2", 0, i=k), kT[:, k, :], ALU.add, ALU.add, i, i_b[k])
            i = tt(pool, y[:, k, :], y[:, k, :], aT[:, k, :], ALU.mult, i, i_g[k])
            late.append(YP.put_late(k, k * T2, y[:, k, :], i))
            if k >= 2:
                late.pop(0)()
        for low in late:
            low()
        sE.close()
        X = Pair(ctx, "x2", KT * T2, "right")
        nrm = tile_squares(h, T, pool, X, ("norm_g_2", 0, 2))
        for n in range(KT):
            b, m = dense(YP, T, KT, ("rk_w_o_2", 0), n * P, P)
            r = tt(dve, h[:, n, :], b.ap[:, 0:T], h[:, n, :], ALU.add, m)
            give(b, r)
            nrm[0](n, r)
        nrm[1]()
        sQ.close()
        sB.close()
        rh, xf, fin = ffn(X, h, T, nrm[2], ("ffn_w_in_2", 0, 1), ("ffn_w_out_2", 0, 1), 0.5,
                          lambda xf: tile_squares(h, T2, pool, X, ("norm_g_2", 1, 0), xf))

        rh, xf, fin = ffn(X, h, T, fin, ("ffn_w_in_2", 1, 0), ("ffn_w_out_2", 1, 0), 0.5,
                          lambda xf: tile_squares(h, T2, pool, X, ("norm_g_2", 1, 1), xf))
        sD = ctx.enter_context(ExitStack())
        csg[3] = alloc(sD, "cs3", CW[3])
        Q = v3(alloc(sD, "Q", KT * T2)[:, :], KT)
        KK = v3(alloc(sD, "KK", 2 * T2)[:, :], 2)
        QI = v3(alloc(sD, "QI", 4 * T2)[:, :], 4)
        KI = v3(alloc(sD, "KI", T2)[:, :], 1)
        Vt = v3(alloc(sD, "Vt", NC * 264)[:, :], NC)
        rsT = alloc(sD, "rsT2", NC)
        oT = v3(alloc(sD, "oT", KT * T2)[:, :], KT)
        tmp = v3(alloc(sD, "rtmp", 4 * T2)[:, :], 4)
        sqr = v3(alloc(sD, "sqr", 3 * T2)[:, :], 3)
        f16 = alloc(sD, "f16", 2 * T2)
        s16q = alloc(sD, "s16q", T2)
        bias = v3(alloc(sD, "bias", NC * T2)[:, :], NC)
        sR2 = alloc(sD, "sR2", 3 * (4 * T2 + 16))
        pt2 = alloc(sD, "pt2", 4 * NC * 4 * C)
        scr = v3(alloc(sD, "scr", NC * T2)[:, :], NC)
        wk = v3(alloc(sD, "wk", NC * T2)[:, :], NC)
        rel = v3(alloc(sD, "rel", 4 * T2)[:, :], 4)
        t8 = alloc(sD, "t8", 32)
        sE = ctx.enter_context(ExitStack())
        eqb, gtb, csb = (v3(alloc(sE, n, NC * T2, side="right")[:, :], NC) for n in ("eqb", "gtb", "csb"))
        barrier_tok = [q.last() for q in (pe, dve, act, pool)]
        i_c3 = sp.dma(lambda e: e.dma_start(csg[3][:, :], cdram[3]), s_in[6], *barrier_tok)
        cosF, sinF = con(3, "cos", T2), con(3, "sin", T2)
        st_ = {}
        r_ki = []
        for n in range(5):
            dst = KI[:, 0, :] if n == 0 else QI[:, n - 1, :]
            b, m = dense(X, T, KT, "at_i", n * P, P)
            if n == 0:
                rs, r_rs = fin()
            r = tt(dve, dst, b.ap[:, 0:T], rs, ALU.mult, m, r_rs)
            give(b, r)
            st_[n] = r
        b = take()
        for c in range(NC):
            m = tr(b.ap[0:CS[c], c * P:c * P + P], rs[:, C0[c]:C0[c] + CS[c]], P, r_rs, *b.free)
        for c in range(NC):
            i_rsT = cp(dve, rsT[0:CS[c], c:c + 1], b.ap[0:CS[c], c * P:c * P + 1], m)
        give(b, i_rsT)
        bs = [take() for _ in range(NC)]
        for k in range(KT):
            wh, wl, ld = st.tile("at_vw", k * P, P, (0, 264), 264)
            xh, xl = X.at(k * T2, T)
            for c in range(NC):
                s_, n = C0[c], CS[c]
                vl = mm3(bs[c].ap[0:n, 0:264], (xh[:, s_:s_ + n], xl[:, s_:s_ + n]), (wh, wl), k == 0, k == KT - 1,
                         *ld, *(bs[c].free if k == 0 else ()))
        r_v = []
        for c in range(NC):
            n = CS[c]
            a = af(Vt[0:n, c, :], bs[c].ap[0:n, 0:264], ACT.Copy, vl, i_rsT, scale=rsT[0:n, c:c + 1])
            give(bs[c], a)
            r_v.append(ts(dve, Vt[0:n, c, 256:264], Vt[0:n, c, 256:264], float(8 ** -0.5 * 64 ** -0.5), None, ALU.mult,
                          None, a))
        rt_use = [None] * 4

        def rope(dst, n, r):
            b = take()
            m = mm(b.ap[:, 0:T], con(3, "RT", P), dst, True, True, r, i_c3, *b.free)
            t_ = tmp[:, n % 4, :]
            i = tt(dve, t_, b.ap[:, 0:T], sinF, ALU.mult, m, rt_use[n % 4])
            give(b, i)
            i2 = tt(pool, dst, dst, cosF, ALU.mult, m)
            i = tt(pool, dst, dst, t_, ALU.add, i, i2)
            rt_use[n % 4] = i
            return i

        for n in range(5):
            st_[n] = rope(KI[:, 0, :] if n == 0 else QI[:, n - 1, :], n, st_[n])
        jobs = [(KK[:, i, :], "at_k_g_2") for i in range(2)] + [(Q[:, i, :], "at_q_g_2") for i in range(8)]
        sq_free = [None] * 3
        zk = {}
        hb = {}

        def qk_dense(n):
            dst, g = jobs[n]
            b, m = dense(X, T, KT, "at_qk", n * P, P)
            r = cp(act, dst, b.ap[:, 0:T], m)
            give(b, r)
            s_ = sqr[:, n % 3, :]
            a = af(s_, dst, ACT.Square, r, sq_free[n % 3])
            zk[n] = (r, a)
            return m

        def qk_sum(n):
            if n in (0, 2, 6):
                hb[n] = take()
            first = 0 if n < 2 else 2 if n < 6 else 6
            b = hb[first]
            m = mm(b.ap[0:16, 0:T], EH[:, n if n < 2 else n - 2, :], sqr[:, n % 3, :], n == first, n in (1, 5, 9),
                   zk[n][1], *b.free)
            sq_free[n % 3] = m
            zk[n] = (zk[n][0], m)

        def qk_factor(first, last):
            f = f16[0:16, first // 2 * T2:first // 2 * T2 + T] if first < 6 else s16q[0:16, 0:T]
            b = hb[first]
            i = stt(f, b.ap[0:16, 0:T], 1.0 / 64, rs[0:16, :], ALU.mult, ALU.mult, zk[last][1])
            give(b, i)
            i = tt(dve, f, f, rs[0:16, :], ALU.mult, i)
            i = ts(dve, f, f, 1e-6, None, ALU.add, None, i)
            i = af(f, f, ACT.Sqrt, i)
            i = rec(f, f, i)
            return f, tt(dve, f, f, rs[0:16, :], ALU.mult, i)

        rel_use = [None] * 4
        i_acc = {}
        idx = [(c, hh) for c in (2, 1, 0) for hh in range(8)]

        def index(n):
            c, hh = idx[n]
            nq, kw, hf = CS[c], C0[c] + CS[c], hh % 2
            b = take()
            m = mm(b.ap[0:nq, 0:kw], QI[64 * hf:64 * hf + 64, hh // 2, C0[c]:kw],
                   KI[64 * hf:64 * hf + 64, 0, 0:kw], True, True, st_[0], st_[1 + hh // 2], *b.free)
            rr = rel[0:nq, n % 4, 0:kw]
            a = af(rr, b.ap[0:nq, 0:kw], ACT.Relu, m, rel_use[n % 4])
            give(b, a)
            w_ = Vt[0:nq, c, 256 + hh:257 + hh]
            o = scr[0:nq, c, 0:kw]
            if hh == 0:
                i = ts(dve, o, rr, w_, None, ALU.mult, None, a, r_v[c])
            else:
                i = stt(o, rr, w_, o, ALU.mult, ALU.add, a, i_acc[c])
            rel_use[n % 4] = i
            if hh == 7:
                d = scr[0:nq, c, C0[c]:kw]
                i = tt(dve, d, d, con(3, "cm", nq, nq), ALU.add, i)
            i_acc[c] = i

        def best(c):
            nq, kw = CS[c], C0[c] + CS[c]
            cur = i_acc[c]
            for rnd in range(8):
                src = (scr if rnd == 0 else wk)[0:nq, c, 0:kw]
                m8, w_ = t8[0:nq, c * 8:c * 8 + 8], wk[0:nq, c, 0:kw]
                cur = dve.op(lambda e, m8=m8, src=src: e.max(m8, src), cur)
                if rnd < 7:
                    cur = dve.op(lambda e, m8=m8, src=src, w_=w_: e.match_replace(w_, m8, src, -BIG), cur)
                yield cur

        r_b = {}

        def choose(c, cur):
            nq, kw = CS[c], C0[c] + CS[c]
            th, cn = t8[0:nq, c * 8 + 7:c * 8 + 8], t8[0:nq, 24 + c:25 + c]
            S_, e_, g_, q_ = (a[0:nq, c, 0:kw] for a in (scr, eqb, gtb, csb))
            i1 = ts(dve, g_, S_, th, None, ALU.is_gt, None, cur)
            i2 = ts(dve, e_, S_, th, None, ALU.is_equal, None)
            i3 = red(cn, g_, ALU.add, i1)
            o_ = ones[0:nq, 0:1].to_broadcast([nq, kw])
            i5 = dve.op(lambda e: e.tensor_tensor_scan(q_, o_, e_, 0.0, ALU.mult, ALU.add), i2)
            i4 = ts(dve, cn, cn, -1.0, 64.0, ALU.mult, ALU.add, i3)
            i6 = stt(q_, q_, cn, e_, ALU.is_le, ALU.mult, i5, i4)
            i7 = tt(dve, q_, q_, g_, ALU.add, i6)
            i8 = ts(dve, bias[0:nq, c, 0:kw], q_, BIG, -BIG, ALU.mult, ALU.add, i7)
            d = bias[0:nq, c, C0[c]:kw]
            r_b[c] = tt(dve, d, d, con(3, "cm", nq, nq), ALU.min, i8)

        r_kq, fac = {}, {}

        def norm_rope(n):
            if n >= 0:
                dst, g = jobs[n]
                f, i = fac[0 if n < 2 else 2 if n < 6 else 6]
                b, m = spread(f, n if n < 2 else n - 2, i)
                i = stt(dst, dst, par(g, 0), b.ap[:, 0:T], ALU.mult, ALU.mult, m, zk[n][0])
                give(b, i)
                r_kq[n] = i

        def turn_(n):
            r_kq[n] = rope(jobs[n][0], n, r_kq[n])

        gens = [best(c) for c in range(NC)]
        cur = [None] * NC
        rounds = [c for c in (2, 1, 0) for _ in range(8)]
        for n in range(10):
            x_last = qk_dense(n)
            if n >= 1:
                qk_sum(n - 1)
            for z in range(6 * n, min(6 * n + 6, 24)):
                index(z)
            for _ in range(4 if n >= 2 else 0):
                if rounds:
                    c = rounds.pop(0)
                    cur[c] = next(gens[c])
            if n == 2:
                fac[0] = qk_factor(0, 1)
            if n == 3:
                norm_rope(0)
                norm_rope(1)
            if n == 4:
                turn_(0)
                turn_(1)
            if n == 6:
                fac[2] = qk_factor(2, 5)
            if n in (7, 8):
                norm_rope(2 * n - 12)
                norm_rope(2 * n - 11)
            if n in (8, 9):
                turn_(2 * n - 14)
                turn_(2 * n - 13)
            if n == 8:
                choose(2, cur[2])
        qk_sum(9)
        fac[6] = qk_factor(6, 9)
        rs_use[(n_stat[0] - 1) % 2] = [fac[6][1]]
        choose(1, cur[1])
        choose(0, cur[0])
        units = [(c, 2 * gp + z) for gp in range(2) for c in (2, 1, 0) for z in range(2)]
        s_use, pt_use, stt_ = [None] * 3, [None] * 4, {}
        r_oT = {}

        def a_s(n):
            c, g = units[n]
            nq, kw, hf, k0 = CS[c], C0[c] + CS[c], g % 2, (g // 2) * 4
            o = n % 3 * (4 * T2 + 16)
            s = v3(sR2[0:nq, o:o + 4 * kw], 4)
            for k in range(4):
                b = take()
                m = mm(b.ap[0:nq, 0:kw], Q[64 * hf:64 * hf + 64, k0 + k, C0[c]:kw],
                       KK[64 * hf:64 * hf + 64, g // 2, 0:kw], True, True, r_kq[g // 2], r_kq[2 + k0 + k], *b.free)
                i = stt(s[:, k, :], b.ap[0:nq, 0:kw], 0.125, bias[0:nq, c, 0:kw], ALU.mult, ALU.add, m, r_b[c],
                        s_use[n % 3])
                give(b, i)
            mx, sm = sR2[0:nq, o + 4 * T2:o + 4 * T2 + 4], sR2[0:nq, o + 4 * T2 + 8:o + 4 * T2 + 12]
            i = red(mx, s, ALU.max, i, negate=True)
            for k in range(4):
                e_ = af(s[:, k, :], s[:, k, :], ACT.Exp, i, bias=mx[:, k:k + 1], acc=sm[:, k:k + 1])
            stt_[n] = (s, sm, e_)

        def a_p(n):
            c, g = units[n]
            s, sm, e_ = stt_[n]
            nq, kw = CS[c], C0[c] + CS[c]
            i = rec(sm, sm, e_)
            i = tt(dve, s, s, sm.unsqueeze(2).to_broadcast([nq, 4, kw]), ALU.mult, i)
            stt_[n] = (s, i)

        def a_t(n):
            c, g = units[n]
            s, i = stt_[n]
            nq = CS[c]
            pt = v3(pt2[:, n % 4 * NC * 4 * C:(n % 4 + 1) * NC * 4 * C], NC)
            for kc in range(c + 1):
                b = take()
                nk = CS[kc]
                for k in range(4):
                    m = tr(b.ap[0:nk, k * nq:k * nq + nq], s[:, k, C0[kc]:C0[kc] + nk], nq, i, *b.free)
                r = cp(act, pt[0:nk, kc, 0:4 * nq], b.ap[0:nk, 0:4 * nq], m, pt_use[n % 4])
                give(b, r)
            s_use[n % 3] = m
            stt_[n] = (pt, r)

        def a_v(n):
            c, g = units[n]
            nq, k0 = CS[c], (g // 2) * 4
            b = take()
            for kc in range(c + 1):
                nk = CS[kc]
                for z in range(2):
                    pt, r = stt_[n + z]
                    m = mm(b.ap[64 * z:64 * z + 64, 0:4 * nq], Vt[0:nk, kc, (g + z) * 64:(g + z) * 64 + 64],
                           pt[0:nk, kc, 0:4 * nq], kc == 0, kc == c, r, r_v[kc], *b.free)
            pt_use[n % 4] = pt_use[(n + 1) % 4] = m
            i = cp(act, oT[:, k0:k0 + 4, C0[c]:C0[c] + nq], v3(b.ap[:, 0:4 * nq], 4), m)
            give(b, i)
            r_oT[(c, g // 2)] = i

        for n in range(len(units) + 5):
            if n < len(units):
                a_s(n)
            if n < 4:
                norm_rope(6 + n)
                if n:
                    turn_(5 + n)
            if n == 4:
                turn_(9)
            if 0 <= n - 1 < len(units):
                a_p(n - 1)
            if 0 <= n - 2 < len(units):
                a_t(n - 2)
            if n >= 4 and n % 2 == 0 and n - 4 < len(units):
                a_v(n - 4)
            if n - 4 == 4 or n - 4 == 10:
                k0 = 0 if n - 4 == 4 else 4
                for k in range(k0, k0 + 4):
                    X.put(k, k * T2, oT[:, k, :], *[r_oT[(c, k0 // 4)] for c in range(NC)], x_last)
        sE.close()
        X2 = Pair(ctx, "x3", KT * T2, "right")
        nrm = tile_squares(h, T, pool, X2, ("norm_g_2", 1, 2))
        for n in range(KT):
            b, m = dense(X, T, KT, "at_w_o_p", n * P, P)
            r = tt(dve, h[:, n, :], b.ap[:, 0:T], h[:, n, :], ALU.add, m)
            give(b, r)
            nrm[0](n, r)
        nrm[1]()
        sD.close()
        rh, xf, fin = ffn(X2, h, T, nrm[2], ("ffn_w_in_2", 1, 1), ("ffn_w_out_2", 1, 1), 0.5,
                          lambda xf: (None, None, None))
        i_o = sp.dma(lambda e: e.dma_start(out, hx), s_out, *rh)
        sp.wait(i_o)

        assert st.n == NCH, st.n
        st.dram = wdecl(st.n)
        counts = {}
        for q in (pe, dve, act, pool, sp):
            q.number(counts)
        block = ctx.enter_context(nc.Block())

        @block.sync
        def _(eng):
            sp.emit(eng)

        @block.scalar
        def _(eng):
            act.emit(eng)

        @block.gpsimd
        def _(eng):
            pool.emit(eng)

        @block.vector
        def _(eng):
            dve.emit(eng)

        @block.tensor
        def _(eng):
            pe.emit(eng)
    return st.plan, st.n


def arrange(inp, plan, n):
    w_in = np.asarray(inp["w_in"])[0]
    q = [w_in[:, 512 + 64 * i:576 + 64 * i] for i in HO1]
    gates = w_in[:, 2816:2852]
    gcol = [h * 3 + br for br in range(3) for h in HO1]
    at = np.asarray(inp["at_w_in_2"])[0]
    wo = np.asarray(inp["w_out"])[0]
    ao = np.asarray(inp["at_w_o_2"])[0]
    w2k = np.asarray(inp["cmp_k_w2"])[0]
    src = {
        ("w_in", 0): np.concatenate([w_in[:, 0:512]] + q + [w_in[:, 1280:]], axis=1),
        "w_vg": np.concatenate([w_in[:, 2048:2304], gates[:, gcol], w_in[:, 2560:2816]], axis=1),
        "cmp_k_w1": np.asarray(inp["cmp_k_w1"])[0].reshape(2048, 256),
        "cmp_v_w1": np.asarray(inp["cmp_v_w1"])[0].reshape(2048, 256),
        "cmp_k_w2d": np.concatenate([w2k, w2k], axis=1),
        "cmp_v_w2": np.asarray(inp["cmp_v_w2"])[0],
        "w_out_p": np.concatenate([wo[0:256]] + [wo[256 + 64 * i:320 + 64 * i] for i in HO1], axis=0),
        "at_i": np.concatenate([at[:, 2048:2112], at[:, 2048:2112], at[:, 1536:2048]], axis=1),
        "at_qk": np.concatenate([at[:, 1024:1280]] + [at[:, 64 * i:64 * i + 64] for i in HO2], axis=1),
        "at_vw": np.concatenate([at[:, 1280:1536], at[:, 2112:2120]], axis=1),
        "at_w_o_p": np.concatenate([ao[64 * i:64 * i + 64] for i in HO2], axis=0),
    }
    W = np.zeros((n, P, CH), np.float32)
    for c, off, key, k0, kp, (c0, cw), w in plan:
        if key not in src:
            src[key] = np.asarray(inp[key[0]])[key[1:]]
        W[c, 0:kp, off:off + w] = src[key][k0:k0 + kp, c0:c0 + cw]
    return W


def kernel(**inputs):
    import concourse.bacc as _bacc
    from concourse.bass_utils import run_bass_kernel_spmd as _run

    nc = _bacc.Bacc("TRN2", target_bir_lowering=False, num_devices=1)
    carr, cat = consts()
    pat, npar = param_offsets()
    arrays = {}

    def declare(name, a):
        arrays[name] = np.ascontiguousarray(a)
        return nc.dram_tensor(name, arrays[name].shape, F32, kind="ExternalInput").ap()

    cd = [declare(f"consts{i}_dram", a) for i, a in enumerate(carr)]
    pd = declare("params_dram", pack_params(inputs))
    x = np.asarray(inputs["x"])[0]
    xd = declare("x_dram", x.T.reshape(KT, P, T1).transpose(1, 0, 2))
    md = declare("meta_dram", np.asarray(inputs["meta_2"]).T.reshape(KT, P, NM).transpose(1, 0, 2))
    out = nc.dram_tensor("out_dram", (P, KT, T1), F32, kind="ExternalOutput").ap()

    def wdecl(n):
        return nc.dram_tensor("w_dram", (n, P, CH), F32, kind="ExternalInput").ap()

    plan, n = build(nc, out, wdecl, cd, pd, xd, md, [a.shape[1] for a in carr], cat, pat, npar)
    arrays["w_dram"] = arrange(inputs, plan, n)
    r = _run(nc, [arrays], core_ids=[0])
    got = r.results[0]["out_dram"]
    return np.ascontiguousarray(got.transpose(1, 0, 2).reshape(1, KT * P, T1).transpose(0, 2, 1))
```
